# Optimizing a Trainium2 kernel written in Bass

```python
import math
import jax, jax.numpy as jnp
from jax import lax
import numpy as np

D_MODEL = 1024
BATCH = 1
SEQ = 512
DEPTH = 2

N_A = DEPTH // 2
N_B = DEPTH - N_A

EXPAND = 2
D_INNER = EXPAND * D_MODEL
SSM_HEAD_DIM = 64
SSM_HEADS = D_INNER // SSM_HEAD_DIM
N_GROUPS = 4
HEADS_PER_GROUP = SSM_HEADS // N_GROUPS
D_STATE = 128
CONV_K = 4
CONV_DIM = D_INNER + 2 * N_GROUPS * D_STATE
IN_PROJ_DIM = 2 * D_INNER + 2 * N_GROUPS * D_STATE + SSM_HEADS
CHUNK = 128
DT_MIN = 0.001
DT_MAX = 0.1

SB_HEAD_DIM = 64
SB_HEADS = D_MODEL // SB_HEAD_DIM
SB_WIDTH = SB_HEADS * SB_HEAD_DIM
SB_BLOCK = 128

PLE_DIM = 256

NORM_EPS = 1e-6


def rms(x):
    xf = x.astype(jnp.float32)
    return (xf * lax.rsqrt(jnp.mean(xf * xf, axis=-1, keepdims=True) + NORM_EPS)).astype(x.dtype)

def rmsnorm(x, g):
    return rms(x) * g.astype(x.dtype)

def causal_depthwise_conv(u, w, b):
    k = w.shape[0]
    s = u.shape[1]
    up = jnp.pad(u, ((0, 0), (k - 1, 0), (0, 0)))
    out = b
    for j in range(k):
        out = out + w[j] * up[:, j:j + s]
    return out

def ssd_chunked_scan(xs, dt, A, Bm, Cm):
    bsz, s, _, _ = xs.shape
    nc = s // CHUNK
    G, HG, P, N, L = N_GROUPS, HEADS_PER_GROUP, SSM_HEAD_DIM, D_STATE, CHUNK
    xc = xs.astype(jnp.float32).reshape(bsz, nc, L, G, HG, P).transpose(1, 0, 2, 3, 4, 5)
    dtc = dt.reshape(bsz, nc, L, G, HG).transpose(1, 0, 2, 3, 4)
    Bc = Bm.astype(jnp.float32).reshape(bsz, nc, L, G, N).transpose(1, 0, 2, 3, 4)
    Cc = Cm.astype(jnp.float32).reshape(bsz, nc, L, G, N).transpose(1, 0, 2, 3, 4)
    Ag = A.reshape(G, HG)
    causal = jnp.tril(jnp.ones((L, L), dtype=bool))

    def step(state, inp):
        x_k, dt_k, B_k, C_k = inp
        acum = jnp.cumsum(dt_k * Ag, axis=1)
        seg = acum[:, :, None] - acum[:, None, :]
        decay = jnp.exp(jnp.where(causal[None, :, :, None, None], seg, -jnp.inf))
        xdt = x_k * dt_k[..., None]
        cb = jnp.einsum('blgn,bsgn->blsg', C_k, B_k)
        y_intra = jnp.einsum('blsgh,bsghp->blghp', cb[..., None] * decay, xdt)
        y_inter = jnp.einsum('blgn,bghpn->blghp', C_k, state) * jnp.exp(acum)[..., None]
        to_end = jnp.exp(acum[:, -1:] - acum)
        new_state = state * jnp.exp(acum[:, -1])[..., None, None] + jnp.einsum(
            'bsgn,bsghp->bghpn', B_k, xdt * to_end[..., None])
        return new_state, y_intra + y_inter

    state0 = jnp.zeros((bsz, G, HG, P, N), jnp.float32)
    _, y = lax.scan(step, state0, (xc, dtc, Bc, Cc))
    y = y.transpose(1, 0, 2, 3, 4, 5).reshape(bsz, s, SSM_HEADS, P)
    return y.astype(xs.dtype)

def mamba2_mixer(h, norm_g, w_in, conv_w, conv_b, dt_bias, A_log, d_skip, y_g, w_out):
    bsz, s, _ = h.shape
    u = rmsnorm(h, norm_g)
    zxbcdt = u @ w_in
    z = zxbcdt[..., :D_INNER]
    xbc = zxbcdt[..., D_INNER:D_INNER + CONV_DIM]
    dt = zxbcdt[..., D_INNER + CONV_DIM:]
    xbc = jax.nn.silu(causal_depthwise_conv(xbc, conv_w, conv_b))
    xs = xbc[..., :D_INNER].reshape(bsz, s, SSM_HEADS, SSM_HEAD_DIM)
    Bm = xbc[..., D_INNER:D_INNER + N_GROUPS * D_STATE].reshape(bsz, s, N_GROUPS, D_STATE)
    Cm = xbc[..., D_INNER + N_GROUPS * D_STATE:].reshape(bsz, s, N_GROUPS, D_STATE)
    dt = jax.nn.softplus(dt.astype(jnp.float32) + dt_bias.astype(jnp.float32))
    A = -jnp.exp(A_log.astype(jnp.float32))
    y = ssd_chunked_scan(xs, dt, A, Bm, Cm)
    y = y + d_skip.astype(y.dtype)[:, None] * xs
    y = y.reshape(bsz, s, D_INNER) * jax.nn.silu(z)
    y = rms(y.reshape(bsz, s, N_GROUPS, D_INNER // N_GROUPS)).reshape(bsz, s, D_INNER) * y_g
    return y @ w_out

def shared_kv(h, norm_g, w_kv, k_g):
    bsz, s, _ = h.shape
    kv = rmsnorm(h, norm_g) @ w_kv
    k = rmsnorm(kv[..., :SB_WIDTH].reshape(bsz, s, SB_HEADS, SB_HEAD_DIM), k_g)
    v = kv[..., SB_WIDTH:].reshape(bsz, s, SB_HEADS, SB_HEAD_DIM)
    return k.transpose(0, 2, 1, 3), v.transpose(0, 2, 1, 3)

def stick_breaking_mixer(h, k, v, norm_g, w_in, q_g, w_out):
    bsz, s, _ = h.shape
    qg = rmsnorm(h, norm_g) @ w_in
    gate = qg[..., SB_WIDTH:]
    q = rmsnorm(qg[..., :SB_WIDTH].reshape(bsz, s, SB_HEADS, SB_HEAD_DIM), q_g)
    q = (q * (1.0 / math.sqrt(SB_HEAD_DIM))).transpose(0, 2, 1, 3)
    outs = []
    for blk in range(s // SB_BLOCK):
        q0 = blk * SB_BLOCK
        kend = q0 + SB_BLOCK
        z = jnp.einsum('bhtd,bhsd->bhts', q[:, :, q0:kend], k[:, :, :kend]).astype(jnp.float32)
        t_idx = q0 + jnp.arange(SB_BLOCK)[:, None]
        s_idx = jnp.arange(kend)[None, :]
        strict = s_idx < t_idx
        log_keep = jnp.where(strict, jax.nn.log_sigmoid(-z), 0.0)
        suffix = lax.cumsum(log_keep, axis=3, reverse=True) - log_keep
        weights = jnp.where(strict, jnp.exp(jax.nn.log_sigmoid(z) + suffix), 0.0)
        outs.append(jnp.einsum('bhts,bhsd->bhtd', weights.astype(v.dtype), v[:, :, :kend]))
    o = jnp.concatenate(outs, axis=2).transpose(0, 2, 1, 3).reshape(bsz, s, SB_WIDTH)
    return (o * jax.nn.silu(gate)) @ w_out

def per_layer_embedding(h, p_i, norm_g, w_gate, w_proj):
    return h + (p_i @ w_proj) * jax.nn.sigmoid(rmsnorm(h, norm_g) @ w_gate)

def first_inputs(seed: int = 0) -> dict:
    key = jax.random.key(seed)
    ks = jax.random.split(key, 24)

    def nrm(k, shape, scale):
        return jax.random.normal(k, shape, jnp.float32) * scale

    def gain(k, shape):
        return 1.0 + 0.05 * jax.random.normal(k, shape, jnp.float32)

    u = jax.random.uniform(ks[6], (N_A, SSM_HEADS), jnp.float32)
    dt = jnp.exp(u * (math.log(DT_MAX) - math.log(DT_MIN)) + math.log(DT_MIN))
    dt_bias = dt + jnp.log(-jnp.expm1(-dt))
    A_log = jnp.log(jax.random.uniform(ks[7], (N_A, SSM_HEADS), jnp.float32, minval=1.0, maxval=16.0))
    return {
        "x": nrm(ks[0], (BATCH, SEQ, D_MODEL), 1.0),
        "p": nrm(ks[1], (DEPTH, BATCH, SEQ, PLE_DIM), 1.0),
        "m_norm": gain(ks[2], (N_A, D_MODEL)),
        "m_in": nrm(ks[3], (N_A, D_MODEL, IN_PROJ_DIM), D_MODEL ** -0.5),
        "m_conv_w": nrm(ks[4], (N_A, CONV_K, CONV_DIM), CONV_K ** -0.5),
        "m_conv_b": nrm(ks[5], (N_A, CONV_DIM), 0.01),
        "m_dt_bias": dt_bias,
        "m_A_log": A_log,
        "m_D": gain(ks[8], (N_A, SSM_HEADS)),
        "m_ynorm": gain(ks[9], (N_A, D_INNER)),
        "m_out": nrm(ks[10], (N_A, D_INNER, D_MODEL), D_INNER ** -0.5),
        "kv_norm": gain(ks[11], (D_MODEL,)),
        "w_kv": nrm(ks[12], (D_MODEL, 2 * SB_WIDTH), D_MODEL ** -0.5),
        "k_norm": gain(ks[13], (SB_HEAD_DIM,)),
        "s_norm": gain(ks[14], (N_B, D_MODEL)),
        "s_in": nrm(ks[15], (N_B, D_MODEL, 2 * SB_WIDTH), D_MODEL ** -0.5),
        "q_norm": gain(ks[16], (N_B, SB_HEAD_DIM)),
        "s_out": nrm(ks[17], (N_B, SB_WIDTH, D_MODEL), SB_WIDTH ** -0.5),
        "ple_norm": gain(ks[18], (DEPTH, D_MODEL)),
        "ple_gate": nrm(ks[19], (DEPTH, D_MODEL, D_MODEL), D_MODEL ** -0.5),
        "ple_proj": nrm(ks[20], (DEPTH, PLE_DIM, D_MODEL), PLE_DIM ** -0.5),
    }

def first_block(x, p, m_norm, m_in, m_conv_w, m_conv_b, m_dt_bias, m_A_log, m_D, m_ynorm, m_out,
              kv_norm, w_kv, k_norm, s_norm, s_in, q_norm, s_out, ple_norm, ple_gate, ple_proj):
    h = x
    k = v = None
    for i in range(DEPTH):
        if i < N_A:
            h = h + mamba2_mixer(h, m_norm[i], m_in[i], m_conv_w[i], m_conv_b[i], m_dt_bias[i],
                                 m_A_log[i], m_D[i], m_ynorm[i], m_out[i])
        else:
            if i == N_A:
                k, v = shared_kv(h, kv_norm, w_kv, k_norm)
            j = i - N_A
            h = h + stick_breaking_mixer(h, k, v, s_norm[j], s_in[j], q_norm[j], s_out[j])
        h = per_layer_embedding(h, p[i], ple_norm[i], ple_gate[i], ple_proj[i])
    return h


DEPTH_2 = 1

N_MEM = 256
GRID_W = 64
HY_W = 512
NA_HEADS = 8
NA_HEAD_DIM = 64
NA_W = NA_HEADS * NA_HEAD_DIM
NA_WIN_ROWS = 8
NA_WIN_COLS = 16
SC_W = 512
XA_HEADS = 4
XA_HEAD_DIM = D_MODEL // XA_HEADS
D_FF = 2816
HY_ORDER = 2
HY_EMB = 33
HY_HIDDEN = 64
HY_FAST_DECAY = 0.3
HY_SLOW_DECAY = 1.5
HY_TARGET = 1e-2
N_BRANCH = 3
EPS = 1e-6
PROJ_W = 3 * HY_W + 3 * NA_W + 3 * SC_W + N_BRANCH * D_MODEL


def rms_norm(x, g):
    xf = x.astype(jnp.float32)
    y = xf * lax.rsqrt(jnp.mean(xf * xf, axis=-1, keepdims=True) + EPS)
    return (y * g.astype(jnp.float32)).astype(x.dtype)

def dwconv3(x, w):
    xp = jnp.pad(x, ((0, 0), (1, 1), (0, 0)))
    return xp[:, :-2] * w[0] + xp[:, 1:-1] * w[1] + xp[:, 2:] * w[2]

def hyena_filters(L, w1, b1, w2, b2, w3, freq):
    f32 = jnp.float32
    t = jnp.linspace(0.0, 1.0, L, dtype=f32)[:, None]
    bands = (HY_EMB - 1) // 2
    w = 2.0 * math.pi * jnp.arange(L, dtype=f32)[:, None] / L
    f = jnp.linspace(1e-4, bands - 1, bands, dtype=f32)[None, :]
    z = jnp.concatenate([t, jnp.cos(f * w), -jnp.sin(f * w)], axis=-1)
    h = jnp.sin(freq[0].astype(f32) * (z @ w1.astype(f32) + b1.astype(f32)))
    h = jnp.sin(freq[1].astype(f32) * (h @ w2.astype(f32) + b2.astype(f32)))
    h = (h @ w3.astype(f32)).reshape(L, 2, HY_ORDER, HY_W)
    deltas = jnp.abs(jnp.linspace(math.log(HY_TARGET) / HY_SLOW_DECAY,
                                  math.log(HY_TARGET) / HY_FAST_DECAY, HY_W, dtype=f32))
    h = h * jnp.exp(-t * deltas)[:, None, None, :]
    h_fwd, h_bwd = h[:, 0], h[:, 1]
    k2 = jnp.concatenate([h_fwd, jnp.zeros((1, HY_ORDER, HY_W), f32), h_bwd[1:][::-1]], axis=0)
    return jnp.fft.rfft(k2, axis=0)

def long_conv(z, kf, bias):
    L = z.shape[1]
    zf32 = z.astype(jnp.float32)
    zf = jnp.fft.rfft(zf32, n=2 * L, axis=1)
    y = jnp.fft.irfft(zf * kf[None], n=2 * L, axis=1)[:, :L]
    return (y + zf32 * bias.astype(jnp.float32)).astype(z.dtype)

def hyena_mixer(u, short_w, kf, bias):
    u = dwconv3(u, short_w)
    v, x1, x2 = jnp.split(u, 3, axis=-1)
    z = x1 * long_conv(v, kf[:, 0], bias[0])
    return x2 * long_conv(z, kf[:, 1], bias[1])

def neighbourhood_attention(q, k, v, rpb):
    B, L, _ = q.shape
    rows = L // GRID_W
    kr = min(NA_WIN_ROWS, rows)

    def grid(t):
        return t.reshape(B, rows, GRID_W, NA_HEADS, NA_HEAD_DIM).transpose(0, 3, 1, 2, 4)

    qg = grid(q) * (NA_HEAD_DIM ** -0.5)
    kg, vg = grid(k), grid(v)
    r = jnp.arange(rows)
    row_idx = jnp.clip(r - kr // 2, 0, rows - kr)[:, None] + jnp.arange(kr)[None, :]
    k_rows = kg[:, :, row_idx]
    v_rows = vg[:, :, row_idx]
    c = jnp.arange(GRID_W)
    col_start = jnp.clip(c - NA_WIN_COLS // 2, 0, GRID_W - NA_WIN_COLS)
    col_mask = (c[None, :] >= col_start[:, None]) & (c[None, :] < col_start[:, None] + NA_WIN_COLS)
    dr = row_idx - r[:, None] + (NA_WIN_ROWS - 1)
    dc = jnp.clip(c[None, :] - c[:, None] + NA_WIN_COLS - 1, 0, 2 * NA_WIN_COLS - 2)
    bias = rpb[:, dr][..., dc].transpose(0, 1, 3, 2, 4)
    s = jnp.einsum('bhrqd,bhrkcd->bhrqkc', qg, k_rows).astype(jnp.float32)
    s = s + bias[None].astype(jnp.float32)
    s = jnp.where(col_mask[:, None, :], s, -1e30)
    p = jax.nn.softmax(s, axis=(-2, -1)).astype(v.dtype)
    o = jnp.einsum('bhrqkc,bhrkcd->bhrqd', p, v_rows)
    return o.transpose(0, 2, 3, 1, 4).reshape(B, L, NA_W)

def short_conv_mixer(b_gate, c_gate, x_in, w):
    return b_gate * dwconv3(c_gate * x_in, w)

def memory_cross_attention(h, mem_n, wq, wkv, wo):
    B, L, _ = h.shape
    M = mem_n.shape[1]
    q = (h @ wq).reshape(B, L, XA_HEADS, XA_HEAD_DIM)
    km, vm = jnp.split(mem_n @ wkv, 2, axis=-1)
    km = km.reshape(B, M, XA_HEADS, XA_HEAD_DIM)
    vm = vm.reshape(B, M, XA_HEADS, XA_HEAD_DIM)
    s = jnp.einsum('bshd,bmhd->bhsm', q, km).astype(jnp.float32) * (XA_HEAD_DIM ** -0.5)
    p = jax.nn.softmax(s, axis=-1).astype(h.dtype)
    o = jnp.einsum('bhsm,bmhd->bshd', p, vm).reshape(B, L, D_MODEL)
    return o @ wo

def conv_glu_ffn(h, w_up, w_conv, w_down):
    u = dwconv3(h @ w_up, w_conv)
    g, val = jnp.split(u, 2, axis=-1)
    return (jax.nn.gelu(g, approximate=True) * val) @ w_down

def second_inputs(seed: int = 0) -> dict:
    key = jax.random.key(seed)
    ks = jax.random.split(key, 24)

    def nrm(k, shape, scale):
        return jax.random.normal(k, shape, jnp.float32) * scale

    return {
        "x": nrm(ks[0], (BATCH, SEQ, D_MODEL), 1.0),
        "mem": nrm(ks[1], (BATCH, N_MEM, D_MODEL), 1.0),
        "norm_gains": 1.0 + nrm(ks[2], (DEPTH_2, 6, D_MODEL), 0.05),
        "mem_norm": 1.0 + nrm(ks[3], (DEPTH_2, D_MODEL), 0.05),
        "w_in": nrm(ks[4], (DEPTH_2, D_MODEL, PROJ_W), D_MODEL ** -0.5),
        "gate_bias": nrm(ks[5], (DEPTH_2, N_BRANCH, D_MODEL), 0.02),
        "hy_short_w": nrm(ks[6], (DEPTH_2, 3, 3 * HY_W), 3 ** -0.5),
        "hy_w1": nrm(ks[7], (DEPTH_2, HY_EMB, HY_HIDDEN), HY_EMB ** -0.5),
        "hy_b1": nrm(ks[8], (DEPTH_2, HY_HIDDEN), 0.02),
        "hy_w2": nrm(ks[9], (DEPTH_2, HY_HIDDEN, HY_HIDDEN), HY_HIDDEN ** -0.5),
        "hy_b2": nrm(ks[10], (DEPTH_2, HY_HIDDEN), 0.02),
        "hy_w3": nrm(ks[11], (DEPTH_2, HY_HIDDEN, 2 * HY_ORDER * HY_W), 0.05 * HY_HIDDEN ** -0.5),
        "hy_freq": 1.0 + nrm(ks[12], (DEPTH_2, 2, HY_HIDDEN), 0.05),
        "hy_bias": nrm(ks[13], (DEPTH_2, HY_ORDER, HY_W), 0.1),
        "na_rpb": nrm(ks[14], (DEPTH_2, NA_HEADS, 2 * NA_WIN_ROWS - 1, 2 * NA_WIN_COLS - 1), 0.02),
        "sc_conv_w": nrm(ks[15], (DEPTH_2, 3, SC_W), 3 ** -0.5),
        "w_branch": nrm(ks[16], (DEPTH_2, N_BRANCH, HY_W, D_MODEL), HY_W ** -0.5),
        "w_out": nrm(ks[17], (DEPTH_2, D_MODEL, D_MODEL), D_MODEL ** -0.5),
        "xa_wq": nrm(ks[18], (DEPTH_2, D_MODEL, D_MODEL), D_MODEL ** -0.5),
        "xa_wkv": nrm(ks[19], (DEPTH_2, D_MODEL, 2 * D_MODEL), D_MODEL ** -0.5),
        "xa_wo": nrm(ks[20], (DEPTH_2, D_MODEL, D_MODEL), D_MODEL ** -0.5),
        "ffn_up": nrm(ks[21], (DEPTH_2, D_MODEL, 2 * D_FF), D_MODEL ** -0.5),
        "ffn_conv": nrm(ks[22], (DEPTH_2, 3, 2 * D_FF), 3 ** -0.5),
        "ffn_down": nrm(ks[23], (DEPTH_2, D_FF, D_MODEL), D_FF ** -0.5),
    }

def second_block(x, mem, norm_gains, mem_norm, w_in, gate_bias, hy_short_w, hy_w1, hy_b1, hy_w2, hy_b2,
              hy_w3, hy_freq, hy_bias, na_rpb, sc_conv_w, w_branch, w_out, xa_wq, xa_wkv, xa_wo,
              ffn_up, ffn_conv, ffn_down):
    B, L, _ = x.shape
    splits = [3 * HY_W, 3 * HY_W + 3 * NA_W, 3 * HY_W + 3 * NA_W + 3 * SC_W]
    for l in range(DEPTH_2):
        g = norm_gains[l]
        h = rms_norm(x, g[0])
        proj = h @ w_in[l]
        hy_u, na_qkv, sc_u, gate_pre = jnp.split(proj, splits, axis=-1)
        kf = hyena_filters(L, hy_w1[l], hy_b1[l], hy_w2[l], hy_b2[l], hy_w3[l], hy_freq[l])
        y_a = hyena_mixer(hy_u, hy_short_w[l], kf, hy_bias[l])
        q, k, v = jnp.split(na_qkv, 3, axis=-1)
        y_b = neighbourhood_attention(q, k, v, na_rpb[l])
        b_gate, c_gate, x_in = jnp.split(sc_u, 3, axis=-1)
        y_c = short_conv_mixer(b_gate, c_gate, x_in, sc_conv_w[l])
        gates = jax.nn.sigmoid(gate_pre.reshape(B, L, N_BRANCH, D_MODEL) + gate_bias[l])
        merged = (gates[:, :, 0] * (y_a @ w_branch[l, 0])
                  + gates[:, :, 1] * (y_b @ w_branch[l, 1])
                  + gates[:, :, 2] * (y_c @ w_branch[l, 2]))
        x = x + rms_norm(merged @ w_out[l], g[1])
        h = rms_norm(x, g[2])
        mem_n = rms_norm(mem, mem_norm[l])
        x = x + rms_norm(memory_cross_attention(h, mem_n, xa_wq[l], xa_wkv[l], xa_wo[l]), g[3])
        h = rms_norm(x, g[4])
        x = x + rms_norm(conv_glu_ffn(h, ffn_up[l], ffn_conv[l], ffn_down[l]), g[5])
    return x


def setup_inputs(seed=0):
    out = dict(first_inputs(seed))
    for name, value in second_inputs(seed + 1).items():
        if name != "x":
            out[name + "_2"] = value
    return out


def reference(
    x, p, m_norm, m_in, m_conv_w, m_conv_b, m_dt_bias, m_A_log, m_D, m_ynorm, m_out, kv_norm,
    w_kv, k_norm, s_norm, s_in, q_norm, s_out, ple_norm, ple_gate, ple_proj, mem_2,
    norm_gains_2, mem_norm_2, w_in_2, gate_bias_2, hy_short_w_2, hy_w1_2, hy_b1_2, hy_w2_2,
    hy_b2_2, hy_w3_2, hy_freq_2, hy_bias_2, na_rpb_2, sc_conv_w_2, w_branch_2, w_out_2, xa_wq_2,
    xa_wkv_2, xa_wo_2, ffn_up_2, ffn_conv_2, ffn_down_2,
):
    x = first_block(
        x, p, m_norm, m_in, m_conv_w, m_conv_b, m_dt_bias, m_A_log, m_D, m_ynorm, m_out,
        kv_norm, w_kv, k_norm, s_norm, s_in, q_norm, s_out, ple_norm, ple_gate, ple_proj,
    )
    return second_block(
        x, mem_2, norm_gains_2, mem_norm_2, w_in_2, gate_bias_2, hy_short_w_2, hy_w1_2, hy_b1_2,
        hy_w2_2, hy_b2_2, hy_w3_2, hy_freq_2, hy_bias_2, na_rpb_2, sc_conv_w_2, w_branch_2,
        w_out_2, xa_wq_2, xa_wkv_2, xa_wo_2, ffn_up_2, ffn_conv_2, ffn_down_2,
    )


_drawn_inputs = setup_inputs


def setup_inputs(seed=0):
    import zlib

    import numpy as np

    out = dict(_drawn_inputs(seed))
    spreads = {}
    factors = {'m_conv_b': 4.257,
     'kv_norm': 3.125,
     'k_norm': 7.627,
     's_norm': 3.112,
     'q_norm': 6.162,
     'ple_norm': 4.375,
     'gate_bias_2': 49.919,
     'hy_b1_2': 8.0,
     'hy_b2_2': 24.091,
     'hy_freq_2': 22.553,
     'hy_bias_2': 7.847,
     'na_rpb_2': 180.493,
     'mem_norm_2': 16.272,
     'hy_w2_2': 2.707,
     'hy_w3_2': 2.679}
    for name, (base, spread) in spreads.items():
        noise = np.random.default_rng([zlib.crc32(name.encode()), seed]).standard_normal(out[name].shape)
        drawn = base * np.exp(spread * noise) if base else spread * noise
        out[name] = __import__('jax').numpy.asarray(drawn.astype(out[name].dtype))
    for name, factor in factors.items():
        out[name] = (out[name] * factor).astype(out[name].dtype)
    return out
```

```python
import math
from contextlib import ExitStack

import numpy as np
import concourse.bass as bass
from concourse import mybir

fp32 = mybir.dt.float32
fp32r = mybir.dt.float32r
ALU = mybir.AluOpType
ACT = mybir.ActivationFunctionType
AX = mybir.AxisListType

P = 128
SEQ = 512
TT = SEQ // P
D = 1024
DK = D // P
EPS = 1e-6

D_INNER = 2048
HEADS = 32
GROUPS = 4
HG = HEADS // GROUPS
HD = 64
CONV_TILES = 24

N_MEM = 256
MT = N_MEM // P
HY = 512
D_FF = 2816
FF_TILES = D_FF // P

PARAM_ROWS = [
    ("m_conv_w", 4 * CONV_TILES), ("m_conv_b", CONV_TILES), ("m_norm", DK),
    ("m_ynorm", 2 * DK), ("kv_norm", DK), ("s_norm", DK), ("ple_norm", 2 * DK), ("norm_gains_2", 6 * DK),
    ("mem_norm_2", DK), ("gate_bias_2", 3 * DK),
    ("hy_short_w_2", 36), ("sc_conv_w_2", 12), ("ffn_conv_2", 3 * 2 * FF_TILES),
]
PARAM_COL = {}
_col = 0
for _name, _rows in PARAM_ROWS:
    PARAM_COL[_name] = _col
    _col += _rows
PARAM_TOTAL = _col


class Chain:

    def __init__(self, eng, sem):
        self.eng, self.sem, self.n = eng, sem, 0

    def __call__(self, instruction):
        instruction.then_inc(self.sem, 1)
        self.n += 1

    def wait(self):
        self.eng.wait_ge(self.sem, self.n)


class Weights:

    def __init__(self, nc, ctx):
        self.raw = [ctx.enter_context(nc.sbuf_tensor(f"w_raw{i}", [P, 2048], fp32)) for i in range(2)]
        self.hi = [ctx.enter_context(nc.sbuf_tensor(f"w_hi{i}", [P, 2048], fp32r)) for i in range(2)]
        self.lo = [ctx.enter_context(nc.sbuf_tensor(f"w_lo{i}", [P, 2048], fp32r)) for i in range(2)]
        self.loaded = [nc.alloc_semaphore(f"w_loaded{i}") for i in range(2)]
        self.hi_done = nc.alloc_semaphore("w_hi_done")
        self.lo_done = nc.alloc_semaphore("w_lo_done")
        self.n_load = self.n_hi = self.n_lo = self.n_use = 0

    def load(self, sp, ap):
        n = self.n_load
        self.n_load += 1
        kt, cols = ap.shape[1], ap.shape[2]
        if n >= 2:
            sp.wait_ge(self.lo_done, n - 1)
        sp.dma_start(self.raw[n % 2][:, 0:kt * cols].rearrange("p (k c) -> p k c", k=kt), ap)\
          .then_inc(self.loaded[n % 2], 16)

    def split_hi(self, act, size):
        n = self.n_hi
        self.n_hi += 1
        act.wait_ge(self.loaded[n % 2], 16 * (n // 2 + 1))
        act.activation(self.hi[n % 2][:, 0:size], self.raw[n % 2][:, 0:size], ACT.Copy).then_inc(self.hi_done, 1)

    def split_lo(self, pool, size):
        n = self.n_lo
        self.n_lo += 1
        pool.wait_ge(self.hi_done, n + 1)
        pool.tensor_tensor(self.lo[n % 2][:, 0:size], self.raw[n % 2][:, 0:size],
                           self.hi[n % 2][:, 0:size].bitcast(fp32), ALU.subtract).then_inc(self.lo_done, 1)

    def take(self, pe, kt, cols):
        n = self.n_use
        self.n_use += 1
        pe.wait_ge(self.lo_done, n + 1)
        return [s[n % 2][:, 0:kt * cols].rearrange("p (k c) -> p k c", k=kt) for s in (self.hi, self.lo)]


def slabs_of(w, cols, c0=0, c1=None):
    v = w.rearrange("(k p) n -> p k n", p=P)
    c1 = w.shape[1] if c1 is None else c1
    return [v[:, :, c:min(c + cols, c1)] for c in range(c0, c1, cols)]


class Core:

    def __init__(self, nc, ctx):
        self.nc = nc
        Sems.retired.clear()
        sb = lambda n, s, d=fp32: ctx.enter_context(nc.sbuf_tensor(n, s, d))
        self.h = sb("h", [P, DK, SEQ])
        self.params = sb("params", [P, PARAM_TOTAL])
        self.ident = sb("ident", [P, P])
        self.ones = sb("ones", [P, P])
        self.head_ones = sb("head_ones", [P, P])
        self.upto = sb("upto", [P, P])
        self.after = sb("after", [P, P])
        self.minus_from = sb("minus_from", [P, P])
        self.minus_ones = sb("minus_ones", [P, P])
        self.ident_r = sb("ident_r", [P, P], fp32r)
        self.causal_r = sb("causal_r", [P, P], fp32r)
        self.head_gain = sb("head_gain", [P, 2])
        self.ps = ctx.enter_context(nc.psum_tensor("ps", [P, 8, 512], fp32))
        self.w = Weights(nc, ctx)
        self.out_stored = nc.alloc_semaphore("out_stored")
        self.split_buf = [sb(f"split_buf{i}", [P, SEQ]) for i in range(2)]

    def gain(self, name, k):
        c = PARAM_COL[name] + k
        return self.params[:, c:c + 1]


class Sems:

    retired = []

    def __init__(self, nc, stage):
        self.nc, self.stage, self.made = nc, stage, {}

    def __getattr__(self, name):
        if name not in self.made:
            self.made[name] = self.nc.alloc_semaphore(f"{self.stage}_{name}")
        return self.made[name]

    def clear(self):
        mine = list(self.made.values())
        for sem in mine:
            self.nc.gpsimd.sem_clear(sem)
        for sem in Sems.retired:
            self.nc.release_semaphore(sem)
        Sems.retired[:] = mine


def products(pe, out, whi, wlo, k, cols, xhi, xlo, xk, start, stop):
    pe.matmul(out, whi[:, k, cols], xhi[:, xk, :], start=start, stop=False)
    pe.matmul(out, whi[:, k, cols], xlo[:, xk, :], start=False, stop=False)
    return pe.matmul(out, wlo[:, k, cols], xhi[:, xk, :], start=False, stop=stop)


def token_products(pe, out, whi, wlo, k, cols, xhi, xlo, xk, toks, start, stop):
    pe.matmul(out, xhi[:, xk, toks], whi[:, k, cols], start=start, stop=False)
    pe.matmul(out, xhi[:, xk, toks], wlo[:, k, cols], start=False, stop=False)
    return pe.matmul(out, xlo[:, xk, toks], whi[:, k, cols], start=False, stop=stop)


def norm_stage(core, name, src, gains, xhi, xlo, kt=DK, toks=SEQ):
    nc, s, ps = core.nc, Sems(core.nc, name), core.ps
    with ExitStack() as ctx:
        sb = lambda n, sh: ctx.enter_context(nc.sbuf_tensor(f"{name}_{n}", sh, fp32))
        sq, root, inv = sb("sq", [P, 2, SEQ]), sb("root", [P, SEQ]), sb("inv", [P, SEQ])
        tmp = core.split_buf
        with nc.Block() as block:
            @block.scalar
            def _(act):
                for k in range(kt):
                    if k >= 2:
                        act.wait_ge(s.sq_used, k - 1)
                    act.activation(sq[:, k % 2, 0:toks], src[:, k, 0:toks], ACT.Square).then_inc(s.sq_ready, 1)
                act.wait_ge(s.mean_ready, 1)
                act.activation(root[:, 0:toks], inv[:, 0:toks], ACT.Sqrt).then_inc(s.root_ready, 1)
                for k in range(kt):
                    act.wait_ge(s.scaled, k + 1)
                    act.activation(xhi[:, k, 0:toks], tmp[k % 2][:, 0:toks], ACT.Copy).then_inc(s.hi_done, 1)

            @block.tensor
            def _(pe):
                for k in range(kt):
                    pe.wait_ge(s.sq_ready, k + 1)
                    pe.matmul(ps[:, 7, 0:toks], core.ones[:, :], sq[:, k % 2, 0:toks],
                              start=(k == 0), stop=(k == kt - 1)).then_inc(s.sq_used, 1)

            @block.vector
            def _(dve):
                dve.wait_ge(s.sq_used, kt)
                dve.tensor_scalar(inv[:, 0:toks], ps[:, 7, 0:toks], 1.0 / (kt * P), EPS, ALU.mult, ALU.add)\
                   .then_inc(s.mean_ready, 1)
                dve.wait_ge(s.root_ready, 1)
                dve.reciprocal(inv[:, 0:toks], root[:, 0:toks]).then_inc(s.inv_ready, 1)
                dve.wait_ge(s.inv_ready, 1)
                for k in range(kt):
                    if k >= 2:
                        dve.wait_ge(s.lo_done, k - 1)
                    dve.scalar_tensor_tensor(out=tmp[k % 2][:, 0:toks], in0=src[:, k, 0:toks], scalar=gains(k),
                                             in1=inv[:, 0:toks], op0=ALU.mult, op1=ALU.mult).then_inc(s.scaled, 1)

            @block.gpsimd
            def _(pool):
                for k in range(kt):
                    pool.wait_ge(s.hi_done, k + 1)
                    pool.tensor_tensor(xlo[:, k, 0:toks], tmp[k % 2][:, 0:toks],
                                       xhi[:, k, 0:toks].bitcast(fp32), ALU.subtract).then_inc(s.lo_done, 1)
        s.clear()


def add_normed_stage(core, name, y, gains):
    nc, s, ps = core.nc, Sems(core.nc, name), core.ps
    with ExitStack() as ctx:
        sb = lambda n, sh: ctx.enter_context(nc.sbuf_tensor(f"{name}_{n}", sh, fp32))
        sq, root, inv, tmp = sb("sq", [P, 2, SEQ]), sb("root", [P, SEQ]), sb("inv", [P, SEQ]), sb("tmp", [P, 2, SEQ])
        with nc.Block() as block:
            @block.scalar
            def _(act):
                for k in range(DK):
                    if k >= 2:
                        act.wait_ge(s.sq_used, k - 1)
                    act.activation(sq[:, k % 2, :], y[:, k, :], ACT.Square).then_inc(s.sq_ready, 1)
                act.wait_ge(s.mean_ready, 1)
                act.activation(root[:, :], inv[:, :], ACT.Sqrt).then_inc(s.root_ready, 1)

            @block.tensor
            def _(pe):
                for k in range(DK):
                    pe.wait_ge(s.sq_ready, k + 1)
                    pe.matmul(ps[:, 7, :], core.ones[:, :], sq[:, k % 2, :],
                              start=(k == 0), stop=(k == DK - 1)).then_inc(s.sq_used, 1)

            @block.vector
            def _(dve):
                dve.wait_ge(s.sq_used, DK)
                dve.tensor_scalar(inv[:, :], ps[:, 7, :], 1.0 / D, EPS, ALU.mult, ALU.add).then_inc(s.mean_ready, 1)
                dve.wait_ge(s.root_ready, 1)
                dve.reciprocal(inv[:, :], root[:, :]).then_inc(s.inv_ready, 1)
                dve.wait_ge(s.inv_ready, 1)
                for k in range(DK):
                    if k >= 2:
                        dve.wait_ge(s.added, k - 1)
                    dve.scalar_tensor_tensor(out=tmp[:, k % 2, :], in0=y[:, k, :], scalar=gains(k),
                                             in1=inv[:, :], op0=ALU.mult, op1=ALU.mult).then_inc(s.scaled, 1)

            @block.gpsimd
            def _(pool):
                for k in range(DK):
                    pool.wait_ge(s.scaled, k + 1)
                    pool.tensor_tensor(core.h[:, k, :], core.h[:, k, :], tmp[:, k % 2, :], ALU.add).then_inc(s.added, 1)
        s.clear()


def linear_stage(core, name, slabs, tiles, xhi, xlo, act_tile=None, dve_tile=None, pool_tile=None, pe_after=None,
                 banks=4, bank_need=None, lead=1):
    nc, s, ps, w = core.nc, Sems(core.nc, name), core.ps, core.w
    sizes = [a.shape[1] * a.shape[2] for a in slabs]
    first_tile, released, parts_done = {}, {}, 0
    for t, parts in enumerate(tiles):
        for slab, *_ in parts:
            first_tile.setdefault(slab, t)
            if slab == parts[-1][0]:
                released[slab] = ("tile", t + 1)
            else:
                parts_done += 1
                released[slab] = ("part", parts_done)
    with nc.Block() as block:
        @block.sync
        def _(sp):
            for a in slabs:
                w.load(sp, a)

        def with_splits(eng, split, step, waits):
            def one(n):
                if waits and n >= 2:
                    kind, count = released[n - 2]
                    eng.wait_ge(s.tile_done if kind == "tile" else s.part_done, count)
                split(eng, sizes[n])
            one(0)
            done = 1
            for t in range(len(tiles)):
                while done < len(slabs) and first_tile[done - 1] <= t:
                    one(done)
                    done += 1
                if step:
                    step(eng, s, t)

        @block.scalar
        def _(act):
            with_splits(act, w.split_hi, act_tile, True)

        @block.gpsimd
        def _(pool):
            with_splits(pool, w.split_lo, pool_tile, False)

        @block.vector
        def _(dve):
            for t in range(len(tiles)):
                if dve_tile:
                    dve_tile(dve, s, t)

        @block.tensor
        def _(pe):
            taken = {}
            for t, parts in enumerate(tiles):
                if t >= banks:
                    pe.wait_ge(s.bank_free, bank_need(t) if bank_need else t - banks + 1)
                bank = t % banks
                total = sum(len(part[2]) for part in parts)
                m = 0
                for n, (slab, cols, ks, toks, *own) in enumerate(parts):
                    ahi, alo = own if own else (xhi, xlo)
                    if slab not in taken:
                        taken[slab] = w.take(pe, slabs[slab].shape[1], slabs[slab].shape[2])
                    whi, wlo = taken[slab]
                    width = cols.stop - cols.start
                    for k, xk in ks:
                        first, end = m == 0, m == total - 1
                        if toks is None:
                            mm = products(pe, ps[0:width, bank, 0:ahi.shape[2]], whi, wlo, k, cols, ahi, alo, xk, first, end)
                        else:
                            mm = token_products(pe, ps[:, bank, 0:width], whi, wlo, k, cols, ahi, alo, xk, toks, first, end)
                        m += 1
                    mm.then_inc(s.tile_done if n == len(parts) - 1 else s.part_done, 1)
                if pe_after and t >= lead:
                    pe_after(pe, s, t - lead)
            if pe_after:
                for t in range(max(0, len(tiles) - lead), len(tiles)):
                    pe_after(pe, s, t)
    s.clear()


def feature_tiles(slab0, n_slabs, cols, kt, width=P):
    return [[(slab0 + j, slice(c, min(c + width, cols)), [(k, k) for k in range(kt)], None)]
            for j in range(n_slabs) for c in range(0, cols, width)]


def token_tiles(slab0, n_slabs, cols, kt, token_tiles_n=TT):
    return [[(slab0 + j, slice(0, cols), [(k, k) for k in range(kt)], slice(P * tt, P * tt + P))]
            for j in range(n_slabs) for tt in range(token_tiles_n)]



def setup_stage(core, ins):
    nc, s, ps = core.nc, Sems(core.nc, "setup"), core.ps
    n_tables = (PARAM_TOTAL + P - 1) // P
    with ExitStack() as ctx:
        rows = ctx.enter_context(nc.sbuf_tensor("setup_rows", [P, n_tables, P], fp32))
        xt = ctx.enter_context(nc.sbuf_tensor("setup_x", [P, TT, D], fp32))

        def stores():
            for name, count in PARAM_ROWS:
                src = ins[name].flatten().rearrange("(r c) -> r c", c=P)
                assert src.shape[0] == count, (name, src.shape)
                done = 0
                while done < count:
                    at = PARAM_COL[name] + done
                    m = min(count - done, P - at % P)
                    yield src[done:done + m, :], at // P, at % P
                    done += m
        parts = list(stores())
        with nc.Block() as block:
            @block.sync
            def _(sp):
                sp.dma_start(xt[:, :, :], ins["x"][0].rearrange("(t p) d -> p t d", p=P)).then_inc(s.x_loaded, 16)
                for half in range(2):
                    for c, name in enumerate(("k_norm", "q_norm")):
                        sp.dma_start(core.head_gain[HD * half:HD * half + HD, c:c + 1],
                                     ins[name].flatten().rearrange("(p a) -> p a", a=1)).then_inc(s.gains_loaded, 16)

            @block.scalar
            def _(act):
                for src, table, p0 in parts:
                    act.dma_start(rows[p0:p0 + src.shape[0], table, :], src).then_inc(s.rows_loaded, 16)
                for t in range(TT):
                    for half in range(2):
                        n = 2 * t + half
                        act.wait_ge(s.x_turned, n + 1)
                        act.activation(core.h[:, 4 * half:4 * half + 4, P * t:P * t + P],
                                       ps[:, 1 + n % 4, :].rearrange("p (k c) -> p k c", k=4), ACT.Copy).then_inc(s.x_stored, 1)

            @block.gpsimd
            def _(pool):
                c = Chain(pool, s.pool_chain)
                c(pool.memset(core.ident[:, :], 0.0))
                c(pool.memset(core.head_ones[:, :], 0.0))
                c(pool.memset(core.ones[:, :], 1.0))
                c(pool.memset(core.minus_ones[:, :], -1.0))
                c.wait()
                c(pool.memset(core.head_ones[0:HD, 0:HD], 1.0))
                c.wait()
                c(pool.memset(core.head_ones[HD:P, HD:P], 1.0))
                c.wait()
                pick = lambda out, src, op, fill, sign, base=0: pool.affine_select(
                    out=out[:, :], in_=src[:, :], compare_op=op, fill=fill, base=base,
                    pattern=[[sign, P]], channel_multiplier=-sign)
                c(pick(core.upto, core.ones, ALU.is_ge, 0.0, 1))
                c(pick(core.after, core.ones, ALU.is_gt, 0.0, -1))
                c(pick(core.minus_from, core.minus_ones, ALU.is_ge, 0.0, -1))
                c.wait()
                pick(core.ident, core.ident, ALU.not_equal, 1.0, 1).then_inc(s.ident_ready, 1)

            @block.vector
            def _(dve):
                for i in range(n_tables):
                    m = min(P, PARAM_TOTAL - i * P)
                    dve.wait_ge(s.rows_turned, i + 1)
                    dve.tensor_copy(core.params[:, i * P:i * P + m], ps[:, 0, 0:m]).then_inc(s.rows_stored, 1)
                dve.wait_ge(s.ident_ready, 1)
                dve.tensor_copy(core.ident_r[:, :], core.ident[:, :]).then_inc(s.rows_stored, 1)
                dve.tensor_scalar(core.causal_r[:, :], core.minus_from[:, :], 1e30, None, ALU.mult)\
                   .then_inc(s.rows_stored, 1)
                dve.wait_ge(s.gains_loaded, 64)
                dve.tensor_scalar(core.head_gain[:, 1:2], core.head_gain[:, 1:2], HD ** -0.5, None, ALU.mult)\
                   .then_inc(s.rows_stored, 1)

            @block.tensor
            def _(pe):
                pe.wait_ge(s.ident_ready, 1)
                pe.wait_ge(s.x_loaded, 16)
                for t in range(TT):
                    for half in range(2):
                        n = 2 * t + half
                        if n >= 4:
                            pe.wait_ge(s.x_stored, n - 3)
                        for k in range(4):
                            mm = pe.transpose(ps[:, 1 + n % 4, P * k:P * k + P],
                                              xt[:, t, P * (4 * half + k):P * (4 * half + k) + P], core.ident[:, :])
                        mm.then_inc(s.x_turned, 1)
                pe.wait_ge(s.rows_loaded, 16 * len(parts))
                for i in range(n_tables):
                    m = min(P, PARAM_TOTAL - i * P)
                    if i >= 1:
                        pe.wait_ge(s.rows_stored, i)
                    pe.transpose(ps[:, 0, 0:m], rows[0:m, i, :], core.ident[0:m, 0:m]).then_inc(s.rows_turned, 1)
        s.clear()


def output_stage(core, out):
    nc, s, ps = core.nc, Sems(core.nc, "output"), core.ps
    with nc.sbuf_tensor("output_y", [P, TT, D], fp32) as y, nc.Block() as block:
        @block.tensor
        def _(pe):
            for t in range(TT):
                for half in range(2):
                    n = 2 * t + half
                    if n >= 4:
                        pe.wait_ge(s.copied, n - 3)
                    for k in range(4):
                        mm = pe.transpose(ps[:, n % 4, P * k:P * k + P],
                                          core.h[:, 4 * half + k, P * t:P * t + P], core.ident[:, :])
                    mm.then_inc(s.turned, 1)

        @block.vector
        def _(dve):
            for t in range(TT):
                for half in range(2):
                    n = 2 * t + half
                    dve.wait_ge(s.turned, n + 1)
                    dve.tensor_copy(y[:, t, 512 * half:512 * half + 512], ps[:, n % 4, :]).then_inc(s.copied, 1)

        @block.sync
        def _(sp):
            for t in range(TT):
                sp.wait_ge(s.copied, 2 * t + 2)
                sp.dma_start(out[0, P * t:P * t + P, :], y[:, t, :]).then_inc(core.out_stored, 16)
            sp.wait_ge(core.out_stored, 16 * TT)
    s.clear()


def residual_tile(core, banks=4):
    def step(dve, s, t):
        dve.wait_ge(s.tile_done, t + 1)
        dve.tensor_tensor(core.h[:, t, :], core.h[:, t, :], core.ps[:, t % banks, :], ALU.add).then_inc(s.bank_free, 1)
    return step


def store_tile(core, dst, banks=4):
    def step(dve, s, t):
        dve.wait_ge(s.tile_done, t + 1)
        dve.tensor_copy(dst(t), core.ps[:, t % banks, 0:dst(t).free_size()]).then_inc(s.bank_free, 1)
    return step



def mamba_in_stages(core, ins, z, xs, bc, dt_raw):
    nc, ps, w = core.nc, core.ps, core.w
    w_in = ins["m_in"][0]
    with ExitStack() as ctx:
        xhi = ctx.enter_context(nc.sbuf_tensor("mi_xhi", [P, DK, SEQ], fp32r))
        xlo = ctx.enter_context(nc.sbuf_tensor("mi_xlo", [P, DK, SEQ], fp32r))
        norm_stage(core, "m_norm", core.h, lambda k: core.gain("m_norm", k), xhi, xlo)

        def z_act(act, s, t):
            j, tt = t // TT, t % TT
            act.wait_ge(s.tile_done, t + 1)
            act.activation(z[:, tt, 256 * j:256 * j + 256], ps[:, t % 4, 0:256], ACT.Silu).then_inc(s.bank_free, 1)
        linear_stage(core, "mz", slabs_of(w_in, 256, 0, D_INNER), token_tiles(0, 8, 256, DK), xhi, xlo, act_tile=z_act)

        c0 = D_INNER + CONV_TILES * P
        def dt_dve(dve, s, t):
            dve.wait_ge(s.tile_done, t + 1)
            dve.tensor_copy(dt_raw[:, HEADS * t:HEADS * t + HEADS], ps[:, t % 4, 0:HEADS]).then_inc(s.bank_free, 1)
        linear_stage(core, "mdt", slabs_of(w_in, HEADS, c0, c0 + HEADS), token_tiles(0, 1, HEADS, DK), xhi, xlo,
                     dve_tile=dt_dve)

        conv = ctx.enter_context(nc.sbuf_tensor("mi_conv", [P, 2, SEQ], fp32))
        act_x = ctx.enter_context(nc.sbuf_tensor("mi_actx", [P, 2, SEQ], fp32))

        def conv_dve(dve, s, t):
            c = Chain(dve, s.conv_chain)
            c.n = 3 * t
            bank, acc = t % 4, conv[:, t % 2, :]
            tap = lambda j: core.gain("m_conv_w", j * CONV_TILES + t)
            dve.wait_ge(s.tile_done, t + 1)
            if t >= 2:
                dve.wait_ge(s.silu_done, t - 1)
            c(dve.tensor_scalar(acc, ps[:, bank, :], tap(3), core.gain("m_conv_b", t), ALU.mult, ALU.add))
            for back in (1, 2, 3):
                c.wait()
                i = dve.scalar_tensor_tensor(out=acc[:, back:SEQ], in0=ps[:, bank, 0:SEQ - back], scalar=tap(3 - back),
                                             in1=acc[:, back:SEQ], op0=ALU.mult, op1=ALU.add)
                if back < 3:
                    c(i)
                else:
                    i.then_inc(s.bank_free, 1)
            if 1 <= t <= 16:
                store_x(dve, s, t - 1)

        def store_x(dve, s, t):
            dve.wait_ge(s.x_turned, t + 1)
            dve.tensor_copy(xs[:, :, P * t:P * t + P], ps[:, 4 + t % 2, :].rearrange("p (c f) -> p c f", c=TT))\
               .then_inc(s.x_stored, 1)

        def silu_act(act, s, t):
            act.wait_ge(s.bank_free, t + 1)
            if t < 16:
                if t >= 2:
                    act.wait_ge(s.x_turned, t - 1)
                act.activation(act_x[:, t % 2, :], conv[:, t % 2, :], ACT.Silu).then_inc(s.silu_done, 1)
            else:
                act.activation(bc[:, t - 16, :], conv[:, t % 2, :], ACT.Silu).then_inc(s.silu_done, 1)

        def turn_pe(pe, s, t):
            if t >= 16:
                return
            pe.wait_ge(s.silu_done, t + 1)
            if t >= 2:
                pe.wait_ge(s.x_stored, t - 1)
            for c in range(TT):
                mm = pe.transpose(ps[:, 4 + t % 2, P * c:P * c + P], act_x[:, t % 2, P * c:P * c + P], core.ident[:, :])
            mm.then_inc(s.x_turned, 1)
        linear_stage(core, "mx", slabs_of(w_in, 256, D_INNER, D_INNER + CONV_TILES * P), feature_tiles(0, 12, 256, DK),
                     xhi, xlo, act_tile=silu_act, dve_tile=conv_dve, pe_after=turn_pe)


def dt_stage(core, ins, dt_raw, dt, da, e_from_start, e_to_end, e_chunk, d_skip):
    nc, s, ps = core.nc, Sems(core.nc, "dt"), core.ps
    with ExitStack() as ctx:
        sb = lambda n: ctx.enter_context(nc.sbuf_tensor(f"dt_{n}", [P, P], fp32))
        bias, a_log, x, e, u, ln, t1, rest = (sb(n) for n in ("bias", "a_log", "x", "e", "u", "ln", "t1", "rest"))
        chunks = lambda a: a[:, :].rearrange("p (c h) -> p c h", c=TT)
        every = lambda a: a[:, 0:HEADS].unsqueeze(1).to_broadcast([P, TT, HEADS])
        with nc.Block() as block:
            @block.sync
            def _(sp):
                for dst, name in ((bias, "m_dt_bias"), (a_log, "m_A_log"), (d_skip, "m_D")):
                    sp.dma_start(dst[:, 0:HEADS], ins[name][0].partition_broadcast(P)).then_inc(s.loaded, 16)

            @block.vector
            def _(dve):
                c = Chain(dve, s.chain)
                dve.wait_ge(s.loaded, 48)
                c(dve.tensor_tensor(chunks(x), chunks(dt_raw), every(bias), ALU.add))
                c.wait()
                dve.scalar_tensor_tensor(out=t1[:, :], in0=x[:, :], scalar=-1.0, in1=x[:, :], op0=ALU.mult, op1=ALU.min)\
                   .then_inc(s.neg_abs, 1)
                dve.wait_ge(s.exp_done, 1)
                c(dve.tensor_scalar(u[:, :], e[:, :], 1.0, None, ALU.add))
                c.wait()
                c(dve.tensor_scalar(rest[:, :], u[:, :], -1.0, None, ALU.add))
                c.wait()
                c(dve.tensor_tensor(rest[:, :], e[:, :], rest[:, :], ALU.subtract))
                c(dve.reciprocal(t1[:, :], u[:, :]))
                c.wait()
                c(dve.tensor_tensor(rest[:, :], rest[:, :], t1[:, :], ALU.mult))
                c.wait()
                dve.wait_ge(s.ln_done, 1)
                c(dve.tensor_tensor(rest[:, :], rest[:, :], ln[:, :], ALU.add))
                c.wait()
                c(dve.scalar_tensor_tensor(out=dt[:, :], in0=x[:, :], scalar=0.0, in1=rest[:, :],
                                           op0=ALU.max, op1=ALU.add))
                c.wait()
                dve.wait_ge(s.a_done, 1)
                c(dve.tensor_tensor(chunks(da), chunks(dt), every(a_log), ALU.mult))
                c.wait()
                dve.tensor_scalar(da[:, :], da[:, :], -1.0, None, ALU.mult).then_inc(s.da_ready, 1)
                dve.wait_ge(s.sums_done, 2)
                c(dve.tensor_copy(t1[:, :], ps[:, 0, 0:P]))
                c.wait()
                dve.tensor_tensor(rest[:, :], ps[:, 1, 0:P], t1[:, :], ALU.subtract).then_inc(s.to_end, 1)

            @block.scalar
            def _(act):
                act.wait_ge(s.neg_abs, 1)
                act.activation(e[:, :], t1[:, :], ACT.Exp).then_inc(s.exp_done, 1)
                act.activation(a_log[:, 0:HEADS], a_log[:, 0:HEADS], ACT.Exp).then_inc(s.a_done, 1)
                act.wait_ge(s.exp_done, 1)
                act.activation(ln[:, :], e[:, :], ACT.Ln, bias=1.0).then_inc(s.ln_done, 1)
                act.wait_ge(s.to_end, 1)
                act.activation(e_from_start[:, :], ps[:, 0, 0:P], ACT.Exp).then_inc(s.exp_done, 1)
                act.activation(e_chunk[:, :], ps[:, 1, 0:P], ACT.Exp).then_inc(s.exp_done, 1)
                act.activation(e_to_end[:, :], rest[:, :], ACT.Exp).then_inc(s.exp_done, 1)

            @block.tensor
            def _(pe):
                pe.wait_ge(s.da_ready, 1)
                pe.matmul(ps[:, 0, 0:P], core.upto[:, :], da[:, :], start=True, stop=True).then_inc(s.sums_done, 1)
                pe.matmul(ps[:, 1, 0:P], core.ones[:, :], da[:, :], start=True, stop=True).then_inc(s.sums_done, 1)
        s.clear()


def scan_stage(core, z, xs, bc, dt, da, e_from_start, e_to_end, e_chunk, d_skip):
    nc, s, ps = core.nc, Sems(core.nc, "scan"), core.ps
    GW = HG * HD
    with ExitStack() as ctx:
        sb = lambda n, sh: ctx.enter_context(nc.sbuf_tensor(f"scan_{n}", sh, fp32))
        b_tok = sb("b_tok", [P, TT - 1, GROUPS, P])
        state = sb("state", [P, GROUPS, GW])
        steps, decay = sb("steps", [P, HG, P]), sb("decay", [P, HG, P])
        mix = sb("mix", [P, HG, P])
        cb = sb("cb", [P, 2, P])
        xdt, xend, skip, inter, both = (sb(n, [P, GW]) for n in ("xdt", "xend", "skip", "inter", "both"))
        units = [(c, g) for c in range(TT) for g in range(GROUPS)]
        heads = lambda a: a.rearrange("p (h d) -> p h d", h=HG)
        per_head = lambda a, c, g, width=HD: a[:, HEADS * c + HG * g:HEADS * c + HG * g + HG].unsqueeze(2)\
            .to_broadcast([P, HG, width])
        tok = lambda c: slice(P * c, P * c + P)
        grp = lambda g: slice(GW * g, GW * g + GW)

        with nc.Block() as block:
            @block.gpsimd
            def _(pool):
                for u, (c, g) in enumerate(units):
                    if u >= 1:
                        pool.wait_ge(s.sums_done, u)
                    pool.tensor_tensor(steps[:, :, :], core.upto[:, :].unsqueeze(1).to_broadcast([P, HG, P]),
                                       per_head(da, c, g, P), ALU.mult).then_inc(s.steps_ready, 1)
                    if c < TT - 1:
                        pool.wait_ge(s.xdt_ready, u + 1)
                        if u >= 1:
                            pool.wait_ge(s.grown, u)
                        pool.tensor_tensor(heads(xend[:, :]), heads(xdt[:, :]), per_head(e_to_end, c, g), ALU.mult)\
                            .then_inc(s.xend_ready, 1)
                    if u >= 1:
                        pool.wait_ge(s.skip_used, u)
                    pool.tensor_tensor(heads(skip[:, :]), heads(xs[:, c, grp(g)]),
                                       d_skip[:, HG * g:HG * g + HG].unsqueeze(2).to_broadcast([P, HG, HD]), ALU.mult)\
                        .then_inc(s.skip_ready, 1)

            @block.scalar
            def _(act):
                for c in range(TT - 1):
                    act.wait_ge(s.b_turned, c + 1)
                    act.activation(b_tok[:, c, :, :].rearrange("p g n -> p (g n)"), ps[:, 7, :], ACT.Copy)\
                       .then_inc(s.b_stored, 1)
                for u in range(len(units)):
                    act.wait_ge(s.sums_done, u + 1)
                    if u >= 1:
                        act.wait_ge(s.mix_ready, u)
                    act.activation(decay[:, :, :].rearrange("p h l -> p (h l)"),
                                   ps[:, 1:3, :].rearrange("p b l -> p (b l)"), ACT.Exp).then_inc(s.decay_ready, 1)

            @block.vector
            def _(dve):
                c_ = Chain(dve, s.dve_chain)
                for u, (c, g) in enumerate(units):
                    dve.wait_ge(s.cb_done, u + 1)
                    c_(dve.tensor_tensor(cb[:, u % 2, :], ps[:, 0, 0:P], core.upto[:, :], ALU.mult))
                    if u >= 1:
                        dve.wait_ge(s.intra_done, u)
                        if units[u - 1][0] < TT - 1:
                            dve.wait_ge(s.xend_ready, min(u, 4 * (TT - 1)))
                    dve.tensor_tensor(heads(xdt[:, :]), heads(xs[:, c, grp(g)]), per_head(dt, c, g), ALU.mult)\
                       .then_inc(s.xdt_ready, 1)
                    c_.wait()
                    dve.wait_ge(s.decay_ready, u + 1)
                    dve.tensor_tensor(mix[:, :, :], decay[:, :, :], cb[:, u % 2, :].unsqueeze(1).to_broadcast([P, HG, P]),
                                      ALU.mult).then_inc(s.mix_ready, 1)
                    dve.wait_ge(s.skip_ready, u + 1)
                    dve.wait_ge(s.intra_done, u + 1)
                    if c > 0:
                        dve.wait_ge(s.inter_done, u - 3)
                        c_(dve.tensor_tensor(heads(inter[:, :]), heads(ps[:, 4, :]), per_head(e_from_start, c, g), ALU.mult))
                        c_.wait()
                        c_(dve.tensor_tensor(both[:, :], ps[:, 3, :], inter[:, :], ALU.add))
                        c_.wait()
                        dve.tensor_tensor(both[:, :], both[:, :], skip[:, :], ALU.add).then_inc(s.skip_used, 1)
                    else:
                        dve.tensor_tensor(both[:, :], ps[:, 3, :], skip[:, :], ALU.add).then_inc(s.skip_used, 1)
                    dve.wait_ge(s.skip_used, u + 1)
                    dve.tensor_tensor(z[:, c, grp(g)], both[:, :], z[:, c, grp(g)], ALU.mult).then_inc(s.y_ready, 1)
                    if c < TT - 1:
                        dve.wait_ge(s.grown, u + 1)
                        if c == 0:
                            dve.tensor_copy(state[:, g, :], ps[:, 5, :]).then_inc(s.state_ready, 1)
                        else:
                            c_(dve.tensor_tensor(heads(state[:, g, :]), heads(state[:, g, :]),
                                                 per_head(e_chunk, c, g), ALU.mult))
                            c_.wait()
                            dve.tensor_tensor(state[:, g, :], state[:, g, :], ps[:, 5, :], ALU.add)\
                               .then_inc(s.state_ready, 1)

            @block.tensor
            def _(pe):
                for c in range(TT - 1):
                    if c >= 1:
                        pe.wait_ge(s.b_stored, c)
                    for g in range(GROUPS):
                        mm = pe.transpose(ps[:, 7, P * g:P * g + P], bc[:, g, tok(c)], core.ident[:, :])
                    mm.then_inc(s.b_turned, 1)

                def front(u):
                    c, g = units[u]
                    if u >= 1:
                        pe.wait_ge(s.xdt_ready, u)
                    pe.matmul(ps[:, 0, 0:P], bc[:, g, tok(c)], bc[:, GROUPS + g, tok(c)], start=True, stop=True)\
                      .then_inc(s.cb_done, 1)
                    pe.wait_ge(s.steps_ready, u + 1)
                    if u >= 1:
                        pe.wait_ge(s.decay_ready, u)
                    for half in range(2):
                        mm = pe.matmul(ps[:, 1 + half, :], core.after[:, :],
                                       steps[:, 4 * half:4 * half + 4, :].rearrange("p h l -> p (h l)"),
                                       start=True, stop=True)
                    mm.then_inc(s.sums_done, 1)

                front(0)
                for u, (c, g) in enumerate(units):
                    if u + 1 < len(units):
                        front(u + 1)
                    if c > 0:
                        pe.wait_ge(s.state_ready, 4 * (c - 1) + g + 1)
                        if u >= 5:
                            pe.wait_ge(s.y_ready, u)
                        pe.matmul(ps[:, 4, :], bc[:, GROUPS + g, tok(c)], state[:, g, :], start=True, stop=True)\
                          .then_inc(s.inter_done, 1)
                    pe.wait_ge(s.mix_ready, u + 1)
                    if u >= 1:
                        pe.wait_ge(s.y_ready, u)
                    for h in range(HG):
                        mm = pe.matmul(ps[:, 3, HD * h:HD * h + HD], mix[:, h, :], xdt[:, HD * h:HD * h + HD],
                                       start=True, stop=True)
                    mm.then_inc(s.intra_done, 1)
                    if c < TT - 1:
                        pe.wait_ge(s.xend_ready, u + 1)
                        if c == 0 and g == 0:
                            pe.wait_ge(s.b_stored, TT - 1)
                        if u >= 1:
                            pe.wait_ge(s.state_ready, u)
                        pe.matmul(ps[:, 5, :], b_tok[:, c, g, :], xend[:, :], start=True, stop=True).then_inc(s.grown, 1)
        s.clear()


def y_norm_stage(core, y, yhi, ylo):
    nc, s, ps = core.nc, Sems(core.nc, "ynorm"), core.ps
    GW = HG * HD
    FT = D_INNER // P
    with ExitStack() as ctx:
        sb = lambda n, sh: ctx.enter_context(nc.sbuf_tensor(f"ynorm_{n}", sh, fp32))
        junk, total = sb("junk", [P, 2, GW]), sb("total", [P, TT * GROUPS])
        root, inv = sb("root", [P, TT * GROUPS]), sb("inv", [P, TT * GROUPS])
        tmp = core.split_buf
        with nc.Block() as block:
            @block.scalar
            def _(act):
                for g in range(GROUPS):
                    for c in range(TT):
                        n = g * TT + c
                        if n >= 2:
                            act.wait_ge(s.squared, n - 1)
                        act.activation(junk[:, n % 2, :], y[:, c, GW * g:GW * g + GW], ACT.Square,
                                       accum_out=total[:, n:n + 1]).then_inc(s.squared, 1)
                act.wait_ge(s.mean_ready, 1)
                act.activation(root[:, :], total[:, :], ACT.Sqrt).then_inc(s.root_ready, 1)
                for f in range(FT):
                    act.wait_ge(s.gained, f + 1)
                    act.activation(yhi[:, f, :], tmp[f % 2][:, :], ACT.Copy).then_inc(s.hi_done, 1)

            @block.vector
            def _(dve):
                dve.wait_ge(s.squared, TT * GROUPS)
                dve.tensor_scalar(total[:, :], total[:, :], 1.0 / GW, EPS, ALU.mult, ALU.add).then_inc(s.mean_ready, 1)
                dve.wait_ge(s.root_ready, 1)
                dve.reciprocal(inv[:, :], root[:, :]).then_inc(s.inv_ready, 1)
                dve.wait_ge(s.inv_ready, 1)
                for g in range(GROUPS):
                    for c in range(TT):
                        n = g * TT + c
                        dve.tensor_scalar(y[:, c, GW * g:GW * g + GW], y[:, c, GW * g:GW * g + GW],
                                          inv[:, n:n + 1], None, ALU.mult).then_inc(s.scaled, 1)
                for f in range(FT):
                    dve.wait_ge(s.turned, f + 1)
                    if f >= 2:
                        dve.wait_ge(s.lo_done, f - 1)
                    dve.tensor_scalar(tmp[f % 2][:, :], ps[:, f % 4, :], core.gain("m_ynorm", f), None, ALU.mult)\
                       .then_inc(s.gained, 1)

            @block.gpsimd
            def _(pool):
                for f in range(FT):
                    pool.wait_ge(s.hi_done, f + 1)
                    pool.tensor_tensor(ylo[:, f, :], tmp[f % 2][:, :], yhi[:, f, :].bitcast(fp32), ALU.subtract)\
                        .then_inc(s.lo_done, 1)

            @block.tensor
            def _(pe):
                for f in range(FT):
                    pe.wait_ge(s.scaled, TT * (f // 4 + 1))
                    if f >= 4:
                        pe.wait_ge(s.gained, f - 3)
                    for c in range(TT):
                        mm = pe.transpose(ps[:, f % 4, P * c:P * c + P], y[:, c, P * f:P * f + P], core.ident[:, :])
                    mm.then_inc(s.turned, 1)
        s.clear()


def mamba(core, ins):
    nc = core.nc
    with ExitStack() as ctx:
        z = ctx.enter_context(nc.sbuf_tensor("mamba_z", [P, TT, D_INNER], fp32))
        with ExitStack() as inner:
            sb = lambda n, sh: inner.enter_context(nc.sbuf_tensor(f"mamba_{n}", sh, fp32))
            xs = sb("xs", [P, TT, D_INNER])
            bc = sb("bc", [P, 2 * GROUPS, SEQ])
            dt_raw, dt, da, e1, e2, e3 = (sb(n, [P, P]) for n in ("dt_raw", "dt", "da", "e_start", "e_end", "e_chunk"))
            d_skip = sb("d_skip", [P, HEADS])
            mamba_in_stages(core, ins, z, xs, bc, dt_raw)
            dt_stage(core, ins, dt_raw, dt, da, e1, e2, e3, d_skip)
            scan_stage(core, z, xs, bc, dt, da, e1, e2, e3, d_skip)
        yhi = ctx.enter_context(nc.sbuf_tensor("mamba_yhi", [P, 16, SEQ], fp32r))
        ylo = ctx.enter_context(nc.sbuf_tensor("mamba_ylo", [P, 16, SEQ], fp32r))
        y_norm_stage(core, z, yhi, ylo)
        linear_stage(core, "mout", slabs_of(ins["m_out"][0], P), feature_tiles(0, DK, P, 16), yhi, ylo,
                     dve_tile=residual_tile(core))



def ple_stages(core, ins, i):
    nc, ps = core.nc, core.ps
    with ExitStack() as ctx:
        sb = lambda n, sh, d=fp32: ctx.enter_context(nc.sbuf_tensor(f"ple{i}_{n}", sh, d))
        xhi, xlo = sb("xhi", [P, DK + 2, SEQ], fp32r), sb("xlo", [P, DK + 2, SEQ], fp32r)
        p_tok, sig, prod = sb("p", [P, TT, 2 * P]), sb("sig", [P, 2, SEQ]), sb("prod", [P, 2, SEQ])
        s = Sems(nc, f"ple{i}_p")
        with nc.Block() as block:
            @block.sync
            def _(sp):
                sp.dma_start(p_tok[:, :, :], ins["p"][i, 0].rearrange("(t p) d -> p t d", p=P)).then_inc(s.loaded, 16)

            @block.tensor
            def _(pe):
                pe.wait_ge(s.loaded, 16)
                for k in range(2):
                    for t in range(TT):
                        mm = pe.transpose(ps[:, k, P * t:P * t + P], p_tok[:, t, P * k:P * k + P], core.ident[:, :])
                    mm.then_inc(s.turned, 1)

            @block.scalar
            def _(act):
                for k in range(2):
                    act.wait_ge(s.turned, k + 1)
                    act.activation(core.split_buf[k][:, :], ps[:, k, :], ACT.Copy).then_inc(s.copied, 1)
                    act.wait_ge(s.copied, k + 1)
                    act.activation(xhi[:, DK + k, :], core.split_buf[k][:, :], ACT.Copy).then_inc(s.hi_done, 1)

            @block.gpsimd
            def _(pool):
                for k in range(2):
                    pool.wait_ge(s.hi_done, k + 1)
                    pool.tensor_tensor(xlo[:, DK + k, :], core.split_buf[k][:, :], xhi[:, DK + k, :].bitcast(fp32),
                                       ALU.subtract).then_inc(s.lo_done, 1)
        s.clear()
        norm_stage(core, f"ple{i}_norm", core.h, lambda k: core.gain("ple_norm", i * DK + k), xhi, xlo)

        add = lambda dve, f, prod: dve.tensor_tensor(core.h[:, f, :], core.h[:, f, :], prod, ALU.add)
        gated_stage(core, f"ple{i}", ins["ple_proj"][i], [(0, DK), (1, DK + 1)], xhi, xlo,
                    ins["ple_gate"][i], 0, xhi, xlo, sig, prod, None, add)


def gated_stage(core, name, w_proj, proj_ks, phi, plo, w_gate, g0, xhi, xlo, sig, prod, gate_bias, finish):
    ps = core.ps
    slabs, tiles, order = [], [], []
    for half in range(2):
        slabs += slabs_of(w_proj, 512, 512 * half, 512 * half + 512)
        slabs += slabs_of(w_gate, 256, g0 + 512 * half, g0 + 512 * half + 512)
        for n in range(4):
            order.append(("proj", 4 * half + n))
            tiles.append([(3 * half, slice(P * n, P * n + P), proj_ks, None, phi, plo)])
        for n in range(4):
            order.append(("gate", 4 * half + n))
            tiles.append([(3 * half + 1 + n // 2, slice(P * (n % 2), P * (n % 2) + P), [(k, k) for k in range(DK)], None)])

    def sig_act(act, s, t):
        kind, f = order[t]
        if kind == "gate":
            act.wait_ge(s.tile_done, t + 1)
            if f >= 2:
                act.wait_ge(s.bank_free, f - 1)
            act.activation(sig[:, f % 2, :], ps[:, t % 8, :], ACT.Sigmoid,
                           bias=gate_bias(f) if gate_bias else 0.0).then_inc(s.sig_done, 1)

    def add_dve(dve, s, t):
        kind, f = order[t]
        if kind == "proj":
            return
        dve.wait_ge(s.sig_done, f + 1)
        if f >= 2:
            dve.wait_ge(s.added, f - 1)
        dve.tensor_tensor(prod[:, f % 2, :], ps[:, (t - 4) % 8, :], sig[:, f % 2, :], ALU.mult).then_inc(s.bank_free, 1)
        dve.wait_ge(s.bank_free, f + 1)
        finish(dve, f, prod[:, f % 2, :]).then_inc(s.added, 1)
    linear_stage(core, name, slabs, tiles, xhi, xlo, act_tile=sig_act, dve_tile=add_dve, banks=8,
                 bank_need=lambda t: t % 4 + 1)



def head_norm_steps(core, name, dst, gain_col, sq, root, inv, banks=4):
    ps = core.ps

    def act_step(act, s, t):
        act.wait_ge(s.tile_done, t + 1)
        if t >= 2:
            act.wait_ge(s.sq_summed, t - 1)
        act.activation(sq[:, t % 2, :], ps[:, t % banks, :], ACT.Square).then_inc(s.sq_ready, 1)
        if t >= 1:
            act_root(act, s, t - 1)

    def act_root(act, s, t):
        act.wait_ge(s.mean_ready, t + 1)
        act.activation(root[:, t % 2, :], inv[:, t % 2, :], ACT.Sqrt).then_inc(s.root_ready, 1)

    def pe_sum(pe, s, t):
        pe.wait_ge(s.sq_ready, t + 1)
        if t >= 2:
            pe.wait_ge(s.mean_ready, t - 1)
        pe.matmul(ps[:, 4 + t % 2, :], core.head_ones[:, :], sq[:, t % 2, :], start=True, stop=True)\
          .then_inc(s.sq_summed, 1)

    def dve_step(dve, s, t):
        if t >= 1:
            dve_finish(dve, s, t - 1)

    def dve_mean(dve, s, t):
        dve.wait_ge(s.sq_summed, t + 1)
        if t >= 2:
            dve.wait_ge(s.bank_free, t - 1)
        dve.tensor_scalar(inv[:, t % 2, :], ps[:, 4 + t % 2, :], 1.0 / HD, EPS, ALU.mult, ALU.add).then_inc(s.mean_ready, 1)

    def dve_finish(dve, s, t):
        dve_mean(dve, s, t)
        dve.wait_ge(s.root_ready, t + 1)
        dve.reciprocal(inv[:, t % 2, :], root[:, t % 2, :]).then_inc(s.inv_ready, 1)
        dve.wait_ge(s.inv_ready, t + 1)
        dve.scalar_tensor_tensor(out=dst[:, t, :], in0=ps[:, t % banks, :], scalar=core.head_gain[:, gain_col:gain_col + 1],
                                 in1=inv[:, t % 2, :], op0=ALU.mult, op1=ALU.mult).then_inc(s.bank_free, 1)
    return act_step, act_root, pe_sum, dve_step, dve_finish


def head_norm_linear(core, name, w, c0, dst, gain_col, xhi, xlo):
    nc = core.nc
    with ExitStack() as ctx:
        sb = lambda n: ctx.enter_context(nc.sbuf_tensor(f"{name}_{n}", [P, 2, SEQ], fp32))
        sq, root, inv = sb("sq"), sb("root"), sb("inv")
        a, a_root, pe_sum, d, d_fin = head_norm_steps(core, name, dst, gain_col, sq, root, inv)

        def act_tile(act, s, t):
            a(act, s, t)
            if t == DK - 1:
                a_root(act, s, t)

        def dve_tile(dve, s, t):
            d(dve, s, t)
            if t == DK - 1:
                d_fin(dve, s, t)
        linear_stage(core, name, slabs_of(w, 256, c0, c0 + D), feature_tiles(0, 4, 256, DK), xhi, xlo,
                     act_tile=act_tile, dve_tile=dve_tile, pe_after=pe_sum)


SB_OFF = [0, 512, 896 + 128, 896]
SB_W = [SEQ - P * i for i in range(TT)]
SB_ALL = sum(SB_W)


def stick_attention_stage(core, qf, kf, v, gate, ohi, olo):
    nc, s, ps = core.nc, Sems(core.nc, "stick"), core.ps
    HN = D // HD
    with ExitStack() as ctx:
        sb = lambda n, sh: ctx.enter_context(nc.sbuf_tensor(f"stick_{n}", sh, fp32))
        mag, ex = sb("mag", [P, SB_ALL]), sb("ex", [P, SB_ALL])
        sp_, wt = sb("sp", [P, 2, SB_ALL]), sb("wt", [P, 2, SB_ALL])
        tmp = core.split_buf
        banks = lambda h: ps[:, 3 * (h % 2):3 * (h % 2) + 3, :].rearrange("p b n -> p (b n)")[:, 0:SB_ALL]
        part = lambda a, i, lo=0, n=None: a[:, SB_OFF[i] + lo:SB_OFF[i] + lo + (SB_W[i] - lo if n is None else n)]

        with nc.Block() as block:
            @block.tensor
            def _(pe):
                def scores(h):
                    t, r = h // 2, HD * (h % 2)
                    if h >= 2:
                        pe.wait_ge(s.weights_out, h - 1)
                    for i in (0, 1, 3, 2):
                        mm = pe.matmul(part(banks(h), i), kf[r:r + HD, t, P * i:P * i + P],
                                       qf[r:r + HD, t, P * i:SEQ], start=(i != 3), stop=False, skip_group_check=True)
                        mm = pe.matmul(part(banks(h), i, 0, P), core.ident_r[:, :], core.causal_r[:, :],
                                       start=False, stop=False, skip_group_check=True)
                    mm.then_inc(s.scores_done, 1)

                def suffix(h):
                    pe.wait_ge(s.sp_made, h + 1)
                    a = sp_[:, h % 2, :]
                    for i in range(TT):
                        mm = pe.matmul(part(banks(h), i), core.minus_from[:, :], part(a, i), start=False,
                                       stop=(i == TT - 1), skip_group_check=True)
                        for j in range(i + 1, TT):
                            mm = pe.matmul(part(banks(h), i, P * (j - i)), core.minus_ones[:, :], part(a, j),
                                           start=False, stop=(j == TT - 1), skip_group_check=True)
                    mm.then_inc(s.logs_done, 1)

                def values(h):
                    t, r = h // 2, HD * (h % 2)
                    pe.wait_ge(s.weights_out, h + 1)
                    if h % 2 == 0 and t >= 2:
                        pe.wait_ge(s.out_used, t - 1)
                    for i in range(TT):
                        mm = pe.matmul(ps[r:r + HD, 6 + t % 2, P * i:SEQ], v[:, i, HD * h:HD * h + HD],
                                       part(wt[:, h % 2, :], i), start=(i == 0), stop=(i == TT - 1),
                                       skip_group_check=True)
                    mm.then_inc(s.values_done, 1)

                for h in range(HN + 2):
                    if h < HN:
                        scores(h)
                    if 1 <= h <= HN:
                        suffix(h - 1)
                    if h >= 2:
                        values(h - 2)

            @block.scalar
            def _(act):
                def high(act, t):
                    act.wait_ge(s.out_used, t + 1)
                    act.activation(ohi[:, t, :], tmp[t % 2][:, :], ACT.Copy).then_inc(s.hi_done, 1)

                def first(h):
                    act.wait_ge(s.scores_done, h + 1)
                    if h >= 1:
                        act.wait_ge(s.exp_done, h)
                    act.activation(mag[:, :], banks(h), ACT.Abs).then_inc(s.mag_done, 1)
                    act.wait_ge(s.mag_done, h + 1)
                    if h >= 1:
                        act.wait_ge(s.sp_made, h)
                    act.activation(ex[:, :], mag[:, :], ACT.Exp, scale=-1.0).then_inc(s.exp_done, 1)
                    act.wait_ge(s.exp_done, h + 1)
                    act.activation(ex[:, :], ex[:, :], ACT.Ln, bias=1.0).then_inc(s.ln_done, 1)

                def second(h):
                    act.wait_ge(s.logs_done, h + 1)
                    if h >= 2:
                        act.wait_ge(s.values_done, h - 1)
                    act.activation(wt[:, h % 2, :], banks(h), ACT.Exp).then_inc(s.weights_out, 1)

                for h in range(HN + 1):
                    if h < HN:
                        first(h)
                    if h >= 1:
                        second(h - 1)
                    if h >= 4 and h % 2 == 0:
                        high(act, h // 2 - 2)
                high(act, HN // 2 - 1)

            @block.vector
            def _(dve):
                def gated(t):
                    dve.wait_ge(s.values_done, 2 * t + 2)
                    if t >= 2:
                        dve.wait_ge(s.lo_done, t - 1)
                    dve.tensor_tensor(tmp[t % 2][:, :], gate[:, t, :], ps[:, 6 + t % 2, :], ALU.mult).then_inc(s.out_used, 1)

                for h in range(HN):
                    dve.wait_ge(s.ln_done, h + 1)
                    if h >= 2:
                        dve.wait_ge(s.logs_done, h - 1)
                    dve.scalar_tensor_tensor(out=sp_[:, h % 2, :], in0=banks(h), scalar=0.0, in1=ex[:, :],
                                             op0=ALU.max, op1=ALU.add).then_inc(s.sp_made, 1)
                    if h >= 3 and h % 2 == 1:
                        gated((h - 3) // 2)
                gated(HN // 2 - 1)

            @block.gpsimd
            def _(pool):
                def low(t):
                    pool.wait_ge(s.hi_done, t + 1)
                    pool.tensor_tensor(olo[:, t, :], tmp[t % 2][:, :], ohi[:, t, :].bitcast(fp32), ALU.subtract)\
                        .then_inc(s.lo_done, 1)
                for t in range(HN // 2 - 1):
                    low(t)
                low(HN // 2 - 1)
        s.clear()


def stick_breaking(core, ins):
    nc, ps = core.nc, core.ps
    with ExitStack() as ctx:
        sb = lambda n, sh, d=fp32: ctx.enter_context(nc.sbuf_tensor(f"sb_{n}", sh, d))
        kf, qf, v, gate = (sb(n, [P, DK, SEQ]) for n in ("k", "q", "v", "gate"))
        v = v[:, :, :].rearrange("p a b -> p (a b)").rearrange("p (t n) -> p t n", t=TT)
        xhi, xlo = sb("xhi", [P, DK, SEQ], fp32r), sb("xlo", [P, DK, SEQ], fp32r)
        norm_stage(core, "kvn", core.h, lambda k: core.gain("kv_norm", k), xhi, xlo)
        head_norm_linear(core, "sbk", ins["w_kv"], 0, kf, 0, xhi, xlo)
        linear_stage(core, "sbv", slabs_of(ins["w_kv"], 256, D, 2 * D), token_tiles(0, 4, 256, DK), xhi, xlo,
                     dve_tile=store_tile(core, lambda t: v[:, t % TT, 256 * (t // TT):256 * (t // TT) + 256]))
        norm_stage(core, "sn", core.h, lambda k: core.gain("s_norm", k), xhi, xlo)
        head_norm_linear(core, "sbq", ins["s_in"][0], 0, qf, 1, xhi, xlo)

        def silu_act(act, s, t):
            act.wait_ge(s.tile_done, t + 1)
            act.activation(gate[:, t, :], ps[:, t % 4, :], ACT.Silu).then_inc(s.bank_free, 1)
        linear_stage(core, "sbg", slabs_of(ins["s_in"][0], 256, D, 2 * D), feature_tiles(0, 4, 256, DK), xhi, xlo,
                     act_tile=silu_act)
        stick_attention_stage(core, qf, kf, v, gate, xhi, xlo)
        linear_stage(core, "sbo", slabs_of(ins["s_out"][0], 256), feature_tiles(0, 4, 256, DK), xhi, xlo,
                     dve_tile=residual_tile(core))



def split_stage(core, name, src, hi, lo, tiles):
    nc, s = core.nc, Sems(core.nc, name)
    with nc.Block() as block:
        @block.scalar
        def _(act):
            for k in range(tiles):
                act.activation(hi[:, k, :], src[:, k, :], ACT.Copy).then_inc(s.hi_done, 1)

        @block.gpsimd
        def _(pool):
            for k in range(0, tiles, 2):
                pool.wait_ge(s.hi_done, k + 1)
                pool.tensor_tensor(lo[:, k, :], src[:, k, :], hi[:, k, :].bitcast(fp32), ALU.subtract).then_inc(s.lo_done, 1)

        @block.vector
        def _(dve):
            for k in range(1, tiles, 2):
                dve.wait_ge(s.hi_done, k + 1)
                dve.tensor_tensor(lo[:, k, :], src[:, k, :], hi[:, k, :].bitcast(fp32), ALU.subtract).then_inc(s.lo_done, 1)
    s.clear()


def centred_conv(dve, c, acc, x, taps, bias=None):
    c(dve.tensor_scalar(acc, x, taps[1], None, ALU.mult))
    c.wait()
    c(dve.scalar_tensor_tensor(out=acc[:, 1:SEQ], in0=x[:, 0:SEQ - 1], scalar=taps[0], in1=acc[:, 1:SEQ],
                               op0=ALU.mult, op1=ALU.add))
    c.wait()
    return dve.scalar_tensor_tensor(out=acc[:, 0:SEQ - 1], in0=x[:, 1:SEQ], scalar=taps[2], in1=acc[:, 0:SEQ - 1],
                                    op0=ALU.mult, op1=ALU.add)


def hyena_in(core, ins, xhi, xlo, v_tok, x1_tok, x2f):
    nc, ps = core.nc, core.ps
    with ExitStack() as ctx:
        conv = ctx.enter_context(nc.sbuf_tensor("hyin_conv", [P, 2, SEQ], fp32))

        def conv_dve(dve, s, t):
            c = Chain(dve, s.conv_chain)
            c.n = 2 * t
            acc = conv[:, t % 2, :] if t < 8 else x2f[:, t - 8, :]
            dve.wait_ge(s.tile_done, t + 1)
            if 2 <= t < 8:
                dve.wait_ge(s.turned, t - 1)
            centred_conv(dve, c, acc, ps[:, t % 4, :],
                         [core.gain("hy_short_w_2", 12 * j + t) for j in range(3)]).then_inc(s.bank_free, 1)

        def turn_pe(pe, s, t):
            if t >= 8:
                return
            pe.wait_ge(s.bank_free, t + 1)
            if t >= 2:
                pe.wait_ge(s.stored, t - 1)
            for c in range(TT):
                mm = pe.transpose(ps[:, 4 + t % 2, P * c:P * c + P], conv[:, t % 2, P * c:P * c + P], core.ident[:, :])
            mm.then_inc(s.turned, 1)

        def store_act(act, s, t):
            if 1 <= t <= 8:
                u = t - 1
                dst = (v_tok if u < 4 else x1_tok)[:, :, P * (u % 4):P * (u % 4) + P]
                act.wait_ge(s.turned, u + 1)
                act.activation(dst, ps[:, 4 + u % 2, :].rearrange("p (c f) -> p c f", c=TT), ACT.Copy).then_inc(s.stored, 1)
        linear_stage(core, "hyin", slabs_of(ins["w_in_2"][0], 256, 0, 3 * HY), feature_tiles(0, 6, 256, DK), xhi, xlo,
                     act_tile=store_act, dve_tile=conv_dve, pe_after=turn_pe)


def short_conv_in(core, ins, xhi, xlo, yc):
    nc, ps = core.nc, core.ps
    c0 = 3 * HY + 3 * HY
    with ExitStack() as ctx:
        sb = lambda n: ctx.enter_context(nc.sbuf_tensor(f"scin_{n}", [P, 4, SEQ], fp32))
        cg, cx = sb("c"), sb("cx")
        slabs = slabs_of(ins["w_in_2"][0], 256, c0 + HY, c0 + 3 * HY) + slabs_of(ins["w_in_2"][0], 256, c0, c0 + HY)

        def step(dve, s, t):
            c = Chain(dve, s.chain)
            f = t % 4
            dve.wait_ge(s.tile_done, t + 1)
            if t < 4:
                dve.tensor_copy(cg[:, f, :], ps[:, t % 4, :]).then_inc(s.bank_free, 1)
            elif t < 8:
                dve.wait_ge(s.bank_free, f + 1)
                dve.tensor_tensor(cx[:, f, :], cg[:, f, :], ps[:, t % 4, :], ALU.mult).then_inc(s.bank_free, 1)
            else:
                c.n = 3 * f
                dve.wait_ge(s.bank_free, 4 + f + 1)
                c(centred_conv(dve, c, cg[:, f, :], cx[:, f, :], [core.gain("sc_conv_w_2", 4 * j + f) for j in range(3)]))
                c.wait()
                dve.tensor_tensor(yc[:, f, :], cg[:, f, :], ps[:, t % 4, :], ALU.mult).then_inc(s.bank_free, 1)
        linear_stage(core, "scin", slabs, feature_tiles(0, 6, 256, DK), xhi, xlo, dve_tile=step)


def filter_basis_stage(core, ins, hidden):
    nc, s, ps = core.nc, Sems(core.nc, "filt"), core.ps
    H, E = 64, 33
    two_pi = 2 * math.pi
    c1 = 6.28125
    c2 = float(np.float32(two_pi - c1))
    c3 = float(np.float32(two_pi - c1 - c2))
    magic = 1.5 * 2.0 ** 23
    pi = float(np.nextafter(np.float32(math.pi), np.float32(0)))
    with ExitStack() as ctx:
        sb = lambda n, sh: ctx.enter_context(nc.sbuf_tensor(f"filt_{n}", sh, fp32))
        w1, w2, emb = sb("w1", [E, H]), sb("w2", [H, H]), sb("emb", [E, SEQ])
        cols = sb("cols", [H, 4])
        arg, turns, first = sb("arg", [H, SEQ]), sb("turns", [H, SEQ]), sb("first", [H, SEQ])
        with nc.Block() as block:
            @block.sync
            def _(sp):
                col = lambda a: a.rearrange("(p a) -> p a", a=1)
                for dst, src in ((w1[:, :], ins["hy_w1_2"][0]), (w2[:, :], ins["hy_w2_2"][0]), (emb[:, :], ins["pos_emb"]),
                                 (cols[:, 0:1], col(ins["hy_b1_2"][0])), (cols[:, 1:2], col(ins["hy_b2_2"][0])),
                                 (cols[:, 2:3], col(ins["hy_freq_2"][0, 0])), (cols[:, 3:4], col(ins["hy_freq_2"][0, 1]))):
                    sp.dma_start(dst, src).then_inc(s.loaded, 16)

            @block.tensor
            def _(pe):
                pe.wait_ge(s.loaded, 16 * 7)
                pe.matmul(ps[0:H, 0, :], w1[:, :], emb[:, :], start=True, stop=True).then_inc(s.product, 1)
                pe.wait_ge(s.sine, 1)
                pe.matmul(ps[0:H, 1, :], w2[:, :], first[:, :], start=True, stop=True).then_inc(s.product, 1)

            @block.vector
            def _(dve):
                c = Chain(dve, s.chain)
                dve.wait_ge(s.loaded, 16 * 7)
                for n in range(2):
                    dve.wait_ge(s.product, n + 1)
                    if n:
                        dve.wait_ge(s.sine, 1)
                    c(dve.tensor_scalar(arg[:, :], ps[0:H, n, :], cols[:, n:n + 1], cols[:, 2 + n:3 + n], ALU.add, ALU.mult))
                    c.wait()
                    c(dve.tensor_scalar(turns[:, :], arg[:, :], 1.0 / two_pi, magic, ALU.mult, ALU.add))
                    c.wait()
                    c(dve.tensor_scalar(turns[:, :], turns[:, :], -magic, None, ALU.add))
                    for part in (c1, c2, c3):
                        c.wait()
                        c(dve.scalar_tensor_tensor(out=arg[:, :], in0=turns[:, :], scalar=-part, in1=arg[:, :],
                                                   op0=ALU.mult, op1=ALU.add))
                    c.wait()
                    dve.tensor_scalar(arg[:, :], arg[:, :], pi, -pi, ALU.min, ALU.max).then_inc(s.reduced, 1)

            @block.scalar
            def _(act):
                for n, dst in ((0, first), (1, hidden)):
                    act.wait_ge(s.reduced, n + 1)
                    act.activation(dst[:, :], arg[:, :], ACT.Sin).then_inc(s.sine, 1)
        s.clear()


def filter_stage(core, ins, order, hidden, su_hi, su_lo, di_hi, di_lo):
    nc, s, ps = core.nc, Sems(core.nc, f"fl{order}"), core.ps
    with ExitStack() as ctx:
        sb = lambda n, sh: ctx.enter_context(nc.sbuf_tensor(f"fl{order}_{n}", sh, fp32))
        w3, decay = sb("w3", [64, 2, HY]), sb("decay", [P, 2, HY])
        fwd, bwd, tmp, bias = sb("fwd", [P, 2, HY]), sb("bwd", [P, 2, HY]), sb("tmp", [P, 2, HY]), sb("bias", [1, HY])
        with nc.Block() as block:
            @block.sync
            def _(sp):
                for direction in range(2):
                    c0 = (2 * direction + order) * HY
                    sp.dma_start(w3[:, direction, :], ins["hy_w3_2"][0, :, c0:c0 + HY]).then_inc(s.loaded, 16)
                sp.dma_start(bias[:, :], ins["hy_bias_2"][0, order:order + 1, :]).then_inc(s.loaded, 16)
                for t in range(TT):
                    if t >= 2:
                        sp.wait_ge(s.halves, 2 * (t - 1))
                    sp.dma_start(decay[:, t % 2, :], ins["hy_decay"][P * t:P * t + P, :]).then_inc(s.decay_even if t % 2 == 0 else s.decay_odd, 16)

            @block.tensor
            def _(pe):
                pe.wait_ge(s.loaded, 48)
                for t in range(TT):
                    if t >= 2:
                        pe.wait_ge(s.halves, 2 * (t - 1))
                    for direction in range(2):
                        pe.matmul(ps[:, 2 * (t % 2) + direction, :], hidden[:, P * t:P * t + P], w3[:, direction, :],
                                  start=True, stop=True).then_inc(s.product, 1)

            @block.vector
            def _(dve):
                c = Chain(dve, s.chain)
                for t in range(TT):
                    b = t % 2
                    dve.wait_ge(s.decay_even if b == 0 else s.decay_odd, 16 * (t // 2 + 1))
                    dve.wait_ge(s.product, 2 * t + 2)
                    if t >= 2:
                        dve.wait_ge(s.lo_done, 2 * (t - 1))
                    dve.tensor_tensor(fwd[:, b, :], ps[:, 2 * b, :], decay[:, b, :], ALU.mult).then_inc(s.halves, 1)
                    dve.tensor_tensor(bwd[:, b, :], ps[:, 2 * b + 1, :], decay[:, b, :], ALU.mult).then_inc(s.halves, 1)
                    dve.wait_ge(s.halves, 2 * t + 2)
                    if t == 0:
                        c(dve.memset(bwd[0:1, 0, :], 0.0))
                        c(dve.tensor_tensor(fwd[0:1, 0, :], fwd[0:1, 0, :], bias[:, :], ALU.add))
                        c.wait()
                    dve.tensor_tensor(tmp[:, b, :], fwd[:, b, :], bwd[:, b, :], ALU.add).then_inc(s.combined, 1)
                    dve.wait_ge(s.combined, 2 * t + 1)
                    dve.tensor_tensor(fwd[:, b, :], fwd[:, b, :], bwd[:, b, :], ALU.subtract).then_inc(s.combined, 1)

            @block.scalar
            def _(act):
                for t in range(TT):
                    act.wait_ge(s.combined, 2 * t + 2)
                    act.activation(su_hi[:, t, :], tmp[:, t % 2, :], ACT.Copy).then_inc(s.hi_done, 1)
                    act.activation(di_hi[:, t, :], fwd[:, t % 2, :], ACT.Copy).then_inc(s.hi_done, 1)

            @block.gpsimd
            def _(pool):
                for t in range(TT):
                    pool.wait_ge(s.hi_done, 2 * t + 2)
                    pool.tensor_tensor(su_lo[:, t, :], tmp[:, t % 2, :], su_hi[:, t, :].bitcast(fp32), ALU.subtract).then_inc(s.lo_done, 1)
                    pool.tensor_tensor(di_lo[:, t, :], fwd[:, t % 2, :], di_hi[:, t, :].bitcast(fp32), ALU.subtract).then_inc(s.lo_done, 1)
        s.clear()


def long_conv(core, ins, order, hidden, src, finish):
    nc, ps = core.nc, core.ps
    with ExitStack() as outer:
        f32t = lambda c, n, sh, d=fp32: c.enter_context(nc.sbuf_tensor(f"lc{order}_{n}", sh, d))
        k_re, k_im = f32t(outer, "k_re", [P, 4, HY]), f32t(outer, "k_im", [P, 4, HY])
        k_re0 = f32t(outer, "k_re0", [P, HY])
        with ExitStack() as ctx:
            su_hi, su_lo, di_hi, di_lo = (f32t(ctx, n, [P, 4, HY], fp32r) for n in ("su_hi", "su_lo", "di_hi", "di_lo"))
            filter_stage(core, ins, order, hidden, su_hi, su_lo, di_hi, di_lo)
            forward = lambda a, b: slabs_of(ins["dft"], 512, a, b)
            linear_stage(core, f"kr{order}", forward(0, 512), feature_tiles(0, 1, 512, 4), su_hi, su_lo,
                         dve_tile=store_tile(core, lambda t: k_re[:, t, :]))
            def keep_im(dve, s, t):
                dve.wait_ge(s.tile_done, t + 1)
                dve.tensor_copy(k_im[:, t, :], ps[:, t % 4, :]).then_inc(s.bank_free, 1)
            linear_stage(core, f"ki{order}", forward(512, 1024), feature_tiles(0, 1, 512, 4), di_hi, di_lo, dve_tile=keep_im)

            def keep_last(dve, s, t):
                dve.wait_ge(s.tile_done, 1)
                dve.tensor_copy(k_re0[:, :], k_re[:, 0, :]).then_inc(s.copied, 1)
                dve.memset(k_im[0:1, 0, :], 0.0).then_inc(s.copied, 1)
                dve.wait_ge(s.copied, 2)
                dve.tensor_copy(k_re0[0:1, :], ps[0:1, 0, :]).then_inc(s.bank_free, 1)
            linear_stage(core, f"kn{order}", forward(512, 544),
                         [[(0, slice(0, 32), [(k, k) for k in range(4)], None)]], su_hi, su_lo, dve_tile=keep_last)

        z_re, z_im = f32t(outer, "z_re", [P, 4, HY]), f32t(outer, "z_im", [P, 4, HY])
        with ExitStack() as ctx:
            z_hi, z_lo = (f32t(ctx, n, [P, 4, HY], fp32r) for n in ("z_hi", "z_lo"))
            split_stage(core, f"zs{order}", src, z_hi, z_lo, 4)
            linear_stage(core, f"zr{order}", forward(0, 1024), feature_tiles(0, 2, 512, 4), z_hi, z_lo,
                         dve_tile=store_tile(core, lambda t: (z_re if t < 4 else z_im)[:, t % 4, :]))
        yhi, ylo = f32t(outer, "yhi", [P, 8, HY], fp32r), f32t(outer, "ylo", [P, 8, HY], fp32r)
        s = Sems(nc, f"cm{order}")
        with ExitStack() as ctx:
            a, b, y = (f32t(ctx, n, [P, 2, HY]) for n in ("a", "b", "y"))
            with nc.Block() as block:
                @block.vector
                def _(dve):
                    for n in range(8):
                        f, im = n // 2, n % 2
                        if n >= 2:
                            dve.wait_ge(s.lo_done, n - 1)
                        re = k_re0[:, :] if f == 0 else k_re[:, f, :]
                        if not im:
                            dve.tensor_tensor(a[:, im, :], z_re[:, f, :], k_re[:, f, :], ALU.mult).then_inc(s.terms, 1)
                            dve.tensor_tensor(b[:, im, :], z_im[:, f, :], k_im[:, f, :], ALU.mult).then_inc(s.terms, 1)
                        else:
                            dve.tensor_tensor(a[:, im, :], z_re[:, f, :], k_im[:, f, :], ALU.mult).then_inc(s.terms, 1)
                            dve.tensor_tensor(b[:, im, :], z_im[:, f, :], re, ALU.mult).then_inc(s.terms, 1)
                        dve.wait_ge(s.terms, 2 * n + 2)
                        dve.tensor_tensor(y[:, im, :], a[:, im, :], b[:, im, :], ALU.add if im else ALU.subtract).then_inc(s.y_ready, 1)

                @block.scalar
                def _(act):
                    for n in range(8):
                        act.wait_ge(s.y_ready, n + 1)
                        act.activation(yhi[:, n // 2 + 4 * (n % 2), :], y[:, n % 2, :], ACT.Copy).then_inc(s.hi_done, 1)

                @block.gpsimd
                def _(pool):
                    for n in range(8):
                        k = n // 2 + 4 * (n % 2)
                        pool.wait_ge(s.hi_done, n + 1)
                        pool.tensor_tensor(ylo[:, k, :], y[:, n % 2, :], yhi[:, k, :].bitcast(fp32), ALU.subtract)\
                            .then_inc(s.lo_done, 1)
            s.clear()
        finish(yhi, ylo)


def hyena(core, ins, v_tok, x1_tok, x2f):
    nc, ps = core.nc, core.ps
    with nc.sbuf_tensor("hy_hidden", [64, SEQ], fp32) as hidden:
        filter_basis_stage(core, ins, hidden)

        def first(yhi, ylo):
            def step(dve, s, t):
                dve.wait_ge(s.tile_done, t + 1)
                dve.tensor_tensor(x1_tok[:, t, :], x1_tok[:, t, :], ps[:, t % 4, :], ALU.mult).then_inc(s.bank_free, 1)
            linear_stage(core, "inv0", slabs_of(ins["idft"], 256), feature_tiles(0, 2, 256, 8), yhi, ylo, dve_tile=step)
        long_conv(core, ins, 0, hidden, v_tok, first)

        def second(yhi, ylo):
            def step(dve, s, t):
                j, f = t // 4, t % 4
                cols = slice(256 * j, 256 * j + 256)
                dve.wait_ge(s.tile_done, t + 1)
                dve.tensor_tensor(x2f[:, f, cols], x2f[:, f, cols], ps[:, t % 4, 0:256], ALU.mult).then_inc(s.bank_free, 1)
            linear_stage(core, "inv1", slabs_of(ins["idft"], 256), token_tiles(0, 2, 256, 8), yhi, ylo, dve_tile=step)
        long_conv(core, ins, 1, hidden, x1_tok, second)


def window_bias_stage(core, ins, bias):
    nc, s, ps = core.nc, Sems(core.nc, "wb"), core.ps
    NH, NR, NC = 8, 15, 31
    with ExitStack() as ctx:
        sb = lambda n, sh: ctx.enter_context(nc.sbuf_tensor(f"wb_{n}", sh, fp32))
        rows, cols, anti, mask = sb("rows", [NH * NR, NC]), sb("cols", [NC, NH * NR]), sb("anti", [NC, 127]), sb("mask", [P, 64])
        with nc.Block() as block:
            @block.sync
            def _(sp):
                sp.dma_start(rows[:, :], ins["na_rpb_2"][0].rearrange("h r c -> (h r) c")).then_inc(s.loaded, 16)
                sp.dma_start(anti[:, :], ins["anti_diagonal"]).then_inc(s.loaded, 16)
                sp.dma_start(mask[:, :], ins["column_mask"]).then_inc(s.loaded, 16)

            @block.tensor
            def _(pe):
                pe.wait_ge(s.loaded, 48)
                pe.transpose(ps[0:NC, 7, 0:NH * NR], rows[:, :], core.ident[0:NH * NR, 0:NH * NR]).then_inc(s.turned, 1)
                pe.wait_ge(s.cols_ready, 1)
                for n in range(16):
                    if n >= 4:
                        pe.wait_ge(s.stored, 2 * (n - 3))
                    for q in range(4):
                        x = 63 - (4 * n + q)
                        for half in range(2):
                            mm = pe.matmul(ps[64 * half:64 * half + 64, n % 4, 120 * q:120 * q + 120],
                                           anti[:, x:x + 64], cols[:, :], start=True, stop=True)
                    mm.then_inc(s.picked, 1)

            @block.vector
            def _(dve):
                dve.wait_ge(s.turned, 1)
                dve.tensor_copy(cols[:, :], ps[0:NC, 7, 0:NH * NR]).then_inc(s.cols_ready, 1)
                for n in range(16):
                    dve.wait_ge(s.picked, n + 1)
                    for half in range(2):
                        r = slice(64 * half, 64 * half + 64)
                        out = bias[r, :, half:half + NR, 4 * n:4 * n + 4].rearrange("p h m c -> p c h m")
                        for h0 in (0,):
                            dve.tensor_tensor(out, ps[r, n % 4, 0:480].rearrange("p (c h m) -> p c h m", c=4, h=NH),
                                              mask[r, 4 * n:4 * n + 4].unsqueeze(2).unsqueeze(3).to_broadcast([64, 4, NH, NR]),
                                              ALU.add).then_inc(s.stored, 1)
        s.clear()


def neighbourhood_stage(core, qf, kf, v, bias, yb):
    nc, s, ps = core.nc, Sems(core.nc, "na"), core.ps
    NH = 8
    with ExitStack() as ctx:
        sb = lambda n, sh: ctx.enter_context(nc.sbuf_tensor(f"na_{n}", sh, fp32))
        sc, pr, pt = sb("sc", [P, 2, SEQ]), sb("pr", [P, 2, SEQ]), sb("pt", [P, 2, TT, SEQ])
        neg, tot, inv = sb("neg", [P, 4]), sb("tot", [P, 4]), sb("inv", [P, 4])
        units = [(h, i) for h in range(NH) for i in range(TT)]
        U = len(units)
        with nc.Block() as block:
            @block.tensor
            def _(pe):
                def scores(u):
                    h, i = units[u]
                    t, r = h // 2, HD * (h % 2)
                    if u >= 2:
                        pe.wait_ge(s.biased, u - 1)
                    pe.matmul(ps[:, u % 2, :], qf[r:r + HD, t, P * i:P * i + P], kf[r:r + HD, t, :],
                              start=True, stop=True).then_inc(s.scores_done, 1)

                def turn(u):
                    pe.wait_ge(s.normed, u + 1)
                    if u >= 2:
                        pe.wait_ge(s.copied, u - 1)
                    for j in range(TT):
                        mm = pe.transpose(ps[:, 2 + u % 2, P * j:P * j + P], pr[:, u % 2, P * j:P * j + P], core.ident[:, :])
                    mm.then_inc(s.turned, 1)

                def values(h):
                    t, r = h // 2, HD * (h % 2)
                    pe.wait_ge(s.copied, 4 * h + 4)
                    if h % 2 == 0 and t >= 2:
                        pe.wait_ge(s.out_done, t - 1)
                    for j in range(TT):
                        mm = pe.matmul(ps[r:r + HD, 4 + t % 2, :], v[:, j, HD * h:HD * h + HD], pt[:, h % 2, j, :],
                                       start=(j == 0), stop=(j == TT - 1))
                    mm.then_inc(s.values_done, 1)
                for u in range(U + 3):
                    if u < U:
                        scores(u)
                    if 2 <= u < U + 2:
                        turn(u - 2)
                    if u >= 3 and (u - 3) % 4 == 3:
                        values((u - 3) // 4)

            @block.vector
            def _(dve):
                def out(dve, t):
                    dve.wait_ge(s.values_done, 2 * t + 2)
                    dve.tensor_copy(yb[:, t, :], ps[:, 4 + t % 2, :]).then_inc(s.out_done, 1)

                def soften(u):
                    h, i = units[u]
                    dve.wait_ge(s.scores_done, u + 1)
                    if u >= 2:
                        dve.wait_ge(s.exp_done, u - 1)
                    m0 = 8 - 2 * i
                    dve.tensor_tensor(sc[:, u % 2, :].rearrange("p (m c) -> p m c", m=8),
                                      ps[:, u % 2, :].rearrange("p (m c) -> p m c", m=8),
                                      bias[:, h, m0 - 1:m0 + 7, :], ALU.add).then_inc(s.biased, 1)
                    dve.wait_ge(s.biased, u + 1)
                    dve.tensor_reduce(neg[:, u % 4:u % 4 + 1], sc[:, u % 2, :], AX.X, ALU.max, negate=True).then_inc(s.max_done, 1)

                def normalise(u):
                    dve.wait_ge(s.exp_done, u + 1)
                    dve.reciprocal(inv[:, u % 4:u % 4 + 1], tot[:, u % 4:u % 4 + 1]).then_inc(s.inv_done, 1)
                    dve.wait_ge(s.inv_done, u + 1)
                    dve.tensor_scalar(pr[:, u % 2, :], pr[:, u % 2, :], inv[:, u % 4:u % 4 + 1], None, ALU.mult).then_inc(s.normed, 1)

                for u in range(U + 1):
                    if u < U:
                        soften(u)
                    if u >= 1:
                        normalise(u - 1)
                    if u >= 10 and u % 8 == 2:
                        out(dve, (u - 10) // 8)
                out(dve, NH // 2 - 1)

            @block.scalar
            def _(act):
                def copy(u):
                    h, i = units[u]
                    act.wait_ge(s.turned, u + 1)
                    if h >= 2:
                        act.wait_ge(s.values_done, h - 1)
                    act.activation(pt[:, h % 2, :, P * i:P * i + P], ps[:, 2 + u % 2, :].rearrange("p (j q) -> p j q", j=TT),
                                   ACT.Copy).then_inc(s.copied, 1)
                for u in range(U + 2):
                    if u < U:
                        act.wait_ge(s.max_done, u + 1)
                        if u >= 2:
                            act.wait_ge(s.turned, u - 1)
                        act.activation(pr[:, u % 2, :], sc[:, u % 2, :], ACT.Exp, bias=neg[:, u % 4:u % 4 + 1],
                                       accum_out=tot[:, u % 4:u % 4 + 1]).then_inc(s.exp_done, 1)
                    if u >= 2:
                        copy(u - 2)
        s.clear()


def merge_stages(core, ins, xhi, xlo, parts, merged):
    nc, ps = core.nc, core.ps
    g0 = 3 * HY * 3
    with ExitStack() as ctx:
        sig, prod = (ctx.enter_context(nc.sbuf_tensor(f"mg_{n}", [P, 2, SEQ], fp32)) for n in ("sig", "prod"))
        for b, (yhi, ylo) in enumerate(parts):
            if b == 0:
                add = lambda dve, f, pr: dve.tensor_copy(merged[:, f, :], pr)
            else:
                add = lambda dve, f, pr: dve.tensor_tensor(merged[:, f, :], merged[:, f, :], pr, ALU.add)
            gated_stage(core, f"mg{b}", ins["w_branch_2"][0, b], [(k, k) for k in range(4)], yhi, ylo,
                        ins["w_in_2"][0], g0 + D * b, xhi, xlo, sig, prod,
                        lambda f: core.gain("gate_bias_2", DK * b + f), add)


def branches(core, ins):
    nc = core.nc
    g = lambda n: (lambda k: core.gain("norm_gains_2", DK * n + k))
    w = ins["w_in_2"][0]
    with ExitStack() as ctx:
        sb = lambda c, n, sh, d=fp32: c.enter_context(nc.sbuf_tensor(f"b2_{n}", sh, d))
        ya, yb, yc = (sb(ctx, n, [P, 4, SEQ]) for n in ("ya", "yb", "yc"))
        with ExitStack() as mid:
            x1_tok = sb(mid, "x1_tok", [P, 4, SEQ])
            with ExitStack() as c1:
                xhi, xlo = sb(c1, "xhi", [P, DK, SEQ], fp32r), sb(c1, "xlo", [P, DK, SEQ], fp32r)
                norm_stage(core, "n0", core.h, g(0), xhi, xlo)
                hyena_in(core, ins, xhi, xlo, yb, x1_tok, ya)
                short_conv_in(core, ins, xhi, xlo, yc)
            hyena(core, ins, yb, x1_tok, ya)
        with ExitStack() as mid:
            qf, kf, nv = (sb(mid, n, [P, 4, SEQ]) for n in ("qf", "kf", "nv"))
            with ExitStack() as c1:
                xhi, xlo = sb(c1, "x1hi", [P, DK, SEQ], fp32r), sb(c1, "x1lo", [P, DK, SEQ], fp32r)
                norm_stage(core, "n0a", core.h, g(0), xhi, xlo)

                def qk(dve, s, t):
                    dve.wait_ge(s.tile_done, t + 1)
                    dst, scale = (qf, HD ** -0.5) if t < 4 else (kf, 1.0)
                    dve.tensor_scalar(dst[:, t % 4, :], core.ps[:, t % 4, :], scale, None, ALU.mult).then_inc(s.bank_free, 1)
                linear_stage(core, "naqk", slabs_of(w, 256, 3 * HY, 5 * HY), feature_tiles(0, 4, 256, DK), xhi, xlo, dve_tile=qk)
                linear_stage(core, "nav", slabs_of(w, 256, 5 * HY, 6 * HY), token_tiles(0, 2, 256, DK), xhi, xlo,
                             dve_tile=store_tile(core, lambda t: nv[:, t % TT, 256 * (t // TT):256 * (t // TT) + 256]))
            bias = sb(mid, "bias", [P, 8, 16, 64])
            window_bias_stage(core, ins, bias)
            neighbourhood_stage(core, qf, kf, nv, bias, yb)
        y3 = (ya, yb, yc)
        parts = []
        for b in range(3):
            hi, lo = sb(ctx, f"yh{b}", [P, 4, SEQ], fp32r), sb(ctx, f"yl{b}", [P, 4, SEQ], fp32r)
            split_stage(core, f"ys{b}", y3[b], hi, lo, 4)
            parts.append((hi, lo))
        merged = sb(ctx, "merged", [P, DK, SEQ])
        with ExitStack() as c2:
            xhi, xlo = sb(c2, "x2hi", [P, DK, SEQ], fp32r), sb(c2, "x2lo", [P, DK, SEQ], fp32r)
            norm_stage(core, "n0b", core.h, g(0), xhi, xlo)
            merge_stages(core, ins, xhi, xlo, parts, merged)
            split_stage(core, "mgs", merged, xhi, xlo, DK)
            linear_stage(core, "wout", slabs_of(ins["w_out_2"][0], 256), feature_tiles(0, 4, 256, DK), xhi, xlo,
                         dve_tile=store_tile(core, lambda t: merged[:, t, :]))
        add_normed_stage(core, "n1", merged, g(1))


def memory_attention_stage(core, qf, kf, v, ohi, olo):
    nc, s, ps = core.nc, Sems(core.nc, "xa"), core.ps
    NH, W = 4, 256
    with ExitStack() as ctx:
        sb = lambda n, sh: ctx.enter_context(nc.sbuf_tensor(f"xa_{n}", sh, fp32))
        pr, pt = sb("pr", [P, 2, W]), sb("pt", [P, 2, MT, SEQ])
        neg, tot, inv = sb("neg", [P, 4]), sb("tot", [P, 4]), sb("inv", [P, 4])
        tmp = core.split_buf
        units = [(h, i) for h in range(NH) for i in range(TT)]
        U = len(units)
        with nc.Block() as block:
            @block.tensor
            def _(pe):
                def scores(u):
                    h, i = units[u]
                    if u >= 2:
                        pe.wait_ge(s.exp_done, u - 1)
                    for k in range(2):
                        mm = pe.matmul(ps[:, u % 2, 0:W], qf[:, 2 * h + k, P * i:P * i + P], kf[:, 2 * h + k, :],
                                       start=(k == 0), stop=(k == 1))
                    mm.then_inc(s.scores_done, 1)

                def turn(u):
                    pe.wait_ge(s.normed, u + 1)
                    if u >= 2:
                        pe.wait_ge(s.copied, u - 1)
                    for j in range(MT):
                        mm = pe.transpose(ps[:, 2 + u % 2, P * j:P * j + P], pr[:, u % 2, P * j:P * j + P], core.ident[:, :])
                    mm.then_inc(s.turned, 1)

                def values(h):
                    pe.wait_ge(s.copied, 4 * h + 4)
                    for d in range(2):
                        n = 2 * h + d
                        if n >= 2:
                            pe.wait_ge(s.out_done, n - 1)
                        for j in range(MT):
                            mm = pe.matmul(ps[:, 4 + n % 2, :], v[:, j, P * n:P * n + P], pt[:, h % 2, j, :],
                                           start=(j == 0), stop=(j == MT - 1))
                        mm.then_inc(s.values_done, 1)
                for u in range(U + 3):
                    if u < U:
                        scores(u)
                    if 2 <= u < U + 2:
                        turn(u - 2)
                    if u >= 3 and (u - 3) % 4 == 3:
                        values((u - 3) // 4)

            @block.vector
            def _(dve):
                def out(n):
                    dve.wait_ge(s.values_done, n + 1)
                    if n >= 2:
                        dve.wait_ge(s.lo_done, n - 1)
                    dve.tensor_copy(tmp[n % 2][:, :], ps[:, 4 + n % 2, :]).then_inc(s.out_done, 1)

                for u in range(U + 1):
                    if u < U:
                        dve.wait_ge(s.scores_done, u + 1)
                        dve.tensor_reduce(neg[:, u % 4:u % 4 + 1], ps[:, u % 2, 0:W], AX.X, ALU.max, negate=True)\
                           .then_inc(s.max_done, 1)
                    if u >= 1:
                        w = u - 1
                        dve.wait_ge(s.exp_done, w + 1)
                        dve.reciprocal(inv[:, w % 4:w % 4 + 1], tot[:, w % 4:w % 4 + 1]).then_inc(s.inv_done, 1)
                        dve.wait_ge(s.inv_done, w + 1)
                        dve.tensor_scalar(pr[:, w % 2, :], pr[:, w % 2, :], inv[:, w % 4:w % 4 + 1], None, ALU.mult)\
                           .then_inc(s.normed, 1)
                    if u >= 7 and (u - 7) % 4 == 0:
                        out(2 * ((u - 7) // 4))
                        out(2 * ((u - 7) // 4) + 1)
                for n in range(6, 8):
                    out(n)

            @block.scalar
            def _(act):
                def high(n):
                    act.wait_ge(s.out_done, n + 1)
                    act.activation(ohi[:, n, :], tmp[n % 2][:, :], ACT.Copy).then_inc(s.hi_done, 1)

                def copy(u):
                    h, i = units[u]
                    act.wait_ge(s.turned, u + 1)
                    if h >= 2:
                        act.wait_ge(s.values_done, 2 * (h - 1))
                    act.activation(pt[:, h % 2, :, P * i:P * i + P],
                                   ps[:, 2 + u % 2, 0:W].rearrange("p (j q) -> p j q", j=MT), ACT.Copy).then_inc(s.copied, 1)
                for u in range(U + 2):
                    if u < U:
                        act.wait_ge(s.max_done, u + 1)
                        if u >= 2:
                            act.wait_ge(s.turned, u - 1)
                        act.activation(pr[:, u % 2, :], ps[:, u % 2, 0:W], ACT.Exp, bias=neg[:, u % 4:u % 4 + 1],
                                       accum_out=tot[:, u % 4:u % 4 + 1]).then_inc(s.exp_done, 1)
                    if u >= 2:
                        copy(u - 2)
                    if u >= 7 and (u - 7) % 4 == 0:
                        high(2 * ((u - 7) // 4))
                        high(2 * ((u - 7) // 4) + 1)
                for n in range(6, 8):
                    high(n)

            @block.gpsimd
            def _(pool):
                for n in range(8):
                    pool.wait_ge(s.hi_done, n + 1)
                    pool.tensor_tensor(olo[:, n, :], tmp[n % 2][:, :], ohi[:, n, :].bitcast(fp32), ALU.subtract)\
                        .then_inc(s.lo_done, 1)
        s.clear()


def memory_attention(core, ins):
    nc, ps = core.nc, core.ps
    g = lambda n: (lambda k: core.gain("norm_gains_2", DK * n + k))
    with ExitStack() as ctx:
        sb = lambda n, sh, d=fp32: ctx.enter_context(nc.sbuf_tensor(f"xm_{n}", sh, d))
        qf, kf, v = sb("q", [P, DK, SEQ]), sb("k", [P, DK, N_MEM]), sb("v", [P, MT, D])
        xhi, xlo = sb("xhi", [P, DK, SEQ], fp32r), sb("xlo", [P, DK, SEQ], fp32r)
        with ExitStack() as c1:
            mem = c1.enter_context(nc.sbuf_tensor("xm_mem", [P, MT, D], fp32))
            mt = c1.enter_context(nc.sbuf_tensor("xm_memt", [P, DK, N_MEM], fp32))
            mhi = c1.enter_context(nc.sbuf_tensor("xm_mhi", [P, DK, N_MEM], fp32r))
            mlo = c1.enter_context(nc.sbuf_tensor("xm_mlo", [P, DK, N_MEM], fp32r))
            s = Sems(nc, "mt")
            with nc.Block() as block:
                @block.sync
                def _(sp):
                    sp.dma_start(mem[:, :, :], ins["mem_2"][0].rearrange("(t p) d -> p t d", p=P)).then_inc(s.loaded, 16)

                @block.tensor
                def _(pe):
                    pe.wait_ge(s.loaded, 16)
                    for n in range(4):
                        t, half = n // 2, n % 2
                        for k in range(4):
                            c = P * (4 * half + k)
                            mm = pe.transpose(ps[:, n, P * k:P * k + P], mem[:, t, c:c + P], core.ident[:, :])
                        mm.then_inc(s.turned, 1)

                @block.scalar
                def _(act):
                    for n in range(4):
                        t, half = n // 2, n % 2
                        act.wait_ge(s.turned, n + 1)
                        act.activation(mt[:, 4 * half:4 * half + 4, P * t:P * t + P],
                                       ps[:, n, :].rearrange("p (k c) -> p k c", k=4), ACT.Copy).then_inc(s.stored, 1)
            s.clear()
            norm_stage(core, "memn", mt, lambda k: core.gain("mem_norm_2", k), mhi, mlo, toks=N_MEM)
            wkv = ins["xa_wkv_2"][0]
            linear_stage(core, "xak", slabs_of(wkv, 256, 0, D), feature_tiles(0, 4, 256, DK), mhi, mlo,
                         dve_tile=store_tile(core, lambda t: kf[:, t, :]))
            linear_stage(core, "xav", slabs_of(wkv, 256, D, 2 * D), token_tiles(0, 4, 256, DK, MT), mhi, mlo,
                         dve_tile=store_tile(core, lambda t: v[:, t % MT, 256 * (t // MT):256 * (t // MT) + 256]))
        norm_stage(core, "n2", core.h, g(2), xhi, xlo)

        def scaled_q(dve, s, t):
            dve.wait_ge(s.tile_done, t + 1)
            dve.tensor_scalar(qf[:, t, :], ps[:, t % 4, :], 256 ** -0.5, None, ALU.mult).then_inc(s.bank_free, 1)
        linear_stage(core, "xaq", slabs_of(ins["xa_wq_2"][0], 256), feature_tiles(0, 4, 256, DK), xhi, xlo, dve_tile=scaled_q)
        memory_attention_stage(core, qf, kf, v, xhi, xlo)
        linear_stage(core, "xao", slabs_of(ins["xa_wo_2"][0], 256), feature_tiles(0, 4, 256, DK), xhi, xlo,
                     dve_tile=store_tile(core, lambda t: qf[:, t, :]))
        add_normed_stage(core, "n3", qf, g(3))


def feed_forward(core, ins):
    nc, ps = core.nc, core.ps
    g = lambda n: (lambda k: core.gain("norm_gains_2", DK * n + k))
    with ExitStack() as ctx:
        sb = lambda c, n, sh, d=fp32: c.enter_context(nc.sbuf_tensor(f"ff_{n}", sh, d))
        ahi, alo = sb(ctx, "ahi", [P, FF_TILES, SEQ], fp32r), sb(ctx, "alo", [P, FF_TILES, SEQ], fp32r)
        with ExitStack() as c1:
            xhi, xlo = sb(c1, "xhi", [P, DK, SEQ], fp32r), sb(c1, "xlo", [P, DK, SEQ], fp32r)
            norm_stage(core, "n4", core.h, g(4), xhi, xlo)
            conv, gel = sb(c1, "conv", [P, 2, SEQ]), sb(c1, "gel", [P, SEQ])
            up = ins["ffn_up_2"][0].rearrange("(k p) n -> p k n", p=P)
            slabs, tiles, order = [], [], []
            for j in range(FF_TILES // 2):
                slabs += [up[:, :, 256 * j:256 * j + 256], up[:, :, D_FF + 256 * j:D_FF + 256 * j + 256]]
                for c in range(2):
                    for kind in range(2):
                        tiles.append([(2 * j + kind, slice(P * c, P * c + P), [(k, k) for k in range(DK)], None)])
                        order.append((kind, 2 * j + c))

            def conv_dve(dve, s, t):
                c = Chain(dve, s.chain)
                c.n = 2 * t
                kind, f = order[t]
                dve.wait_ge(s.tile_done, t + 1)
                if t >= 2:
                    if kind == 0:
                        dve.wait_ge(s.gelu_done, f)
                    else:
                        dve.wait_ge(s.lo_done, f)
                centred_conv(dve, c, conv[:, kind, :], ps[:, t % 4, :],
                             [core.gain("ffn_conv_2", 2 * FF_TILES * j + FF_TILES * kind + f) for j in range(3)])\
                    .then_inc(s.bank_free, 1)
                if kind == 1:
                    dve.wait_ge(s.gelu_done, f + 1)
                    dve.wait_ge(s.bank_free, t + 1)
                    dve.tensor_tensor(conv[:, 1, :], conv[:, 1, :], gel[:, :], ALU.mult).then_inc(s.product, 1)

            def gelu_act(act, s, t):
                kind, f = order[t]
                if kind == 0:
                    act.wait_ge(s.bank_free, t + 1)
                    if f >= 1:
                        act.wait_ge(s.product, f)
                    act.activation(gel[:, :], conv[:, 0, :], ACT.Gelu_apprx_tanh).then_inc(s.gelu_done, 1)
                else:
                    act.wait_ge(s.product, f + 1)
                    act.activation(ahi[:, f, :], conv[:, 1, :], ACT.Copy).then_inc(s.hi_done, 1)

            def low_pool(pool, s, t):
                kind, f = order[t]
                if kind == 1:
                    pool.wait_ge(s.hi_done, f + 1)
                    pool.tensor_tensor(alo[:, f, :], conv[:, 1, :], ahi[:, f, :].bitcast(fp32), ALU.subtract).then_inc(s.lo_done, 1)
            linear_stage(core, "up", slabs, tiles, xhi, xlo, act_tile=gelu_act, dve_tile=conv_dve, pool_tile=low_pool)
        y = sb(ctx, "y", [P, DK, SEQ])
        down = ins["ffn_down_2"][0].rearrange("(k p) n -> p k n", p=P)
        half = FF_TILES // 2
        slabs = [down[:, half * q:half * q + half, P * t:P * t + P] for t in range(DK) for q in range(2)]
        tiles = [[(2 * t + q, slice(0, P), [(k, half * q + k) for k in range(half)], None) for q in range(2)]
                 for t in range(DK)]
        linear_stage(core, "down", slabs, tiles, ahi, alo, dve_tile=store_tile(core, lambda t: y[:, t, :]))
        add_normed_stage(core, "n5", y, g(5))


def constants():
    f32 = np.float32
    L, N = SEQ, 2 * SEQ
    t = np.arange(L)[:, None]
    f = np.arange(L)[None, :]
    angle = 2 * np.pi * ((t * f) % N) / N
    nyquist = (-1.0) ** np.arange(L)
    cos, sin = np.cos(angle), -np.sin(angle)
    sin[:, 0] = nyquist
    dft = np.concatenate([cos, sin], axis=1)
    weight = np.full(N, 2.0 / N)
    weight[0] = weight[L] = 1.0 / N
    idft = weight[:, None] * dft.T

    pos = np.linspace(0.0, 1.0, L, dtype=f32)[:, None]
    bands = 16
    w = (f32(2.0 * math.pi) * np.arange(L, dtype=f32)[:, None] / f32(L)).astype(f32)
    fr = np.linspace(1e-4, bands - 1, bands, dtype=f32)[None, :]
    fw = (fr * w).astype(f32)
    emb = np.concatenate([pos, np.cos(fw), -np.sin(fw)], axis=-1)
    deltas = np.abs(np.linspace(math.log(1e-2) / 1.5, math.log(1e-2) / 0.3, HY, dtype=f32))
    decay = np.exp(-pos * deltas)

    c = np.arange(64)
    start = np.clip(c - 8, 0, 48)
    inside = (c[None, :] >= start[:, None]) & (c[None, :] < start[:, None] + 16)
    mask = np.where(inside, 0.0, -1e30)
    anti = (np.arange(31)[:, None] + np.arange(127)[None, :] == 78)
    return {"dft": dft.astype(f32), "idft": idft.astype(f32), "pos_emb": emb.T.astype(f32),
            "hy_decay": decay.astype(f32), "column_mask": np.concatenate([mask, mask]).astype(f32),
            "anti_diagonal": anti.astype(f32)}


def program(nc, ins, out):
    with ExitStack() as ctx:
        core = Core(nc, ctx)
        setup_stage(core, ins)
        mamba(core, ins)
        ple_stages(core, ins, 0)
        stick_breaking(core, ins)
        ple_stages(core, ins, 1)
        branches(core, ins)
        memory_attention(core, ins)
        feed_forward(core, ins)
        output_stage(core, out)


def kernel(**inputs):
    import numpy as _np
    import concourse.bacc as _bacc
    from concourse import mybir as _mybir
    from concourse.bass_utils import run_bass_kernel_spmd as _run

    nc = _bacc.Bacc("TRN2", target_bir_lowering=False, num_devices=1)
    arrays, ins = {}, {}
    for name, a in list(inputs.items()) + list(constants().items()):
        a = _np.ascontiguousarray(a)
        arrays[f"in_{name}"] = a
        ins[name] = nc.dram_tensor(f"in_{name}", a.shape, _mybir.dt.from_np(a.dtype), kind="ExternalInput").ap()
    out = nc.dram_tensor("out", (1, SEQ, D), _mybir.dt.float32, kind="ExternalOutput").ap()
    program(nc, ins, out)
    r = _run(nc, [arrays], core_ids=[0])
    return r.results[0]["out"]
```

```python
import math
from contextlib import ExitStack

import numpy as np
import concourse.bass as bass
from concourse import mybir

fp32 = mybir.dt.float32
fp32r = mybir.dt.float32r
ALU = mybir.AluOpType
ACT = mybir.ActivationFunctionType
AX = mybir.AxisListType

P = 128
SEQ = 512
TT = SEQ // P
D = 1024
DK = D // P
EPS = 1e-6

D_INNER = 2048
HEADS = 32
GROUPS = 4
HG = HEADS // GROUPS
HD = 64
CONV_TILES = 24

N_MEM = 256
MT = N_MEM // P
HY = 512
D_FF = 2816
FF_TILES = D_FF // P

PARAM_ROWS = [
    ("m_conv_w", 4 * CONV_TILES), ("m_conv_b", CONV_TILES), ("m_norm", DK),
    ("m_ynorm", 2 * DK), ("kv_norm", DK), ("s_norm", DK), ("ple_norm", 2 * DK), ("norm_gains_2", 6 * DK),
    ("mem_norm_2", DK), ("gate_bias_2", 3 * DK),
    ("hy_short_w_2", 36), ("sc_conv_w_2", 12), ("ffn_conv_2", 3 * 2 * FF_TILES),
]
PARAM_COL = {}
_col = 0
for _name, _rows in PARAM_ROWS:
    PARAM_COL[_name] = _col
    _col += _rows
PARAM_TOTAL = _col


class Chain:

    def __init__(self, eng, sem):
        self.eng, self.sem, self.n = eng, sem, 0

    def __call__(self, instruction):
        instruction.then_inc(self.sem, 1)
        self.n += 1

    def wait(self):
        self.eng.wait_ge(self.sem, self.n)


class Weights:

    def __init__(self, nc, ctx, schedule):
        self.raw = [ctx.enter_context(nc.sbuf_tensor(f"w_raw{i}", [P, 2048], fp32)) for i in range(2)]
        self.hi = [ctx.enter_context(nc.sbuf_tensor(f"w_hi{i}", [P, 2048], fp32r)) for i in range(2)]
        self.lo = [ctx.enter_context(nc.sbuf_tensor(f"w_lo{i}", [P, 2048], fp32r)) for i in range(2)]
        self.loaded = [nc.alloc_semaphore(f"w_loaded{i}") for i in range(2)]
        self.hi_done = nc.alloc_semaphore("w_hi_done")
        self.lo_done = nc.alloc_semaphore("w_lo_done")
        self.slabs, self.first = [], {}
        for name, slabs in schedule:
            self.first[name] = len(self.slabs)
            self.slabs += slabs

    def size(self, n):
        return self.slabs[n].shape[1] * self.slabs[n].shape[2]

    def load(self, sp, n):
        if n >= len(self.slabs):
            return
        if n >= 2:
            sp.wait_ge(self.lo_done, n - 1)
        sp.dma_start(self.raw[n % 2][:, 0:self.size(n)].rearrange("p (k c) -> p k c", k=self.slabs[n].shape[1]),
                     self.slabs[n]).then_inc(self.loaded[n % 2], 16)

    def split_hi(self, act, n):
        if n >= len(self.slabs):
            return
        act.wait_ge(self.loaded[n % 2], 16 * (n // 2 + 1))
        act.activation(self.hi[n % 2][:, 0:self.size(n)], self.raw[n % 2][:, 0:self.size(n)], ACT.Copy)\
           .then_inc(self.hi_done, 1)

    def split_lo(self, pool, n):
        if n >= len(self.slabs):
            return
        pool.wait_ge(self.hi_done, n + 1)
        pool.tensor_tensor(self.lo[n % 2][:, 0:self.size(n)], self.raw[n % 2][:, 0:self.size(n)],
                           self.hi[n % 2][:, 0:self.size(n)].bitcast(fp32), ALU.subtract).then_inc(self.lo_done, 1)

    def take(self, pe, n):
        pe.wait_ge(self.lo_done, n + 1)
        return [s[n % 2][:, 0:self.size(n)].rearrange("p (k c) -> p k c", k=self.slabs[n].shape[1])
                for s in (self.hi, self.lo)]


def slabs_of(w, cols, c0=0, c1=None):
    v = w.rearrange("(k p) n -> p k n", p=P)
    c1 = w.shape[1] if c1 is None else c1
    return [v[:, :, c:min(c + cols, c1)] for c in range(c0, c1, cols)]


class Core:

    def __init__(self, nc, ctx, schedule):
        self.nc = nc
        Sems.retired.clear()
        sb = lambda n, s, d=fp32: ctx.enter_context(nc.sbuf_tensor(n, s, d))
        self.h = sb("h", [P, DK, SEQ])
        self.params = sb("params", [P, PARAM_TOTAL])
        self.ident = sb("ident", [P, P])
        self.ones = sb("ones", [P, P])
        self.head_ones = sb("head_ones", [P, P])
        self.upto = sb("upto", [P, P])
        self.after = sb("after", [P, P])
        self.minus_from = sb("minus_from", [P, P])
        self.minus_ones = sb("minus_ones", [P, P])
        self.ident_r = sb("ident_r", [P, P], fp32r)
        self.causal_r = sb("causal_r", [P, P], fp32r)
        self.head_gain = sb("head_gain", [P, 2])
        self.ps = ctx.enter_context(nc.psum_tensor("ps", [P, 8, 512], fp32))
        self.w = Weights(nc, ctx, schedule)
        self.out_stored = nc.alloc_semaphore("out_stored")
        self.sq = [sb(f"sq{i}", [P, SEQ]) for i in range(2)]
        self.sq_sum = sb("sq_sum", [P, SEQ])
        self.inv = sb("inv", [P, SEQ])
        self.split_buf = [sb(f"split_buf{i}", [P, SEQ]) for i in range(2)]

    def gain(self, name, k):
        c = PARAM_COL[name] + k
        return self.params[:, c:c + 1]


class Sems:

    retired = []

    def __init__(self, nc, stage):
        self.nc, self.stage, self.made = nc, stage, {}

    def __getattr__(self, name):
        if name not in self.made:
            self.made[name] = self.nc.alloc_semaphore(f"{self.stage}_{name}")
        return self.made[name]

    def clear(self):
        mine = list(self.made.values())
        for sem in mine:
            self.nc.gpsimd.sem_clear(sem)
        for sem in Sems.retired:
            self.nc.release_semaphore(sem)
        Sems.retired[:] = mine


def products(pe, out, whi, wlo, k, cols, xhi, xlo, xk, start, stop):
    pe.matmul(out, whi[:, k, cols], xhi[:, xk, :], start=start, stop=False)
    pe.matmul(out, whi[:, k, cols], xlo[:, xk, :], start=False, stop=False)
    return pe.matmul(out, wlo[:, k, cols], xhi[:, xk, :], start=False, stop=stop)


def token_products(pe, out, whi, wlo, k, cols, xhi, xlo, xk, toks, start, stop):
    pe.matmul(out, xhi[:, xk, toks], whi[:, k, cols], start=start, stop=False)
    pe.matmul(out, xhi[:, xk, toks], wlo[:, k, cols], start=False, stop=False)
    return pe.matmul(out, xlo[:, xk, toks], whi[:, k, cols], start=False, stop=stop)


class Norm:

    def __init__(self, core, src, gains, xhi, xlo, have, kt=DK, toks=SEQ, bank=7):
        self.bank = bank
        self.core, self.src, self.gains, self.xhi, self.xlo = core, src, gains, xhi, xlo
        self.have, self.kt, self.toks = have, kt, toks

    def act_squares(self, act, s):
        core, n = self.core, self.toks
        if self.have == "nothing":
            for k in range(self.kt):
                if k >= 2:
                    act.wait_ge(s.sq_used, k - 1)
                act.activation(core.sq[k % 2][:, 0:n], self.src[:, k, 0:n], ACT.Square).then_inc(s.sq_ready, 1)

    def act_scale(self, act, s):
        core, n = self.core, self.toks
        if self.have != "inverse":
            act.wait_ge(s.mean_ready, 1)
            act.activation(core.sq_sum[:, 0:n], core.inv[:, 0:n], ACT.Sqrt).then_inc(s.root_ready, 1)
        for k in range(self.kt):
            act.wait_ge(s.scaled, k + 1)
            act.activation(self.xhi[:, k, 0:n], core.split_buf[k % 2][:, 0:n], ACT.Copy).then_inc(s.x_hi, 1)

    def pe_sum(self, pe, s):
        core, n, ps = self.core, self.toks, self.core.ps
        if self.have == "nothing":
            for k in range(self.kt):
                pe.wait_ge(s.sq_ready, k + 1)
                pe.matmul(ps[:, self.bank, 0:n], core.ones[:, :], core.sq[k % 2][:, 0:n],
                          start=(k == 0), stop=(k == self.kt - 1)).then_inc(s.sq_used, 1)
        elif self.have == "sum":
            pe.matmul(ps[:, self.bank, 0:n], core.ones[:, :], core.sq_sum[:, 0:n], start=True, stop=True).then_inc(s.sq_used, 1)

    def pe_wait(self, pe, s, k):
        if k % 2 == 0:
            pe.wait_ge(s.x_lo_even, k // 2 + 1)
        else:
            pe.wait_ge(s.x_lo_odd, k // 2 + 1)

    def dve(self, dve, s):
        core, n, tmp = self.core, self.toks, self.core.split_buf
        if self.have != "inverse":
            if self.have != "total":
                dve.wait_ge(s.sq_used, self.kt if self.have == "nothing" else 1)
            dve.tensor_scalar(core.inv[:, 0:n], core.ps[:, self.bank, 0:n], 1.0 / (self.kt * P), EPS, ALU.mult, ALU.add)\
               .then_inc(s.mean_ready, 1)
            dve.wait_ge(s.root_ready, 1)
            dve.reciprocal(core.inv[:, 0:n], core.sq_sum[:, 0:n]).then_inc(s.inv_ready, 1)
            dve.wait_ge(s.inv_ready, 1)

        def low(k):
            dve.wait_ge(s.x_hi, k + 1)
            dve.tensor_tensor(self.xlo[:, k, 0:n], tmp[k % 2][:, 0:n], self.xhi[:, k, 0:n].bitcast(fp32), ALU.subtract)\
               .then_inc(s.x_lo_odd, 1)
        for k in range(self.kt):
            if k >= 2 and k % 2 == 0:
                dve.wait_ge(s.x_lo_even, k // 2)
            if k >= 2 and k % 2 == 1:
                dve.wait_ge(s.x_lo_odd, k // 2)
            dve.scalar_tensor_tensor(out=tmp[k % 2][:, 0:n], in0=self.src[:, k, 0:n], scalar=self.gains(k),
                                     in1=core.inv[:, 0:n], op0=ALU.mult, op1=ALU.mult).then_inc(s.scaled, 1)
            if k % 2 == 1:
                low(k)

    def pool(self, pool, s):
        n, tmp = self.toks, self.core.split_buf
        for k in range(0, self.kt, 2):
            pool.wait_ge(s.x_hi, k + 1)
            pool.tensor_tensor(self.xlo[:, k, 0:n], tmp[0][:, 0:n], self.xhi[:, k, 0:n].bitcast(fp32), ALU.subtract)\
                .then_inc(s.x_lo_even, 1)


class SquareSum:

    def __init__(self, core, tile, wait):
        self.core, self.tile, self.wait = core, tile, wait

    def act(self, act, s, t):
        core = self.core
        self.wait(act, s, t)
        if t >= 3:
            act.wait_ge(s.sq_added, t - 2)
        act.activation((core.sq[t % 2] if t else core.sq_sum)[:, :], self.tile(t), ACT.Square).then_inc(s.sq_made, 1)

    def pool(self, pool, s, t):
        core = self.core
        if t >= 1:
            pool.wait_ge(s.sq_made, t + 1)
            if t >= 2:
                pool.wait_ge(s.sq_added, t - 1)
            pool.tensor_tensor(core.sq_sum[:, :], core.sq_sum[:, :], core.sq[t % 2][:, :], ALU.add).then_inc(s.sq_added, 1)


def add_normed_stage(core, name, y, gains, total=True):
    nc, s, ps = core.nc, Sems(core.nc, name), core.ps
    with ExitStack() as ctx:
        tmp, root = core.split_buf, core.sq_sum
        with nc.Block() as block:
            @block.tensor
            def _(pe):
                pe.matmul(ps[:, 7, :], core.ones[:, :], core.sq_sum[:, :], start=True, stop=True).then_inc(s.total_done, 1)
                pe.wait_ge(s.mean_ready, 1)
                for k in range(DK if total else 0):
                    pe.wait_ge(s.sq_ready, k + 1)
                    pe.matmul(ps[:, 7, :], core.ones[:, :], core.sq[k % 2][:, :],
                              start=(k == 0), stop=(k == DK - 1)).then_inc(s.sq_used, 1)

            @block.scalar
            def _(act):
                act.wait_ge(s.mean_ready, 1)
                act.activation(root[:, :], core.inv[:, :], ACT.Sqrt).then_inc(s.root_ready, 1)
                for k in range(DK if total else 0):
                    if k % 2 == 0:
                        act.wait_ge(s.added_even, k // 2 + 1)
                    else:
                        act.wait_ge(s.added_odd, k // 2 + 1)
                    if k >= 2:
                        act.wait_ge(s.sq_used, k - 1)
                    act.activation(core.sq[k % 2][:, :], core.h[:, k, :], ACT.Square).then_inc(s.sq_ready, 1)

            @block.vector
            def _(dve):
                dve.wait_ge(s.total_done, 1)
                dve.tensor_scalar(core.inv[:, :], ps[:, 7, :], 1.0 / D, EPS, ALU.mult, ALU.add).then_inc(s.mean_ready, 1)
                dve.wait_ge(s.root_ready, 1)
                dve.reciprocal(core.inv[:, :], root[:, :]).then_inc(s.inv_ready, 1)
                dve.wait_ge(s.inv_ready, 1)
                for k in range(DK):
                    if k >= 2:
                        if k % 2 == 0:
                            dve.wait_ge(s.added_even, k // 2)
                        else:
                            dve.wait_ge(s.added_odd, k // 2)
                    dve.scalar_tensor_tensor(out=tmp[k % 2][:, :], in0=y[:, k, :], scalar=gains(k),
                                             in1=core.inv[:, :], op0=ALU.mult, op1=ALU.mult).then_inc(s.scaled, 1)
                    if k % 2 == 1:
                        dve.wait_ge(s.scaled, k + 1)
                        dve.tensor_tensor(core.h[:, k, :], core.h[:, k, :], tmp[1][:, :], ALU.add).then_inc(s.added_odd, 1)

            @block.gpsimd
            def _(pool):
                for k in range(0, DK, 2):
                    pool.wait_ge(s.scaled, k + 1)
                    pool.tensor_tensor(core.h[:, k, :], core.h[:, k, :], tmp[0][:, :], ALU.add).then_inc(s.added_even, 1)
        s.clear()


def linear_stage(core, name, tiles, xhi, xlo, act_tile=None, dve_tile=None, pool_tile=None, pe_after=None,
                 banks=4, bank_need=None, lead=1, norm=None, squares=None):
    nc, s, ps, w = core.nc, Sems(core.nc, name), core.ps, core.w
    base = w.first[name]
    slabs = 1 + max(part[0] for parts in tiles for part in parts)
    first_tile, released, parts_done = {}, {}, 0
    for t, parts in enumerate(tiles):
        for slab, *_ in parts:
            first_tile.setdefault(slab, t)
            if slab == parts[-1][0]:
                released[slab] = ("tile", t + 1)
            else:
                parts_done += 1
                released[slab] = ("part", parts_done)
    with nc.Block() as block:
        @block.sync
        def _(sp):
            for n in range(base + 2, base + slabs + 2):
                w.load(sp, n)

        def split(eng, n):
            if eng is nc.scalar and n >= 2:
                kind, count = released[n - 2]
                eng.wait_ge(s.tile_done if kind == "tile" else s.part_done, count)
            (w.split_hi if eng is nc.scalar else w.split_lo)(eng, base + n)

        @block.scalar
        def _(act):
            if norm:
                norm.act_squares(act, s)
            split(act, 1)
            if norm:
                norm.act_scale(act, s)
            done = 2
            for t in range(len(tiles)):
                while done <= slabs and first_tile[done - 1] <= t:
                    split(act, done)
                    done += 1
                if act_tile:
                    act_tile(act, s, t)
                if squares:
                    squares.act(act, s, t)

        @block.gpsimd
        def _(pool):
            split(pool, 1)
            if norm:
                norm.pool(pool, s)
            done = 2
            for t in range(len(tiles)):
                while done <= slabs and first_tile[done - 1] <= t:
                    split(pool, done)
                    done += 1
                if pool_tile:
                    pool_tile(pool, s, t)
                if squares:
                    squares.pool(pool, s, t)

        @block.vector
        def _(dve):
            if norm:
                norm.dve(dve, s)
            for t in range(len(tiles)):
                if dve_tile:
                    dve_tile(dve, s, t)

        @block.tensor
        def _(pe):
            if norm:
                norm.pe_sum(pe, s)
            waited = set()
            taken = {}
            for t, parts in enumerate(tiles):
                if t >= banks:
                    pe.wait_ge(s.bank_free, bank_need(t) if bank_need else t - banks + 1)
                bank = t % banks
                total = sum(len(part[2]) for part in parts)
                m = 0
                for n, (slab, cols, ks, toks, *own) in enumerate(parts):
                    ahi, alo = own if own else (xhi, xlo)
                    if slab not in taken:
                        taken[slab] = w.take(pe, base + slab)
                    whi, wlo = taken[slab]
                    width = cols.stop - cols.start
                    for k, xk in ks:
                        first, end = m == 0, m == total - 1
                        if norm and ahi is norm.xhi and xk < norm.kt and xk not in waited:
                            waited.add(xk)
                            norm.pe_wait(pe, s, xk)
                        if toks is None:
                            mm = products(pe, ps[0:width, bank, 0:ahi.shape[2]], whi, wlo, k, cols, ahi, alo, xk, first, end)
                        else:
                            mm = token_products(pe, ps[:, bank, 0:width], whi, wlo, k, cols, ahi, alo, xk, toks, first, end)
                        m += 1
                    mm.then_inc(s.tile_done if n == len(parts) - 1 else s.part_done, 1)
                if pe_after and t >= lead:
                    pe_after(pe, s, t - lead)
            if pe_after:
                for t in range(max(0, len(tiles) - lead), len(tiles)):
                    pe_after(pe, s, t)
    s.clear()


def feature_tiles(slab0, n_slabs, cols, kt, width=P):
    return [[(slab0 + j, slice(c, min(c + width, cols)), [(k, k) for k in range(kt)], None)]
            for j in range(n_slabs) for c in range(0, cols, width)]


def token_tiles(slab0, n_slabs, cols, kt, token_tiles_n=TT):
    return [[(slab0 + j, slice(0, cols), [(k, k) for k in range(kt)], slice(P * tt, P * tt + P))]
            for j in range(n_slabs) for tt in range(token_tiles_n)]



def setup_stage(core, ins):
    nc, s, ps = core.nc, Sems(core.nc, "setup"), core.ps
    n_tables = (PARAM_TOTAL + P - 1) // P
    with ExitStack() as ctx:
        rows = ctx.enter_context(nc.sbuf_tensor("setup_rows", [P, n_tables, P], fp32))
        xt = ctx.enter_context(nc.sbuf_tensor("setup_x", [P, TT, D], fp32))

        def stores():
            for name, count in PARAM_ROWS:
                src = ins[name].flatten().rearrange("(r c) -> r c", c=P)
                assert src.shape[0] == count, (name, src.shape)
                done = 0
                while done < count:
                    at = PARAM_COL[name] + done
                    m = min(count - done, P - at % P)
                    yield src[done:done + m, :], at // P, at % P
                    done += m
        parts = list(stores())
        with nc.Block() as block:
            @block.sync
            def _(sp):
                core.w.load(sp, 0)
                core.w.load(sp, 1)
                sp.dma_start(xt[:, :, :], ins["x"][0].rearrange("(t p) d -> p t d", p=P)).then_inc(s.x_loaded, 16)
                for half in range(2):
                    for c, name in enumerate(("k_norm", "q_norm")):
                        sp.dma_start(core.head_gain[HD * half:HD * half + HD, c:c + 1],
                                     ins[name].flatten().rearrange("(p a) -> p a", a=1)).then_inc(s.gains_loaded, 16)

            @block.scalar
            def _(act):
                for src, table, p0 in parts:
                    act.dma_start(rows[p0:p0 + src.shape[0], table, :], src).then_inc(s.rows_loaded, 16)
                core.w.split_hi(act, 0)
                for t in range(TT):
                    for half in range(2):
                        n = 2 * t + half
                        act.wait_ge(s.x_turned, n + 1)
                        act.activation(core.h[:, 4 * half:4 * half + 4, P * t:P * t + P],
                                       ps[:, 1 + n % 4, :].rearrange("p (k c) -> p k c", k=4), ACT.Copy).then_inc(s.x_stored, 1)

            @block.gpsimd
            def _(pool):
                c = Chain(pool, s.pool_chain)
                c(pool.memset(core.ident[:, :], 0.0))
                c(pool.memset(core.head_ones[:, :], 0.0))
                c(pool.memset(core.ones[:, :], 1.0))
                c(pool.memset(core.minus_ones[:, :], -1.0))
                c.wait()
                c(pool.memset(core.head_ones[0:HD, 0:HD], 1.0))
                c.wait()
                c(pool.memset(core.head_ones[HD:P, HD:P], 1.0))
                c.wait()
                pick = lambda out, src, op, fill, sign, base=0: pool.affine_select(
                    out=out[:, :], in_=src[:, :], compare_op=op, fill=fill, base=base,
                    pattern=[[sign, P]], channel_multiplier=-sign)
                c(pick(core.upto, core.ones, ALU.is_ge, 0.0, 1))
                c(pick(core.after, core.ones, ALU.is_gt, 0.0, -1))
                c(pick(core.minus_from, core.minus_ones, ALU.is_ge, 0.0, -1))
                c.wait()
                pick(core.ident, core.ident, ALU.not_equal, 1.0, 1).then_inc(s.ident_ready, 1)
                core.w.split_lo(pool, 0)

            @block.vector
            def _(dve):
                for i in range(n_tables):
                    m = min(P, PARAM_TOTAL - i * P)
                    dve.wait_ge(s.rows_turned, i + 1)
                    dve.tensor_copy(core.params[:, i * P:i * P + m], ps[:, 0, 0:m]).then_inc(s.rows_stored, 1)
                dve.wait_ge(s.ident_ready, 1)
                dve.tensor_copy(core.ident_r[:, :], core.ident[:, :]).then_inc(s.rows_stored, 1)
                dve.tensor_scalar(core.causal_r[:, :], core.minus_from[:, :], 1e30, None, ALU.mult)\
                   .then_inc(s.rows_stored, 1)
                dve.wait_ge(s.gains_loaded, 64)
                dve.tensor_scalar(core.head_gain[:, 1:2], core.head_gain[:, 1:2], HD ** -0.5, None, ALU.mult)\
                   .then_inc(s.rows_stored, 1)

            @block.tensor
            def _(pe):
                pe.wait_ge(s.ident_ready, 1)
                pe.wait_ge(s.x_loaded, 16)
                for t in range(TT):
                    for half in range(2):
                        n = 2 * t + half
                        if n >= 4:
                            pe.wait_ge(s.x_stored, n - 3)
                        for k in range(4):
                            mm = pe.transpose(ps[:, 1 + n % 4, P * k:P * k + P],
                                              xt[:, t, P * (4 * half + k):P * (4 * half + k) + P], core.ident[:, :])
                        mm.then_inc(s.x_turned, 1)
                pe.wait_ge(s.rows_loaded, 16 * len(parts))
                for i in range(n_tables):
                    m = min(P, PARAM_TOTAL - i * P)
                    if i >= 1:
                        pe.wait_ge(s.rows_stored, i)
                    pe.transpose(ps[:, 0, 0:m], rows[0:m, i, :], core.ident[0:m, 0:m]).then_inc(s.rows_turned, 1)
        s.clear()


def output_stage(core, out):
    nc, s, ps = core.nc, Sems(core.nc, "output"), core.ps
    with nc.sbuf_tensor("output_y", [P, TT, D], fp32) as y, nc.Block() as block:
        @block.tensor
        def _(pe):
            for t in range(TT):
                for half in range(2):
                    n = 2 * t + half
                    if n >= 4:
                        pe.wait_ge(s.copied, n - 3)
                    for k in range(4):
                        mm = pe.transpose(ps[:, n % 4, P * k:P * k + P],
                                          core.h[:, 4 * half + k, P * t:P * t + P], core.ident[:, :])
                    mm.then_inc(s.turned, 1)

        @block.vector
        def _(dve):
            for t in range(TT):
                for half in range(2):
                    n = 2 * t + half
                    dve.wait_ge(s.turned, n + 1)
                    dve.tensor_copy(y[:, t, 512 * half:512 * half + 512], ps[:, n % 4, :]).then_inc(s.copied, 1)

        @block.sync
        def _(sp):
            for t in range(TT):
                sp.wait_ge(s.copied, 2 * t + 2)
                sp.dma_start(out[0, P * t:P * t + P, :], y[:, t, :]).then_inc(core.out_stored, 16)
            sp.wait_ge(core.out_stored, 16 * TT)
    s.clear()


def residual_tile(core, banks=4):
    def step(dve, s, t):
        dve.wait_ge(s.tile_done, t + 1)
        dve.tensor_tensor(core.h[:, t, :], core.h[:, t, :], core.ps[:, t % banks, :], ALU.add).then_inc(s.bank_free, 1)
    return step


def residual_squares(core):
    return SquareSum(core, lambda t: core.h[:, t, :], lambda act, s, t: act.wait_ge(s.bank_free, t + 1))


def stored_squares(core, y):
    return SquareSum(core, lambda t: y[:, t, :], lambda act, s, t: act.wait_ge(s.bank_free, t + 1))


def store_tile(core, dst, banks=4):
    def step(dve, s, t):
        dve.wait_ge(s.tile_done, t + 1)
        dve.tensor_copy(dst(t), core.ps[:, t % banks, 0:dst(t).free_size()]).then_inc(s.bank_free, 1)
    return step



def mamba_in_stages(core, ins, z, xs, bc, dt_raw):
    nc, ps, w = core.nc, core.ps, core.w
    with ExitStack() as ctx:
        xhi = ctx.enter_context(nc.sbuf_tensor("mi_xhi", [P, DK, SEQ], fp32r))
        xlo = ctx.enter_context(nc.sbuf_tensor("mi_xlo", [P, DK, SEQ], fp32r))
        norm = Norm(core, core.h, lambda k: core.gain("m_norm", k), xhi, xlo, "nothing")

        def z_act(act, s, t):
            j, tt = t // TT, t % TT
            act.wait_ge(s.tile_done, t + 1)
            act.activation(z[:, tt, 256 * j:256 * j + 256], ps[:, t % 4, 0:256], ACT.Silu).then_inc(s.bank_free, 1)
        linear_stage(core, "mz", token_tiles(0, 8, 256, DK), xhi, xlo, act_tile=z_act, norm=norm)

        def dt_dve(dve, s, t):
            dve.wait_ge(s.tile_done, t + 1)
            dve.tensor_copy(dt_raw[:, HEADS * t:HEADS * t + HEADS], ps[:, t % 4, 0:HEADS]).then_inc(s.bank_free, 1)
        linear_stage(core, "mdt", token_tiles(0, 1, HEADS, DK), xhi, xlo,
                     dve_tile=dt_dve)

        conv = ctx.enter_context(nc.sbuf_tensor("mi_conv", [P, 2, SEQ], fp32))
        act_x = ctx.enter_context(nc.sbuf_tensor("mi_actx", [P, 2, SEQ], fp32))

        def conv_dve(dve, s, t):
            c = Chain(dve, s.conv_chain)
            c.n = 3 * t
            bank, acc = t % 4, conv[:, t % 2, :]
            tap = lambda j: core.gain("m_conv_w", j * CONV_TILES + t)
            dve.wait_ge(s.tile_done, t + 1)
            if t >= 2:
                dve.wait_ge(s.silu_done, t - 1)
            c(dve.tensor_scalar(acc, ps[:, bank, :], tap(3), core.gain("m_conv_b", t), ALU.mult, ALU.add))
            for back in (1, 2, 3):
                c.wait()
                i = dve.scalar_tensor_tensor(out=acc[:, back:SEQ], in0=ps[:, bank, 0:SEQ - back], scalar=tap(3 - back),
                                             in1=acc[:, back:SEQ], op0=ALU.mult, op1=ALU.add)
                if back < 3:
                    c(i)
                else:
                    i.then_inc(s.bank_free, 1)
            if 1 <= t <= 16:
                store_x(dve, s, t - 1)

        def store_x(dve, s, t):
            dve.wait_ge(s.x_turned, t + 1)
            dve.tensor_copy(xs[:, :, P * t:P * t + P], ps[:, 4 + t % 2, :].rearrange("p (c f) -> p c f", c=TT))\
               .then_inc(s.x_stored, 1)

        def silu_act(act, s, t):
            act.wait_ge(s.bank_free, t + 1)
            if t < 16:
                if t >= 2:
                    act.wait_ge(s.x_turned, t - 1)
                act.activation(act_x[:, t % 2, :], conv[:, t % 2, :], ACT.Silu).then_inc(s.silu_done, 1)
            else:
                act.activation(bc[:, t - 16, :], conv[:, t % 2, :], ACT.Silu).then_inc(s.silu_done, 1)

        def turn_pe(pe, s, t):
            if t >= 16:
                return
            pe.wait_ge(s.silu_done, t + 1)
            if t >= 2:
                pe.wait_ge(s.x_stored, t - 1)
            for c in range(TT):
                mm = pe.transpose(ps[:, 4 + t % 2, P * c:P * c + P], act_x[:, t % 2, P * c:P * c + P], core.ident[:, :])
            mm.then_inc(s.x_turned, 1)
        linear_stage(core, "mx", feature_tiles(0, 12, 256, DK),
                     xhi, xlo, act_tile=silu_act, dve_tile=conv_dve, pe_after=turn_pe)


def dt_stage(core, ins, dt_raw, dt, da, e_from_start, e_to_end, e_chunk, d_skip):
    nc, s, ps = core.nc, Sems(core.nc, "dt"), core.ps
    with ExitStack() as ctx:
        sb = lambda n: ctx.enter_context(nc.sbuf_tensor(f"dt_{n}", [P, P], fp32))
        bias, a_log, x, e, u, ln, t1, rest = (sb(n) for n in ("bias", "a_log", "x", "e", "u", "ln", "t1", "rest"))
        chunks = lambda a: a[:, :].rearrange("p (c h) -> p c h", c=TT)
        every = lambda a: a[:, 0:HEADS].unsqueeze(1).to_broadcast([P, TT, HEADS])
        with nc.Block() as block:
            @block.sync
            def _(sp):
                for dst, name in ((bias, "m_dt_bias"), (a_log, "m_A_log"), (d_skip, "m_D")):
                    sp.dma_start(dst[:, 0:HEADS], ins[name][0].partition_broadcast(P)).then_inc(s.loaded, 16)

            @block.vector
            def _(dve):
                c = Chain(dve, s.chain)
                dve.wait_ge(s.loaded, 48)
                c(dve.tensor_tensor(chunks(x), chunks(dt_raw), every(bias), ALU.add))
                c.wait()
                dve.scalar_tensor_tensor(out=t1[:, :], in0=x[:, :], scalar=-1.0, in1=x[:, :], op0=ALU.mult, op1=ALU.min)\
                   .then_inc(s.neg_abs, 1)
                dve.wait_ge(s.exp_done, 1)
                c(dve.tensor_scalar(u[:, :], e[:, :], 1.0, None, ALU.add))
                c.wait()
                c(dve.tensor_scalar(rest[:, :], u[:, :], -1.0, None, ALU.add))
                c.wait()
                c(dve.tensor_tensor(rest[:, :], e[:, :], rest[:, :], ALU.subtract))
                c(dve.reciprocal(t1[:, :], u[:, :]))
                c.wait()
                c(dve.tensor_tensor(rest[:, :], rest[:, :], t1[:, :], ALU.mult))
                c.wait()
                dve.wait_ge(s.ln_done, 1)
                c(dve.tensor_tensor(rest[:, :], rest[:, :], ln[:, :], ALU.add))
                c.wait()
                c(dve.scalar_tensor_tensor(out=dt[:, :], in0=x[:, :], scalar=0.0, in1=rest[:, :],
                                           op0=ALU.max, op1=ALU.add))
                c.wait()
                dve.wait_ge(s.a_done, 1)
                c(dve.tensor_tensor(chunks(da), chunks(dt), every(a_log), ALU.mult))
                c.wait()
                dve.tensor_scalar(da[:, :], da[:, :], -1.0, None, ALU.mult).then_inc(s.da_ready, 1)
                dve.wait_ge(s.sums_done, 2)
                c(dve.tensor_copy(t1[:, :], ps[:, 0, 0:P]))
                c.wait()
                dve.tensor_tensor(rest[:, :], ps[:, 1, 0:P], t1[:, :], ALU.subtract).then_inc(s.to_end, 1)

            @block.scalar
            def _(act):
                act.wait_ge(s.neg_abs, 1)
                act.activation(e[:, :], t1[:, :], ACT.Exp).then_inc(s.exp_done, 1)
                act.activation(a_log[:, 0:HEADS], a_log[:, 0:HEADS], ACT.Exp).then_inc(s.a_done, 1)
                act.wait_ge(s.exp_done, 1)
                act.activation(ln[:, :], e[:, :], ACT.Ln, bias=1.0).then_inc(s.ln_done, 1)
                act.wait_ge(s.to_end, 1)
                act.activation(e_from_start[:, :], ps[:, 0, 0:P], ACT.Exp).then_inc(s.exp_done, 1)
                act.activation(e_chunk[:, :], ps[:, 1, 0:P], ACT.Exp).then_inc(s.exp_done, 1)
                act.activation(e_to_end[:, :], rest[:, :], ACT.Exp).then_inc(s.exp_done, 1)

            @block.tensor
            def _(pe):
                pe.wait_ge(s.da_ready, 1)
                pe.matmul(ps[:, 0, 0:P], core.upto[:, :], da[:, :], start=True, stop=True).then_inc(s.sums_done, 1)
                pe.matmul(ps[:, 1, 0:P], core.ones[:, :], da[:, :], start=True, stop=True).then_inc(s.sums_done, 1)
        s.clear()


def scan_stage(core, z, xs, bc, dt, da, e_from_start, e_to_end, e_chunk, d_skip):
    nc, s, ps = core.nc, Sems(core.nc, "scan"), core.ps
    GW = HG * HD
    with ExitStack() as ctx:
        sb = lambda n, sh: ctx.enter_context(nc.sbuf_tensor(f"scan_{n}", sh, fp32))
        b_tok = sb("b_tok", [P, TT - 1, GROUPS, P])
        state = sb("state", [P, GROUPS, GW])
        steps, decay = sb("steps", [P, HG, P]), sb("decay", [P, HG, P])
        mix = sb("mix", [P, HG, P])
        cb = sb("cb", [P, 2, P])
        xdt, xend, skip, inter, both = (sb(n, [P, GW]) for n in ("xdt", "xend", "skip", "inter", "both"))
        units = [(c, g) for c in range(TT) for g in range(GROUPS)]
        heads = lambda a: a.rearrange("p (h d) -> p h d", h=HG)
        per_head = lambda a, c, g, width=HD: a[:, HEADS * c + HG * g:HEADS * c + HG * g + HG].unsqueeze(2)\
            .to_broadcast([P, HG, width])
        tok = lambda c: slice(P * c, P * c + P)
        grp = lambda g: slice(GW * g, GW * g + GW)

        with nc.Block() as block:
            @block.gpsimd
            def _(pool):
                for u, (c, g) in enumerate(units):
                    if u >= 1:
                        pool.wait_ge(s.sums_done, u)
                    pool.tensor_tensor(steps[:, :, :], core.upto[:, :].unsqueeze(1).to_broadcast([P, HG, P]),
                                       per_head(da, c, g, P), ALU.mult).then_inc(s.steps_ready, 1)
                    if c < TT - 1:
                        pool.wait_ge(s.xdt_ready, u + 1)
                        if u >= 1:
                            pool.wait_ge(s.grown, u)
                        pool.tensor_tensor(heads(xend[:, :]), heads(xdt[:, :]), per_head(e_to_end, c, g), ALU.mult)\
                            .then_inc(s.xend_ready, 1)
                    if u >= 1:
                        pool.wait_ge(s.skip_used, u)
                    pool.tensor_tensor(heads(skip[:, :]), heads(xs[:, c, grp(g)]),
                                       d_skip[:, HG * g:HG * g + HG].unsqueeze(2).to_broadcast([P, HG, HD]), ALU.mult)\
                        .then_inc(s.skip_ready, 1)

            @block.scalar
            def _(act):
                for c in range(TT - 1):
                    act.wait_ge(s.b_turned, c + 1)
                    act.activation(b_tok[:, c, :, :].rearrange("p g n -> p (g n)"), ps[:, 7, :], ACT.Copy)\
                       .then_inc(s.b_stored, 1)
                for u in range(len(units)):
                    act.wait_ge(s.sums_done, u + 1)
                    if u >= 1:
                        act.wait_ge(s.mix_ready, u)
                    act.activation(decay[:, :, :].rearrange("p h l -> p (h l)"),
                                   ps[:, 1:3, :].rearrange("p b l -> p (b l)"), ACT.Exp).then_inc(s.decay_ready, 1)

            @block.vector
            def _(dve):
                c_ = Chain(dve, s.dve_chain)
                for u, (c, g) in enumerate(units):
                    dve.wait_ge(s.cb_done, u + 1)
                    c_(dve.tensor_tensor(cb[:, u % 2, :], ps[:, 0, 0:P], core.upto[:, :], ALU.mult))
                    if u >= 1:
                        dve.wait_ge(s.intra_done, u)
                        if units[u - 1][0] < TT - 1:
                            dve.wait_ge(s.xend_ready, min(u, 4 * (TT - 1)))
                    dve.tensor_tensor(heads(xdt[:, :]), heads(xs[:, c, grp(g)]), per_head(dt, c, g), ALU.mult)\
                       .then_inc(s.xdt_ready, 1)
                    c_.wait()
                    dve.wait_ge(s.decay_ready, u + 1)
                    dve.tensor_tensor(mix[:, :, :], decay[:, :, :], cb[:, u % 2, :].unsqueeze(1).to_broadcast([P, HG, P]),
                                      ALU.mult).then_inc(s.mix_ready, 1)
                    dve.wait_ge(s.skip_ready, u + 1)
                    dve.wait_ge(s.intra_done, u + 1)
                    if c > 0:
                        dve.wait_ge(s.inter_done, u - 3)
                        c_(dve.tensor_tensor(heads(inter[:, :]), heads(ps[:, 4, :]), per_head(e_from_start, c, g), ALU.mult))
                        c_.wait()
                        c_(dve.tensor_tensor(both[:, :], ps[:, 3, :], inter[:, :], ALU.add))
                        c_.wait()
                        dve.tensor_tensor(both[:, :], both[:, :], skip[:, :], ALU.add).then_inc(s.skip_used, 1)
                    else:
                        dve.tensor_tensor(both[:, :], ps[:, 3, :], skip[:, :], ALU.add).then_inc(s.skip_used, 1)
                    dve.wait_ge(s.skip_used, u + 1)
                    dve.tensor_tensor(z[:, c, grp(g)], both[:, :], z[:, c, grp(g)], ALU.mult).then_inc(s.y_ready, 1)
                    if c < TT - 1:
                        dve.wait_ge(s.grown, u + 1)
                        if c == 0:
                            dve.tensor_copy(state[:, g, :], ps[:, 5, :]).then_inc(s.state_ready, 1)
                        else:
                            c_(dve.tensor_tensor(heads(state[:, g, :]), heads(state[:, g, :]),
                                                 per_head(e_chunk, c, g), ALU.mult))
                            c_.wait()
                            dve.tensor_tensor(state[:, g, :], state[:, g, :], ps[:, 5, :], ALU.add)\
                               .then_inc(s.state_ready, 1)

            @block.tensor
            def _(pe):
                for c in range(TT - 1):
                    if c >= 1:
                        pe.wait_ge(s.b_stored, c)
                    for g in range(GROUPS):
                        mm = pe.transpose(ps[:, 7, P * g:P * g + P], bc[:, g, tok(c)], core.ident[:, :])
                    mm.then_inc(s.b_turned, 1)

                def front(u):
                    c, g = units[u]
                    if u >= 1:
                        pe.wait_ge(s.xdt_ready, u)
                    pe.matmul(ps[:, 0, 0:P], bc[:, g, tok(c)], bc[:, GROUPS + g, tok(c)], start=True, stop=True)\
                      .then_inc(s.cb_done, 1)
                    pe.wait_ge(s.steps_ready, u + 1)
                    if u >= 1:
                        pe.wait_ge(s.decay_ready, u)
                    for half in range(2):
                        mm = pe.matmul(ps[:, 1 + half, :], core.after[:, :],
                                       steps[:, 4 * half:4 * half + 4, :].rearrange("p h l -> p (h l)"),
                                       start=True, stop=True)
                    mm.then_inc(s.sums_done, 1)

                front(0)
                for u, (c, g) in enumerate(units):
                    if u + 1 < len(units):
                        front(u + 1)
                    if c > 0:
                        pe.wait_ge(s.state_ready, 4 * (c - 1) + g + 1)
                        if u >= 5:
                            pe.wait_ge(s.y_ready, u)
                        pe.matmul(ps[:, 4, :], bc[:, GROUPS + g, tok(c)], state[:, g, :], start=True, stop=True)\
                          .then_inc(s.inter_done, 1)
                    pe.wait_ge(s.mix_ready, u + 1)
                    if u >= 1:
                        pe.wait_ge(s.y_ready, u)
                    for h in range(HG):
                        mm = pe.matmul(ps[:, 3, HD * h:HD * h + HD], mix[:, h, :], xdt[:, HD * h:HD * h + HD],
                                       start=True, stop=True)
                    mm.then_inc(s.intra_done, 1)
                    if c < TT - 1:
                        pe.wait_ge(s.xend_ready, u + 1)
                        if c == 0 and g == 0:
                            pe.wait_ge(s.b_stored, TT - 1)
                        if u >= 1:
                            pe.wait_ge(s.state_ready, u)
                        pe.matmul(ps[:, 5, :], b_tok[:, c, g, :], xend[:, :], start=True, stop=True).then_inc(s.grown, 1)
        s.clear()


def y_norm_stage(core, y, yhi, ylo):
    nc, s, ps = core.nc, Sems(core.nc, "ynorm"), core.ps
    GW = HG * HD
    FT = D_INNER // P
    with ExitStack() as ctx:
        sb = lambda n, sh: ctx.enter_context(nc.sbuf_tensor(f"ynorm_{n}", sh, fp32))
        junk, total = sb("junk", [P, 2, GW]), sb("total", [P, TT * GROUPS])
        root, inv = sb("root", [P, TT * GROUPS]), sb("inv", [P, TT * GROUPS])
        tmp = core.split_buf
        with nc.Block() as block:
            @block.scalar
            def _(act):
                for g in range(GROUPS):
                    for c in range(TT):
                        n = g * TT + c
                        if n >= 2:
                            act.wait_ge(s.squared, n - 1)
                        act.activation(junk[:, n % 2, :], y[:, c, GW * g:GW * g + GW], ACT.Square,
                                       accum_out=total[:, n:n + 1]).then_inc(s.squared, 1)
                act.wait_ge(s.mean_ready, 1)
                act.activation(root[:, :], total[:, :], ACT.Sqrt).then_inc(s.root_ready, 1)
                for f in range(FT):
                    act.wait_ge(s.gained, f + 1)
                    act.activation(yhi[:, f, :], tmp[f % 2][:, :], ACT.Copy).then_inc(s.hi_done, 1)

            @block.vector
            def _(dve):
                dve.wait_ge(s.squared, TT * GROUPS)
                dve.tensor_scalar(total[:, :], total[:, :], 1.0 / GW, EPS, ALU.mult, ALU.add).then_inc(s.mean_ready, 1)
                dve.wait_ge(s.root_ready, 1)
                dve.reciprocal(inv[:, :], root[:, :]).then_inc(s.inv_ready, 1)
                dve.wait_ge(s.inv_ready, 1)
                for g in range(GROUPS):
                    for c in range(TT):
                        n = g * TT + c
                        dve.tensor_scalar(y[:, c, GW * g:GW * g + GW], y[:, c, GW * g:GW * g + GW],
                                          inv[:, n:n + 1], None, ALU.mult).then_inc(s.scaled, 1)
                for f in range(FT):
                    dve.wait_ge(s.turned, f + 1)
                    if f >= 2:
                        dve.wait_ge(s.lo_done, f - 1)
                    dve.tensor_scalar(tmp[f % 2][:, :], ps[:, f % 4, :], core.gain("m_ynorm", f), None, ALU.mult)\
                       .then_inc(s.gained, 1)

            @block.gpsimd
            def _(pool):
                for f in range(FT):
                    pool.wait_ge(s.hi_done, f + 1)
                    pool.tensor_tensor(ylo[:, f, :], tmp[f % 2][:, :], yhi[:, f, :].bitcast(fp32), ALU.subtract)\
                        .then_inc(s.lo_done, 1)

            @block.tensor
            def _(pe):
                for f in range(FT):
                    pe.wait_ge(s.scaled, TT * (f // 4 + 1))
                    if f >= 4:
                        pe.wait_ge(s.gained, f - 3)
                    for c in range(TT):
                        mm = pe.transpose(ps[:, f % 4, P * c:P * c + P], y[:, c, P * f:P * f + P], core.ident[:, :])
                    mm.then_inc(s.turned, 1)
        s.clear()


def mamba(core, ins):
    nc = core.nc
    with ExitStack() as ctx:
        z = ctx.enter_context(nc.sbuf_tensor("mamba_z", [P, TT, D_INNER], fp32))
        with ExitStack() as inner:
            sb = lambda n, sh: inner.enter_context(nc.sbuf_tensor(f"mamba_{n}", sh, fp32))
            xs = sb("xs", [P, TT, D_INNER])
            bc = sb("bc", [P, 2 * GROUPS, SEQ])
            dt_raw, dt, da, e1, e2, e3 = (sb(n, [P, P]) for n in ("dt_raw", "dt", "da", "e_start", "e_end", "e_chunk"))
            d_skip = sb("d_skip", [P, HEADS])
            mamba_in_stages(core, ins, z, xs, bc, dt_raw)
            dt_stage(core, ins, dt_raw, dt, da, e1, e2, e3, d_skip)
            scan_stage(core, z, xs, bc, dt, da, e1, e2, e3, d_skip)
        yhi = ctx.enter_context(nc.sbuf_tensor("mamba_yhi", [P, 16, SEQ], fp32r))
        ylo = ctx.enter_context(nc.sbuf_tensor("mamba_ylo", [P, 16, SEQ], fp32r))
        y_norm_stage(core, z, yhi, ylo)
        linear_stage(core, "mout", feature_tiles(0, DK, P, 16), yhi, ylo,
                     dve_tile=residual_tile(core), squares=residual_squares(core))



def ple_stages(core, ins, i):
    nc, ps = core.nc, core.ps
    with ExitStack() as ctx:
        sb = lambda n, sh, d=fp32: ctx.enter_context(nc.sbuf_tensor(f"ple{i}_{n}", sh, d))
        xhi, xlo = sb("xhi", [P, DK + 2, SEQ], fp32r), sb("xlo", [P, DK + 2, SEQ], fp32r)
        p_tok, sig, prod = sb("p", [P, TT, 2 * P]), sb("sig", [P, 2, SEQ]), sb("prod", [P, 2, SEQ])
        s = Sems(nc, f"ple{i}_p")
        with nc.Block() as block:
            @block.sync
            def _(sp):
                sp.dma_start(p_tok[:, :, :], ins["p"][i, 0].rearrange("(t p) d -> p t d", p=P)).then_inc(s.loaded, 16)

            @block.tensor
            def _(pe):
                pe.wait_ge(s.loaded, 16)
                for k in range(2):
                    for t in range(TT):
                        mm = pe.transpose(ps[:, k, P * t:P * t + P], p_tok[:, t, P * k:P * k + P], core.ident[:, :])
                    mm.then_inc(s.turned, 1)

            @block.scalar
            def _(act):
                for k in range(2):
                    act.wait_ge(s.turned, k + 1)
                    act.activation(core.split_buf[k][:, :], ps[:, k, :], ACT.Copy).then_inc(s.copied, 1)
                    act.wait_ge(s.copied, k + 1)
                    act.activation(xhi[:, DK + k, :], core.split_buf[k][:, :], ACT.Copy).then_inc(s.hi_done, 1)

            @block.gpsimd
            def _(pool):
                for k in range(2):
                    pool.wait_ge(s.hi_done, k + 1)
                    pool.tensor_tensor(xlo[:, DK + k, :], core.split_buf[k][:, :], xhi[:, DK + k, :].bitcast(fp32),
                                       ALU.subtract).then_inc(s.lo_done, 1)
        s.clear()
        norm = Norm(core, core.h, lambda k: core.gain("ple_norm", i * DK + k), xhi, xlo, "sum")

        add = lambda dve, f, prod: dve.tensor_tensor(core.h[:, f, :], core.h[:, f, :], prod, ALU.add)
        squares = SquareSum(core, lambda f: core.h[:, f, :], lambda act, s, f: act.wait_ge(s.added, f + 1))
        gated_stage(core, f"ple{i}", [(0, DK), (1, DK + 1)], xhi, xlo, xhi, xlo, sig, prod, None, add, norm, squares)


def gated_slabs(w_proj, w_gate, g0):
    return [a for c in (0, 512) for a in slabs_of(w_proj, 512, c, c + 512) + slabs_of(w_gate, 256, g0 + c, g0 + c + 512)]


def gated_stage(core, name, proj_ks, phi, plo, xhi, xlo, sig, prod, gate_bias, finish, norm=None, squares=None):
    ps = core.ps
    tiles, order = [], []
    for half in range(2):
        for n in range(4):
            order.append(("proj", 4 * half + n))
            tiles.append([(3 * half, slice(P * n, P * n + P), proj_ks, None, phi, plo)])
        for n in range(4):
            order.append(("gate", 4 * half + n))
            tiles.append([(3 * half + 1 + n // 2, slice(P * (n % 2), P * (n % 2) + P), [(k, k) for k in range(DK)], None)])

    def sig_act(act, s, t):
        kind, f = order[t]
        if kind == "gate":
            act.wait_ge(s.tile_done, t + 1)
            if f >= 2:
                act.wait_ge(s.bank_free, f - 1)
            act.activation(sig[:, f % 2, :], ps[:, t % 8, :], ACT.Sigmoid,
                           bias=gate_bias(f) if gate_bias else 0.0).then_inc(s.sig_done, 1)
            if squares and f >= 1:
                squares.act(act, s, f - 1)
            if squares and f == DK - 1:
                squares.act(act, s, f)

    def sq_pool(pool, s, t):
        kind, f = order[t]
        if squares and kind == "gate" and f >= 1:
            squares.pool(pool, s, f - 1)
        if squares and kind == "gate" and f == DK - 1:
            squares.pool(pool, s, f)

    def add_dve(dve, s, t):
        kind, f = order[t]
        if kind == "proj":
            return
        dve.wait_ge(s.sig_done, f + 1)
        if f >= 2:
            dve.wait_ge(s.added, f - 1)
        dve.tensor_tensor(prod[:, f % 2, :], ps[:, (t - 4) % 8, :], sig[:, f % 2, :], ALU.mult).then_inc(s.bank_free, 1)
        dve.wait_ge(s.bank_free, f + 1)
        finish(dve, f, prod[:, f % 2, :]).then_inc(s.added, 1)
    linear_stage(core, name, tiles, xhi, xlo, act_tile=sig_act, dve_tile=add_dve, pool_tile=sq_pool, banks=8, norm=norm,
                 bank_need=lambda t: t % 4 + 1)



def head_norm_steps(core, name, dst, gain_col, sq, root, inv, banks=4):
    ps = core.ps

    def act_step(act, s, t):
        act.wait_ge(s.tile_done, t + 1)
        if t >= 2:
            act.wait_ge(s.sq_summed, t - 1)
        act.activation(sq[:, t % 2, :], ps[:, t % banks, :], ACT.Square).then_inc(s.head_sq_ready, 1)
        if t >= 1:
            act_root(act, s, t - 1)

    def act_root(act, s, t):
        act.wait_ge(s.head_mean_ready, t + 1)
        act.activation(root[:, t % 2, :], inv[:, t % 2, :], ACT.Sqrt).then_inc(s.head_root_ready, 1)

    def pe_sum(pe, s, t):
        pe.wait_ge(s.head_sq_ready, t + 1)
        if t >= 2:
            pe.wait_ge(s.head_mean_ready, t - 1)
        pe.matmul(ps[:, 4 + t % 2, :], core.head_ones[:, :], sq[:, t % 2, :], start=True, stop=True)\
          .then_inc(s.sq_summed, 1)

    def dve_step(dve, s, t):
        if t >= 1:
            dve_finish(dve, s, t - 1)

    def dve_mean(dve, s, t):
        dve.wait_ge(s.sq_summed, t + 1)
        if t >= 2:
            dve.wait_ge(s.bank_free, t - 1)
        dve.tensor_scalar(inv[:, t % 2, :], ps[:, 4 + t % 2, :], 1.0 / HD, EPS, ALU.mult, ALU.add).then_inc(s.head_mean_ready, 1)

    def dve_finish(dve, s, t):
        dve_mean(dve, s, t)
        dve.wait_ge(s.head_root_ready, t + 1)
        dve.reciprocal(inv[:, t % 2, :], root[:, t % 2, :]).then_inc(s.head_inv_ready, 1)
        dve.wait_ge(s.head_inv_ready, t + 1)
        dve.scalar_tensor_tensor(out=dst[:, t, :], in0=ps[:, t % banks, :], scalar=core.head_gain[:, gain_col:gain_col + 1],
                                 in1=inv[:, t % 2, :], op0=ALU.mult, op1=ALU.mult).then_inc(s.bank_free, 1)
    return act_step, act_root, pe_sum, dve_step, dve_finish


def head_norm_linear(core, name, dst, gain_col, xhi, xlo, norm):
    nc = core.nc
    with ExitStack() as ctx:
        sb = lambda n: ctx.enter_context(nc.sbuf_tensor(f"{name}_{n}", [P, 2, SEQ], fp32))
        sq, root, inv = sb("sq"), sb("root"), sb("inv")
        a, a_root, pe_sum, d, d_fin = head_norm_steps(core, name, dst, gain_col, sq, root, inv)

        def act_tile(act, s, t):
            a(act, s, t)
            if t == DK - 1:
                a_root(act, s, t)

        def dve_tile(dve, s, t):
            d(dve, s, t)
            if t == DK - 1:
                d_fin(dve, s, t)
        linear_stage(core, name, feature_tiles(0, 4, 256, DK), xhi, xlo, norm=norm,
                     act_tile=act_tile, dve_tile=dve_tile, pe_after=pe_sum)


SB_OFF = [0, 512, 896 + 128, 896]
SB_W = [SEQ - P * i for i in range(TT)]
SB_ALL = sum(SB_W)


def stick_attention_stage(core, qf, kf, v, gate, ohi, olo):
    nc, s, ps = core.nc, Sems(core.nc, "stick"), core.ps
    HN = D // HD
    with ExitStack() as ctx:
        sb = lambda n, sh: ctx.enter_context(nc.sbuf_tensor(f"stick_{n}", sh, fp32))
        ex = sb("ex", [P, SB_ALL])
        sp_, wt = sb("sp", [P, 2, SB_ALL]), sb("wt", [P, 2, SB_ALL])
        tmp = core.split_buf
        banks = lambda h: ps[:, 3 * (h % 2):3 * (h % 2) + 3, :].rearrange("p b n -> p (b n)")[:, 0:SB_ALL]
        part = lambda a, i, lo=0, n=None: a[:, SB_OFF[i] + lo:SB_OFF[i] + lo + (SB_W[i] - lo if n is None else n)]

        with nc.Block() as block:
            @block.tensor
            def _(pe):
                def scores(h):
                    t, r = h // 2, HD * (h % 2)
                    if h >= 2:
                        pe.wait_ge(s.weights_out, h - 1)
                    for i in (0, 1, 3, 2):
                        mm = pe.matmul(part(banks(h), i), kf[r:r + HD, t, P * i:P * i + P],
                                       qf[r:r + HD, t, P * i:SEQ], start=(i != 3), stop=False, skip_group_check=True)
                        mm = pe.matmul(part(banks(h), i, 0, P), core.ident_r[:, :], core.causal_r[:, :],
                                       start=False, stop=False, skip_group_check=True)
                    mm.then_inc(s.scores_done, 1)

                def suffix(h):
                    pe.wait_ge(s.sp_made, h + 1)
                    a = sp_[:, h % 2, :]
                    for i in range(TT):
                        mm = pe.matmul(part(banks(h), i), core.minus_from[:, :], part(a, i), start=False,
                                       stop=(i == TT - 1), skip_group_check=True)
                        for j in range(i + 1, TT):
                            mm = pe.matmul(part(banks(h), i, P * (j - i)), core.minus_ones[:, :], part(a, j),
                                           start=False, stop=(j == TT - 1), skip_group_check=True)
                    mm.then_inc(s.logs_done, 1)

                def values(h):
                    t, r = h // 2, HD * (h % 2)
                    pe.wait_ge(s.weights_out, h + 1)
                    if h % 2 == 0 and t >= 2:
                        pe.wait_ge(s.out_used, t - 1)
                    for i in range(TT):
                        mm = pe.matmul(ps[r:r + HD, 6 + t % 2, P * i:SEQ], v[:, i, HD * h:HD * h + HD],
                                       part(wt[:, h % 2, :], i), start=(i == 0), stop=(i == TT - 1),
                                       skip_group_check=True)
                    mm.then_inc(s.values_done, 1)

                for h in range(HN + 2):
                    if h < HN:
                        scores(h)
                    if 1 <= h <= HN:
                        suffix(h - 1)
                    if h >= 2:
                        values(h - 2)

            @block.scalar
            def _(act):
                def high(act, t):
                    act.wait_ge(s.out_used, t + 1)
                    act.activation(ohi[:, t, :], tmp[t % 2][:, :], ACT.Copy).then_inc(s.hi_done, 1)

                def first(h):
                    act.wait_ge(s.scores_done, h + 1)
                    if h >= 1:
                        act.wait_ge(s.sp_made, h)
                    act.activation(ex[:, :], banks(h), ACT.Abs).then_inc(s.mag_done, 1)
                    act.wait_ge(s.mag_done, h + 1)
                    act.activation(ex[:, :], ex[:, :], ACT.Exp, scale=-1.0).then_inc(s.exp_done, 1)
                    act.wait_ge(s.exp_done, h + 1)
                    act.activation(ex[:, :], ex[:, :], ACT.Ln, bias=1.0).then_inc(s.ln_done, 1)

                def second(h):
                    act.wait_ge(s.logs_done, h + 1)
                    if h >= 2:
                        act.wait_ge(s.values_done, h - 1)
                    act.activation(wt[:, h % 2, :], banks(h), ACT.Exp).then_inc(s.weights_out, 1)

                for h in range(HN + 1):
                    if h < HN:
                        first(h)
                    if h >= 1:
                        second(h - 1)
                    if h >= 4 and h % 2 == 0:
                        high(act, h // 2 - 2)
                high(act, HN // 2 - 1)

            @block.vector
            def _(dve):
                def gated(t):
                    dve.wait_ge(s.values_done, 2 * t + 2)
                    if t >= 2:
                        dve.wait_ge(s.lo_done, t - 1)
                    dve.tensor_tensor(tmp[t % 2][:, :], gate[:, t, :], ps[:, 6 + t % 2, :], ALU.mult).then_inc(s.out_used, 1)

                for h in range(HN):
                    dve.wait_ge(s.ln_done, h + 1)
                    if h >= 2:
                        dve.wait_ge(s.logs_done, h - 1)
                    dve.scalar_tensor_tensor(out=sp_[:, h % 2, :], in0=banks(h), scalar=0.0, in1=ex[:, :],
                                             op0=ALU.max, op1=ALU.add).then_inc(s.sp_made, 1)
                    if h >= 3 and h % 2 == 1:
                        gated((h - 3) // 2)
                gated(HN // 2 - 1)

            @block.gpsimd
            def _(pool):
                def low(t):
                    pool.wait_ge(s.hi_done, t + 1)
                    pool.tensor_tensor(olo[:, t, :], tmp[t % 2][:, :], ohi[:, t, :].bitcast(fp32), ALU.subtract)\
                        .then_inc(s.lo_done, 1)
                for t in range(HN // 2 - 1):
                    low(t)
                low(HN // 2 - 1)
        s.clear()


def stick_breaking(core, ins):
    nc, ps = core.nc, core.ps
    with ExitStack() as ctx:
        sb = lambda n, sh, d=fp32: ctx.enter_context(nc.sbuf_tensor(f"sb_{n}", sh, d))
        kf, qf, v, gate = (sb(n, [P, DK, SEQ]) for n in ("k", "q", "v", "gate"))
        v = v[:, :, :].rearrange("p a b -> p (a b)").rearrange("p (t n) -> p t n", t=TT)
        xhi, xlo = sb("xhi", [P, DK, SEQ], fp32r), sb("xlo", [P, DK, SEQ], fp32r)
        head_norm_linear(core, "sbk", kf, 0, xhi, xlo,
                         Norm(core, core.h, lambda k: core.gain("kv_norm", k), xhi, xlo, "sum"))
        linear_stage(core, "sbv", token_tiles(0, 4, 256, DK), xhi, xlo,
                     dve_tile=store_tile(core, lambda t: v[:, t % TT, 256 * (t // TT):256 * (t // TT) + 256]))
        head_norm_linear(core, "sbq", qf, 1, xhi, xlo,
                         Norm(core, core.h, lambda k: core.gain("s_norm", k), xhi, xlo, "inverse"))

        def silu_act(act, s, t):
            act.wait_ge(s.tile_done, t + 1)
            act.activation(gate[:, t, :], ps[:, t % 4, :], ACT.Silu).then_inc(s.bank_free, 1)
        linear_stage(core, "sbg", feature_tiles(0, 4, 256, DK), xhi, xlo,
                     act_tile=silu_act)
        stick_attention_stage(core, qf, kf, v, gate, xhi, xlo)
        linear_stage(core, "sbo", feature_tiles(0, 4, 256, DK), xhi, xlo,
                     dve_tile=residual_tile(core), squares=residual_squares(core))



def split_stage(core, name, src, hi, lo, tiles):
    nc, s = core.nc, Sems(core.nc, name)
    with nc.Block() as block:
        @block.scalar
        def _(act):
            for k in range(tiles):
                act.activation(hi[:, k, :], src[:, k, :], ACT.Copy).then_inc(s.hi_done, 1)

        @block.gpsimd
        def _(pool):
            for k in range(0, tiles, 2):
                pool.wait_ge(s.hi_done, k + 1)
                pool.tensor_tensor(lo[:, k, :], src[:, k, :], hi[:, k, :].bitcast(fp32), ALU.subtract).then_inc(s.lo_done, 1)

        @block.vector
        def _(dve):
            for k in range(1, tiles, 2):
                dve.wait_ge(s.hi_done, k + 1)
                dve.tensor_tensor(lo[:, k, :], src[:, k, :], hi[:, k, :].bitcast(fp32), ALU.subtract).then_inc(s.lo_done, 1)
    s.clear()


def centred_conv(dve, c, acc, x, taps, bias=None):
    c(dve.tensor_scalar(acc, x, taps[1], None, ALU.mult))
    c.wait()
    c(dve.scalar_tensor_tensor(out=acc[:, 1:SEQ], in0=x[:, 0:SEQ - 1], scalar=taps[0], in1=acc[:, 1:SEQ],
                               op0=ALU.mult, op1=ALU.add))
    c.wait()
    return dve.scalar_tensor_tensor(out=acc[:, 0:SEQ - 1], in0=x[:, 1:SEQ], scalar=taps[2], in1=acc[:, 0:SEQ - 1],
                                    op0=ALU.mult, op1=ALU.add)


def hyena_in(core, xhi, xlo, v_tok, x1_tok, x2f, norm):
    nc, ps = core.nc, core.ps
    with ExitStack() as ctx:
        conv = ctx.enter_context(nc.sbuf_tensor("hyin_conv", [P, 2, SEQ], fp32))

        def conv_dve(dve, s, t):
            c = Chain(dve, s.conv_chain)
            c.n = 2 * t
            acc = conv[:, t % 2, :] if t < 8 else x2f[:, t - 8, :]
            dve.wait_ge(s.tile_done, t + 1)
            if 2 <= t < 8:
                dve.wait_ge(s.turned, t - 1)
            centred_conv(dve, c, acc, ps[:, t % 4, :],
                         [core.gain("hy_short_w_2", 12 * j + t) for j in range(3)]).then_inc(s.bank_free, 1)

        def turn_pe(pe, s, t):
            if t >= 8:
                return
            pe.wait_ge(s.bank_free, t + 1)
            if t >= 2:
                pe.wait_ge(s.stored, t - 1)
            for c in range(TT):
                mm = pe.transpose(ps[:, 4 + t % 2, P * c:P * c + P], conv[:, t % 2, P * c:P * c + P], core.ident[:, :])
            mm.then_inc(s.turned, 1)

        def store_act(act, s, t):
            if 1 <= t <= 8:
                u = t - 1
                dst = (v_tok if u < 4 else x1_tok)[:, :, P * (u % 4):P * (u % 4) + P]
                act.wait_ge(s.turned, u + 1)
                act.activation(dst, ps[:, 4 + u % 2, :].rearrange("p (c f) -> p c f", c=TT), ACT.Copy).then_inc(s.stored, 1)
        linear_stage(core, "hyin", feature_tiles(0, 6, 256, DK), xhi, xlo, norm=norm,
                     act_tile=store_act, dve_tile=conv_dve, pe_after=turn_pe)


def short_conv_in(core, xhi, xlo, yc):
    nc, ps = core.nc, core.ps
    with ExitStack() as ctx:
        sb = lambda n: ctx.enter_context(nc.sbuf_tensor(f"scin_{n}", [P, 4, SEQ], fp32))
        cg, cx = sb("c"), sb("cx")

        def step(dve, s, t):
            c = Chain(dve, s.chain)
            f = t % 4
            dve.wait_ge(s.tile_done, t + 1)
            if t < 4:
                dve.tensor_copy(cg[:, f, :], ps[:, t % 4, :]).then_inc(s.bank_free, 1)
            elif t < 8:
                dve.wait_ge(s.bank_free, f + 1)
                dve.tensor_tensor(cx[:, f, :], cg[:, f, :], ps[:, t % 4, :], ALU.mult).then_inc(s.bank_free, 1)
            else:
                c.n = 3 * f
                dve.wait_ge(s.bank_free, 4 + f + 1)
                c(centred_conv(dve, c, cg[:, f, :], cx[:, f, :], [core.gain("sc_conv_w_2", 4 * j + f) for j in range(3)]))
                c.wait()
                dve.tensor_tensor(yc[:, f, :], cg[:, f, :], ps[:, t % 4, :], ALU.mult).then_inc(s.bank_free, 1)
        linear_stage(core, "scin", feature_tiles(0, 6, 256, DK), xhi, xlo, dve_tile=step)


def filter_basis_stage(core, ins, hidden):
    nc, s, ps = core.nc, Sems(core.nc, "filt"), core.ps
    H, E = 64, 33
    two_pi = 2 * math.pi
    c1 = 6.28125
    c2 = float(np.float32(two_pi - c1))
    c3 = float(np.float32(two_pi - c1 - c2))
    magic = 1.5 * 2.0 ** 23
    pi = float(np.nextafter(np.float32(math.pi), np.float32(0)))
    with ExitStack() as ctx:
        sb = lambda n, sh: ctx.enter_context(nc.sbuf_tensor(f"filt_{n}", sh, fp32))
        w1, w2, emb = sb("w1", [E, H]), sb("w2", [H, H]), sb("emb", [E, SEQ])
        cols = sb("cols", [H, 4])
        arg, turns, first = sb("arg", [H, SEQ]), sb("turns", [H, SEQ]), sb("first", [H, SEQ])
        with nc.Block() as block:
            @block.sync
            def _(sp):
                col = lambda a: a.rearrange("(p a) -> p a", a=1)
                for dst, src in ((w1[:, :], ins["hy_w1_2"][0]), (w2[:, :], ins["hy_w2_2"][0]), (emb[:, :], ins["pos_emb"]),
                                 (cols[:, 0:1], col(ins["hy_b1_2"][0])), (cols[:, 1:2], col(ins["hy_b2_2"][0])),
                                 (cols[:, 2:3], col(ins["hy_freq_2"][0, 0])), (cols[:, 3:4], col(ins["hy_freq_2"][0, 1]))):
                    sp.dma_start(dst, src).then_inc(s.loaded, 16)

            @block.tensor
            def _(pe):
                pe.wait_ge(s.loaded, 16 * 7)
                pe.matmul(ps[0:H, 0, :], w1[:, :], emb[:, :], start=True, stop=True).then_inc(s.product, 1)
                pe.wait_ge(s.sine, 1)
                pe.matmul(ps[0:H, 1, :], w2[:, :], first[:, :], start=True, stop=True).then_inc(s.product, 1)

            @block.vector
            def _(dve):
                c = Chain(dve, s.chain)
                dve.wait_ge(s.loaded, 16 * 7)
                for n in range(2):
                    dve.wait_ge(s.product, n + 1)
                    if n:
                        dve.wait_ge(s.sine, 1)
                    c(dve.tensor_scalar(arg[:, :], ps[0:H, n, :], cols[:, n:n + 1], cols[:, 2 + n:3 + n], ALU.add, ALU.mult))
                    c.wait()
                    c(dve.tensor_scalar(turns[:, :], arg[:, :], 1.0 / two_pi, magic, ALU.mult, ALU.add))
                    c.wait()
                    c(dve.tensor_scalar(turns[:, :], turns[:, :], -magic, None, ALU.add))
                    for part in (c1, c2, c3):
                        c.wait()
                        c(dve.scalar_tensor_tensor(out=arg[:, :], in0=turns[:, :], scalar=-part, in1=arg[:, :],
                                                   op0=ALU.mult, op1=ALU.add))
                    c.wait()
                    dve.tensor_scalar(arg[:, :], arg[:, :], pi, -pi, ALU.min, ALU.max).then_inc(s.reduced, 1)

            @block.scalar
            def _(act):
                for n, dst in ((0, first), (1, hidden)):
                    act.wait_ge(s.reduced, n + 1)
                    act.activation(dst[:, :], arg[:, :], ACT.Sin).then_inc(s.sine, 1)
        s.clear()


def filter_stage(core, ins, order, hidden, su_hi, su_lo, di_hi, di_lo):
    nc, s, ps = core.nc, Sems(core.nc, f"fl{order}"), core.ps
    with ExitStack() as ctx:
        sb = lambda n, sh: ctx.enter_context(nc.sbuf_tensor(f"fl{order}_{n}", sh, fp32))
        w3, decay = sb("w3", [64, 2, HY]), sb("decay", [P, 2, HY])
        fwd, bwd, tmp, bias = sb("fwd", [P, 2, HY]), sb("bwd", [P, 2, HY]), sb("tmp", [P, 2, HY]), sb("bias", [1, HY])
        with nc.Block() as block:
            @block.sync
            def _(sp):
                for direction in range(2):
                    c0 = (2 * direction + order) * HY
                    sp.dma_start(w3[:, direction, :], ins["hy_w3_2"][0, :, c0:c0 + HY]).then_inc(s.loaded, 16)
                sp.dma_start(bias[:, :], ins["hy_bias_2"][0, order:order + 1, :]).then_inc(s.loaded, 16)
                for t in range(TT):
                    if t >= 2:
                        sp.wait_ge(s.halves, 2 * (t - 1))
                    sp.dma_start(decay[:, t % 2, :], ins["hy_decay"][P * t:P * t + P, :]).then_inc(s.decay_even if t % 2 == 0 else s.decay_odd, 16)

            @block.tensor
            def _(pe):
                pe.wait_ge(s.loaded, 48)
                for t in range(TT):
                    if t >= 2:
                        pe.wait_ge(s.halves, 2 * (t - 1))
                    for direction in range(2):
                        pe.matmul(ps[:, 2 * (t % 2) + direction, :], hidden[:, P * t:P * t + P], w3[:, direction, :],
                                  start=True, stop=True).then_inc(s.product, 1)

            @block.vector
            def _(dve):
                c = Chain(dve, s.chain)
                for t in range(TT):
                    b = t % 2
                    dve.wait_ge(s.decay_even if b == 0 else s.decay_odd, 16 * (t // 2 + 1))
                    dve.wait_ge(s.product, 2 * t + 2)
                    if t >= 2:
                        dve.wait_ge(s.lo_done, 2 * (t - 1))
                    dve.tensor_tensor(fwd[:, b, :], ps[:, 2 * b, :], decay[:, b, :], ALU.mult).then_inc(s.halves, 1)
                    dve.tensor_tensor(bwd[:, b, :], ps[:, 2 * b + 1, :], decay[:, b, :], ALU.mult).then_inc(s.halves, 1)
                    dve.wait_ge(s.halves, 2 * t + 2)
                    if t == 0:
                        c(dve.memset(bwd[0:1, 0, :], 0.0))
                        c(dve.tensor_tensor(fwd[0:1, 0, :], fwd[0:1, 0, :], bias[:, :], ALU.add))
                        c.wait()
                    dve.tensor_tensor(tmp[:, b, :], fwd[:, b, :], bwd[:, b, :], ALU.add).then_inc(s.combined, 1)
                    dve.wait_ge(s.combined, 2 * t + 1)
                    dve.tensor_tensor(fwd[:, b, :], fwd[:, b, :], bwd[:, b, :], ALU.subtract).then_inc(s.combined, 1)

            @block.scalar
            def _(act):
                for t in range(TT):
                    act.wait_ge(s.combined, 2 * t + 2)
                    act.activation(su_hi[:, t, :], tmp[:, t % 2, :], ACT.Copy).then_inc(s.hi_done, 1)
                    act.activation(di_hi[:, t, :], fwd[:, t % 2, :], ACT.Copy).then_inc(s.hi_done, 1)

            @block.gpsimd
            def _(pool):
                for t in range(TT):
                    pool.wait_ge(s.hi_done, 2 * t + 2)
                    pool.tensor_tensor(su_lo[:, t, :], tmp[:, t % 2, :], su_hi[:, t, :].bitcast(fp32), ALU.subtract).then_inc(s.lo_done, 1)
                    pool.tensor_tensor(di_lo[:, t, :], fwd[:, t % 2, :], di_hi[:, t, :].bitcast(fp32), ALU.subtract).then_inc(s.lo_done, 1)
        s.clear()


def long_conv(core, ins, order, hidden, src, finish):
    nc, ps = core.nc, core.ps
    with ExitStack() as outer:
        f32t = lambda c, n, sh, d=fp32: c.enter_context(nc.sbuf_tensor(f"lc{order}_{n}", sh, d))
        k_re, k_im = f32t(outer, "k_re", [P, 4, HY]), f32t(outer, "k_im", [P, 4, HY])
        k_re0 = f32t(outer, "k_re0", [P, HY])
        with ExitStack() as ctx:
            su_hi, su_lo, di_hi, di_lo = (f32t(ctx, n, [P, 4, HY], fp32r) for n in ("su_hi", "su_lo", "di_hi", "di_lo"))
            filter_stage(core, ins, order, hidden, su_hi, su_lo, di_hi, di_lo)
            linear_stage(core, f"kr{order}", feature_tiles(0, 1, 512, 4), su_hi, su_lo,
                         dve_tile=store_tile(core, lambda t: k_re[:, t, :]))
            def keep_im(dve, s, t):
                dve.wait_ge(s.tile_done, t + 1)
                dve.tensor_copy(k_im[:, t, :], ps[:, t % 4, :]).then_inc(s.bank_free, 1)
            linear_stage(core, f"ki{order}", feature_tiles(0, 1, 512, 4), di_hi, di_lo, dve_tile=keep_im)

            def keep_last(dve, s, t):
                dve.wait_ge(s.tile_done, 1)
                dve.tensor_copy(k_re0[:, :], k_re[:, 0, :]).then_inc(s.copied, 1)
                dve.memset(k_im[0:1, 0, :], 0.0).then_inc(s.copied, 1)
                dve.wait_ge(s.copied, 2)
                dve.tensor_copy(k_re0[0:1, :], ps[0:1, 0, :]).then_inc(s.bank_free, 1)
            linear_stage(core, f"kn{order}",
                         [[(0, slice(0, 32), [(k, k) for k in range(4)], None)]], su_hi, su_lo, dve_tile=keep_last)

        z_re, z_im = f32t(outer, "z_re", [P, 4, HY]), f32t(outer, "z_im", [P, 4, HY])
        with ExitStack() as ctx:
            z_hi, z_lo = (f32t(ctx, n, [P, 4, HY], fp32r) for n in ("z_hi", "z_lo"))
            split_stage(core, f"zs{order}", src, z_hi, z_lo, 4)
            linear_stage(core, f"zr{order}", feature_tiles(0, 2, 512, 4), z_hi, z_lo,
                         dve_tile=store_tile(core, lambda t: (z_re if t < 4 else z_im)[:, t % 4, :]))
        yhi, ylo = f32t(outer, "yhi", [P, 8, HY], fp32r), f32t(outer, "ylo", [P, 8, HY], fp32r)
        s = Sems(nc, f"cm{order}")
        with ExitStack() as ctx:
            a, b, y = (f32t(ctx, n, [P, 2, HY]) for n in ("a", "b", "y"))
            with nc.Block() as block:
                @block.vector
                def _(dve):
                    for n in range(8):
                        f, im = n // 2, n % 2
                        if n >= 2:
                            dve.wait_ge(s.lo_done, n - 1)
                        re = k_re0[:, :] if f == 0 else k_re[:, f, :]
                        if not im:
                            dve.tensor_tensor(a[:, im, :], z_re[:, f, :], k_re[:, f, :], ALU.mult).then_inc(s.terms, 1)
                            dve.tensor_tensor(b[:, im, :], z_im[:, f, :], k_im[:, f, :], ALU.mult).then_inc(s.terms, 1)
                        else:
                            dve.tensor_tensor(a[:, im, :], z_re[:, f, :], k_im[:, f, :], ALU.mult).then_inc(s.terms, 1)
                            dve.tensor_tensor(b[:, im, :], z_im[:, f, :], re, ALU.mult).then_inc(s.terms, 1)
                        dve.wait_ge(s.terms, 2 * n + 2)
                        dve.tensor_tensor(y[:, im, :], a[:, im, :], b[:, im, :], ALU.add if im else ALU.subtract).then_inc(s.y_ready, 1)

                @block.scalar
                def _(act):
                    for n in range(8):
                        act.wait_ge(s.y_ready, n + 1)
                        act.activation(yhi[:, n // 2 + 4 * (n % 2), :], y[:, n % 2, :], ACT.Copy).then_inc(s.hi_done, 1)

                @block.gpsimd
                def _(pool):
                    for n in range(8):
                        k = n // 2 + 4 * (n % 2)
                        pool.wait_ge(s.hi_done, n + 1)
                        pool.tensor_tensor(ylo[:, k, :], y[:, n % 2, :], yhi[:, k, :].bitcast(fp32), ALU.subtract)\
                            .then_inc(s.lo_done, 1)
            s.clear()
        finish(yhi, ylo)


def hyena(core, ins, v_tok, x1_tok, x2f):
    nc, ps = core.nc, core.ps
    with nc.sbuf_tensor("hy_hidden", [64, SEQ], fp32) as hidden:
        filter_basis_stage(core, ins, hidden)

        def first(yhi, ylo):
            def step(dve, s, t):
                dve.wait_ge(s.tile_done, t + 1)
                dve.tensor_tensor(x1_tok[:, t, :], x1_tok[:, t, :], ps[:, t % 4, :], ALU.mult).then_inc(s.bank_free, 1)
            linear_stage(core, "inv0", feature_tiles(0, 2, 256, 8), yhi, ylo, dve_tile=step)
        long_conv(core, ins, 0, hidden, v_tok, first)

        def second(yhi, ylo):
            def step(dve, s, t):
                j, f = t // 4, t % 4
                cols = slice(256 * j, 256 * j + 256)
                dve.wait_ge(s.tile_done, t + 1)
                dve.tensor_tensor(x2f[:, f, cols], x2f[:, f, cols], ps[:, t % 4, 0:256], ALU.mult).then_inc(s.bank_free, 1)
            linear_stage(core, "inv1", token_tiles(0, 2, 256, 8), yhi, ylo, dve_tile=step)
        long_conv(core, ins, 1, hidden, x1_tok, second)


def window_bias_stage(core, ins, bias):
    nc, s, ps = core.nc, Sems(core.nc, "wb"), core.ps
    NH, NR, NC = 8, 15, 31
    with ExitStack() as ctx:
        sb = lambda n, sh: ctx.enter_context(nc.sbuf_tensor(f"wb_{n}", sh, fp32))
        rows, cols, anti, mask = sb("rows", [NH * NR, NC]), sb("cols", [NC, NH * NR]), sb("anti", [NC, 127]), sb("mask", [P, 64])
        with nc.Block() as block:
            @block.sync
            def _(sp):
                sp.dma_start(rows[:, :], ins["na_rpb_2"][0].rearrange("h r c -> (h r) c")).then_inc(s.loaded, 16)
                sp.dma_start(anti[:, :], ins["anti_diagonal"]).then_inc(s.loaded, 16)
                sp.dma_start(mask[:, :], ins["column_mask"]).then_inc(s.loaded, 16)

            @block.tensor
            def _(pe):
                pe.wait_ge(s.loaded, 48)
                pe.transpose(ps[0:NC, 7, 0:NH * NR], rows[:, :], core.ident[0:NH * NR, 0:NH * NR]).then_inc(s.turned, 1)
                pe.wait_ge(s.cols_ready, 1)
                for n in range(16):
                    if n >= 4:
                        pe.wait_ge(s.stored, 2 * (n - 3))
                    for q in range(4):
                        x = 63 - (4 * n + q)
                        for half in range(2):
                            mm = pe.matmul(ps[64 * half:64 * half + 64, n % 4, 120 * q:120 * q + 120],
                                           anti[:, x:x + 64], cols[:, :], start=True, stop=True)
                    mm.then_inc(s.picked, 1)

            @block.vector
            def _(dve):
                dve.wait_ge(s.turned, 1)
                dve.tensor_copy(cols[:, :], ps[0:NC, 7, 0:NH * NR]).then_inc(s.cols_ready, 1)
                for n in range(16):
                    dve.wait_ge(s.picked, n + 1)
                    for half in range(2):
                        r = slice(64 * half, 64 * half + 64)
                        out = bias[r, :, half:half + NR, 4 * n:4 * n + 4].rearrange("p h m c -> p c h m")
                        for h0 in (0,):
                            dve.tensor_tensor(out, ps[r, n % 4, 0:480].rearrange("p (c h m) -> p c h m", c=4, h=NH),
                                              mask[r, 4 * n:4 * n + 4].unsqueeze(2).unsqueeze(3).to_broadcast([64, 4, NH, NR]),
                                              ALU.add).then_inc(s.stored, 1)
        s.clear()


def neighbourhood_stage(core, qf, kf, v, bias, yb):
    nc, s, ps = core.nc, Sems(core.nc, "na"), core.ps
    NH = 8
    with ExitStack() as ctx:
        sb = lambda n, sh: ctx.enter_context(nc.sbuf_tensor(f"na_{n}", sh, fp32))
        sc, pr, pt = sb("sc", [P, 2, SEQ]), sb("pr", [P, 2, SEQ]), sb("pt", [P, 2, TT, SEQ])
        neg, tot, inv = sb("neg", [P, 4]), sb("tot", [P, 4]), sb("inv", [P, 4])
        units = [(h, i) for h in range(NH) for i in range(TT)]
        U = len(units)
        with nc.Block() as block:
            @block.tensor
            def _(pe):
                def scores(u):
                    h, i = units[u]
                    t, r = h // 2, HD * (h % 2)
                    if u >= 2:
                        pe.wait_ge(s.biased, u - 1)
                    pe.matmul(ps[:, u % 2, :], qf[r:r + HD, t, P * i:P * i + P], kf[r:r + HD, t, :],
                              start=True, stop=True).then_inc(s.scores_done, 1)

                def turn(u):
                    pe.wait_ge(s.normed, u + 1)
                    if u >= 2:
                        pe.wait_ge(s.copied, u - 1)
                    for j in range(TT):
                        mm = pe.transpose(ps[:, 2 + u % 2, P * j:P * j + P], pr[:, u % 2, P * j:P * j + P], core.ident[:, :])
                    mm.then_inc(s.turned, 1)

                def values(h):
                    t, r = h // 2, HD * (h % 2)
                    pe.wait_ge(s.copied, 4 * h + 4)
                    if h % 2 == 0 and t >= 2:
                        pe.wait_ge(s.out_done, t - 1)
                    for j in range(TT):
                        mm = pe.matmul(ps[r:r + HD, 4 + t % 2, :], v[:, j, HD * h:HD * h + HD], pt[:, h % 2, j, :],
                                       start=(j == 0), stop=(j == TT - 1))
                    mm.then_inc(s.values_done, 1)
                for u in range(U + 3):
                    if u < U:
                        scores(u)
                    if 2 <= u < U + 2:
                        turn(u - 2)
                    if u >= 3 and (u - 3) % 4 == 3:
                        values((u - 3) // 4)

            @block.vector
            def _(dve):
                def out(dve, t):
                    dve.wait_ge(s.values_done, 2 * t + 2)
                    dve.tensor_copy(yb[:, t, :], ps[:, 4 + t % 2, :]).then_inc(s.out_done, 1)

                def soften(u):
                    h, i = units[u]
                    dve.wait_ge(s.scores_done, u + 1)
                    if u >= 2:
                        dve.wait_ge(s.exp_done, u - 1)
                    m0 = 8 - 2 * i
                    dve.tensor_tensor(sc[:, u % 2, :].rearrange("p (m c) -> p m c", m=8),
                                      ps[:, u % 2, :].rearrange("p (m c) -> p m c", m=8),
                                      bias[:, h, m0 - 1:m0 + 7, :], ALU.add).then_inc(s.biased, 1)
                    dve.wait_ge(s.biased, u + 1)
                    dve.tensor_reduce(neg[:, u % 4:u % 4 + 1], sc[:, u % 2, :], AX.X, ALU.max, negate=True).then_inc(s.max_done, 1)

                def normalise(u):
                    dve.wait_ge(s.exp_done, u + 1)
                    dve.reciprocal(inv[:, u % 4:u % 4 + 1], tot[:, u % 4:u % 4 + 1]).then_inc(s.inv_done, 1)
                    dve.wait_ge(s.inv_done, u + 1)
                    dve.tensor_scalar(pr[:, u % 2, :], pr[:, u % 2, :], inv[:, u % 4:u % 4 + 1], None, ALU.mult).then_inc(s.normed, 1)

                for u in range(U + 1):
                    if u < U:
                        soften(u)
                    if u >= 1:
                        normalise(u - 1)
                    if u >= 10 and u % 8 == 2:
                        out(dve, (u - 10) // 8)
                out(dve, NH // 2 - 1)

            @block.scalar
            def _(act):
                def copy(u):
                    h, i = units[u]
                    act.wait_ge(s.turned, u + 1)
                    if h >= 2:
                        act.wait_ge(s.values_done, h - 1)
                    act.activation(pt[:, h % 2, :, P * i:P * i + P], ps[:, 2 + u % 2, :].rearrange("p (j q) -> p j q", j=TT),
                                   ACT.Copy).then_inc(s.copied, 1)
                for u in range(U + 2):
                    if u < U:
                        act.wait_ge(s.max_done, u + 1)
                        if u >= 2:
                            act.wait_ge(s.turned, u - 1)
                        act.activation(pr[:, u % 2, :], sc[:, u % 2, :], ACT.Exp, bias=neg[:, u % 4:u % 4 + 1],
                                       accum_out=tot[:, u % 4:u % 4 + 1]).then_inc(s.exp_done, 1)
                    if u >= 2:
                        copy(u - 2)
        s.clear()


def merge_stages(core, xhi, xlo, parts, merged, norm):
    nc, ps = core.nc, core.ps
    with ExitStack() as ctx:
        sig, prod = (ctx.enter_context(nc.sbuf_tensor(f"mg_{n}", [P, 2, SEQ], fp32)) for n in ("sig", "prod"))
        for b, (yhi, ylo) in enumerate(parts):
            if b == 0:
                add = lambda dve, f, pr: dve.tensor_copy(merged[:, f, :], pr)
            else:
                add = lambda dve, f, pr: dve.tensor_tensor(merged[:, f, :], merged[:, f, :], pr, ALU.add)
            gated_stage(core, f"mg{b}", [(k, k) for k in range(4)], yhi, ylo, xhi, xlo, sig, prod,
                        lambda f: core.gain("gate_bias_2", DK * b + f), add, norm if b == 0 else None)


def branches(core, ins):
    nc = core.nc
    g = lambda n: (lambda k: core.gain("norm_gains_2", DK * n + k))
    with ExitStack() as ctx:
        sb = lambda c, n, sh, d=fp32: c.enter_context(nc.sbuf_tensor(f"b2_{n}", sh, d))
        y_all = sb(ctx, "y_all", [P, 12, SEQ])
        ya, yb, yc = (y_all[:, 4 * b:4 * b + 4, :] for b in range(3))
        with ExitStack() as mid:
            x1_tok = sb(mid, "x1_tok", [P, 4, SEQ])
            with ExitStack() as c1:
                xhi, xlo = sb(c1, "xhi", [P, DK, SEQ], fp32r), sb(c1, "xlo", [P, DK, SEQ], fp32r)
                hyena_in(core, xhi, xlo, yb, x1_tok, ya, Norm(core, core.h, g(0), xhi, xlo, "sum"))
                short_conv_in(core, xhi, xlo, yc)
            hyena(core, ins, yb, x1_tok, ya)
        with ExitStack() as mid:
            qf, kf, nv = (sb(mid, n, [P, 4, SEQ]) for n in ("qf", "kf", "nv"))
            with ExitStack() as c1:
                xhi, xlo = sb(c1, "x1hi", [P, DK, SEQ], fp32r), sb(c1, "x1lo", [P, DK, SEQ], fp32r)
                def qk(dve, s, t):
                    dve.wait_ge(s.tile_done, t + 1)
                    dst, scale = (qf, HD ** -0.5) if t < 4 else (kf, 1.0)
                    dve.tensor_scalar(dst[:, t % 4, :], core.ps[:, t % 4, :], scale, None, ALU.mult).then_inc(s.bank_free, 1)
                linear_stage(core, "naqk", feature_tiles(0, 4, 256, DK), xhi, xlo, dve_tile=qk,
                             norm=Norm(core, core.h, g(0), xhi, xlo, "inverse"))
                linear_stage(core, "nav", token_tiles(0, 2, 256, DK), xhi, xlo,
                             dve_tile=store_tile(core, lambda t: nv[:, t % TT, 256 * (t // TT):256 * (t // TT) + 256]))
            bias = sb(mid, "bias", [P, 8, 16, 64])
            window_bias_stage(core, ins, bias)
            neighbourhood_stage(core, qf, kf, nv, bias, yb)
        y3 = (ya, yb, yc)
        parts = []
        for b in range(3):
            hi, lo = sb(ctx, f"yh{b}", [P, 4, SEQ], fp32r), sb(ctx, f"yl{b}", [P, 4, SEQ], fp32r)
            split_stage(core, f"ys{b}", y3[b], hi, lo, 4)
            parts.append((hi, lo))
        merged = y_all[:, 0:DK, :]
        with ExitStack() as c2:
            xhi, xlo = sb(c2, "x2hi", [P, DK, SEQ], fp32r), sb(c2, "x2lo", [P, DK, SEQ], fp32r)
            merge_stages(core, xhi, xlo, parts, merged, Norm(core, core.h, g(0), xhi, xlo, "inverse"))
            split_stage(core, "mgs", merged, xhi, xlo, DK)
            linear_stage(core, "wout", feature_tiles(0, 4, 256, DK), xhi, xlo,
                         dve_tile=store_tile(core, lambda t: merged[:, t, :]), squares=stored_squares(core, merged))
        add_normed_stage(core, "n1", merged, g(1))


def memory_attention_stage(core, qf, kf, v, ohi, olo):
    nc, s, ps = core.nc, Sems(core.nc, "xa"), core.ps
    NH, W = 4, 256
    with ExitStack() as ctx:
        sb = lambda n, sh: ctx.enter_context(nc.sbuf_tensor(f"xa_{n}", sh, fp32))
        pr, pt = sb("pr", [P, 2, W]), sb("pt", [P, 2, MT, SEQ])
        neg, tot, inv = sb("neg", [P, 4]), sb("tot", [P, 4]), sb("inv", [P, 4])
        tmp = core.split_buf
        units = [(h, i) for h in range(NH) for i in range(TT)]
        U = len(units)
        with nc.Block() as block:
            @block.tensor
            def _(pe):
                def scores(u):
                    h, i = units[u]
                    if u >= 2:
                        pe.wait_ge(s.exp_done, u - 1)
                    for k in range(2):
                        mm = pe.matmul(ps[:, u % 2, 0:W], qf[:, 2 * h + k, P * i:P * i + P], kf[:, 2 * h + k, :],
                                       start=(k == 0), stop=(k == 1))
                    mm.then_inc(s.scores_done, 1)

                def turn(u):
                    pe.wait_ge(s.normed, u + 1)
                    if u >= 2:
                        pe.wait_ge(s.copied, u - 1)
                    for j in range(MT):
                        mm = pe.transpose(ps[:, 2 + u % 2, P * j:P * j + P], pr[:, u % 2, P * j:P * j + P], core.ident[:, :])
                    mm.then_inc(s.turned, 1)

                def values(h):
                    pe.wait_ge(s.copied, 4 * h + 4)
                    for d in range(2):
                        n = 2 * h + d
                        if n >= 2:
                            pe.wait_ge(s.out_done, n - 1)
                        for j in range(MT):
                            mm = pe.matmul(ps[:, 4 + n % 2, :], v[:, j, P * n:P * n + P], pt[:, h % 2, j, :],
                                           start=(j == 0), stop=(j == MT - 1))
                        mm.then_inc(s.values_done, 1)
                for u in range(U + 3):
                    if u < U:
                        scores(u)
                    if 2 <= u < U + 2:
                        turn(u - 2)
                    if u >= 3 and (u - 3) % 4 == 3:
                        values((u - 3) // 4)

            @block.vector
            def _(dve):
                def out(n):
                    dve.wait_ge(s.values_done, n + 1)
                    if n >= 2:
                        dve.wait_ge(s.lo_done, n - 1)
                    dve.tensor_copy(tmp[n % 2][:, :], ps[:, 4 + n % 2, :]).then_inc(s.out_done, 1)

                for u in range(U + 1):
                    if u < U:
                        dve.wait_ge(s.scores_done, u + 1)
                        dve.tensor_reduce(neg[:, u % 4:u % 4 + 1], ps[:, u % 2, 0:W], AX.X, ALU.max, negate=True)\
                           .then_inc(s.max_done, 1)
                    if u >= 1:
                        w = u - 1
                        dve.wait_ge(s.exp_done, w + 1)
                        dve.reciprocal(inv[:, w % 4:w % 4 + 1], tot[:, w % 4:w % 4 + 1]).then_inc(s.inv_done, 1)
                        dve.wait_ge(s.inv_done, w + 1)
                        dve.tensor_scalar(pr[:, w % 2, :], pr[:, w % 2, :], inv[:, w % 4:w % 4 + 1], None, ALU.mult)\
                           .then_inc(s.normed, 1)
                    if u >= 7 and (u - 7) % 4 == 0:
                        out(2 * ((u - 7) // 4))
                        out(2 * ((u - 7) // 4) + 1)
                for n in range(6, 8):
                    out(n)

            @block.scalar
            def _(act):
                def high(n):
                    act.wait_ge(s.out_done, n + 1)
                    act.activation(ohi[:, n, :], tmp[n % 2][:, :], ACT.Copy).then_inc(s.hi_done, 1)

                def copy(u):
                    h, i = units[u]
                    act.wait_ge(s.turned, u + 1)
                    if h >= 2:
                        act.wait_ge(s.values_done, 2 * (h - 1))
                    act.activation(pt[:, h % 2, :, P * i:P * i + P],
                                   ps[:, 2 + u % 2, 0:W].rearrange("p (j q) -> p j q", j=MT), ACT.Copy).then_inc(s.copied, 1)
                for u in range(U + 2):
                    if u < U:
                        act.wait_ge(s.max_done, u + 1)
                        if u >= 2:
                            act.wait_ge(s.turned, u - 1)
                        act.activation(pr[:, u % 2, :], ps[:, u % 2, 0:W], ACT.Exp, bias=neg[:, u % 4:u % 4 + 1],
                                       accum_out=tot[:, u % 4:u % 4 + 1]).then_inc(s.exp_done, 1)
                    if u >= 2:
                        copy(u - 2)
                    if u >= 7 and (u - 7) % 4 == 0:
                        high(2 * ((u - 7) // 4))
                        high(2 * ((u - 7) // 4) + 1)
                for n in range(6, 8):
                    high(n)

            @block.gpsimd
            def _(pool):
                for n in range(8):
                    pool.wait_ge(s.hi_done, n + 1)
                    pool.tensor_tensor(olo[:, n, :], tmp[n % 2][:, :], ohi[:, n, :].bitcast(fp32), ALU.subtract)\
                        .then_inc(s.lo_done, 1)
        s.clear()


def memory_attention(core, ins):
    nc, ps = core.nc, core.ps
    g = lambda n: (lambda k: core.gain("norm_gains_2", DK * n + k))
    with ExitStack() as ctx:
        sb = lambda n, sh, d=fp32: ctx.enter_context(nc.sbuf_tensor(f"xm_{n}", sh, d))
        qf, kf, v = sb("q", [P, DK, SEQ]), sb("k", [P, DK, N_MEM]), sb("v", [P, MT, D])
        xhi, xlo = sb("xhi", [P, DK, SEQ], fp32r), sb("xlo", [P, DK, SEQ], fp32r)
        with ExitStack() as c1:
            mem = c1.enter_context(nc.sbuf_tensor("xm_mem", [P, MT, D], fp32))
            mt = c1.enter_context(nc.sbuf_tensor("xm_memt", [P, DK, N_MEM], fp32))
            mhi = c1.enter_context(nc.sbuf_tensor("xm_mhi", [P, DK, N_MEM], fp32r))
            mlo = c1.enter_context(nc.sbuf_tensor("xm_mlo", [P, DK, N_MEM], fp32r))
            s = Sems(nc, "mt")
            with nc.Block() as block:
                @block.sync
                def _(sp):
                    sp.dma_start(mem[:, :, :], ins["mem_2"][0].rearrange("(t p) d -> p t d", p=P)).then_inc(s.loaded, 16)

                @block.tensor
                def _(pe):
                    pe.wait_ge(s.loaded, 16)
                    for n in range(4):
                        t, half = n // 2, n % 2
                        for k in range(4):
                            c = P * (4 * half + k)
                            mm = pe.transpose(ps[:, n, P * k:P * k + P], mem[:, t, c:c + P], core.ident[:, :])
                        mm.then_inc(s.turned, 1)

                @block.scalar
                def _(act):
                    for n in range(4):
                        t, half = n // 2, n % 2
                        act.wait_ge(s.turned, n + 1)
                        act.activation(mt[:, 4 * half:4 * half + 4, P * t:P * t + P],
                                       ps[:, n, :].rearrange("p (k c) -> p k c", k=4), ACT.Copy).then_inc(s.stored, 1)
            s.clear()
            linear_stage(core, "xak", feature_tiles(0, 4, 256, DK), mhi, mlo,
                         norm=Norm(core, mt, lambda k: core.gain("mem_norm_2", k), mhi, mlo, "nothing", toks=N_MEM,
                                   bank=6),
                         dve_tile=store_tile(core, lambda t: kf[:, t, :]))
            linear_stage(core, "xav", token_tiles(0, 4, 256, DK, MT), mhi, mlo,
                         dve_tile=store_tile(core, lambda t: v[:, t % MT, 256 * (t // MT):256 * (t // MT) + 256]))
        def scaled_q(dve, s, t):
            dve.wait_ge(s.tile_done, t + 1)
            dve.tensor_scalar(qf[:, t, :], ps[:, t % 4, :], 256 ** -0.5, None, ALU.mult).then_inc(s.bank_free, 1)
        linear_stage(core, "xaq", feature_tiles(0, 4, 256, DK), xhi, xlo, dve_tile=scaled_q,
                     norm=Norm(core, core.h, g(2), xhi, xlo, "total"))
        memory_attention_stage(core, qf, kf, v, xhi, xlo)
        linear_stage(core, "xao", feature_tiles(0, 4, 256, DK), xhi, xlo,
                     dve_tile=store_tile(core, lambda t: qf[:, t, :]), squares=stored_squares(core, qf))
        add_normed_stage(core, "n3", qf, g(3))


def feed_forward(core, ins):
    nc, ps = core.nc, core.ps
    g = lambda n: (lambda k: core.gain("norm_gains_2", DK * n + k))
    with ExitStack() as ctx:
        sb = lambda c, n, sh, d=fp32: c.enter_context(nc.sbuf_tensor(f"ff_{n}", sh, d))
        ahi, alo = sb(ctx, "ahi", [P, FF_TILES, SEQ], fp32r), sb(ctx, "alo", [P, FF_TILES, SEQ], fp32r)
        with ExitStack() as c1:
            xhi, xlo = sb(c1, "xhi", [P, DK, SEQ], fp32r), sb(c1, "xlo", [P, DK, SEQ], fp32r)
            gate = sb(c1, "gate", [P, 2, SEQ])
            cg, cv, gel = (gate[:, 0, :], gate[:, 1, :]), core.sq, core.split_buf
            tiles, order = [], []
            for j in range(FF_TILES // 2):
                for kind in range(2):
                    for c in range(2):
                        tiles.append([(2 * j + kind, slice(P * c, P * c + P), [(k, k) for k in range(DK)], None)])
                        order.append((kind, 2 * j + c))

            def conv_dve(dve, s, t):
                c = Chain(dve, s.chain)
                c.n = 2 * t
                kind, f = order[t]
                dve.wait_ge(s.tile_done, t + 1)
                if f >= 2:
                    if kind == 0:
                        dve.wait_ge(s.gelu_done, f - 1)
                    else:
                        dve.wait_ge(s.lo_done, f - 1)
                buf = (cv if kind else cg)[f % 2][:, 0:SEQ]
                centred_conv(dve, c, buf, ps[:, t % 4, :],
                             [core.gain("ffn_conv_2", 2 * FF_TILES * j + FF_TILES * kind + f) for j in range(3)])\
                    .then_inc(s.bank_free, 1)
                if kind == 1:
                    dve.wait_ge(s.gelu_done, f + 1)
                    dve.wait_ge(s.bank_free, t + 1)
                    dve.tensor_tensor(buf, buf, gel[f % 2][:, :], ALU.mult).then_inc(s.product, 1)

            def gelu_act(act, s, t):
                kind, f = order[t]
                if kind == 0:
                    act.wait_ge(s.bank_free, t + 1)
                    if f >= 2:
                        act.wait_ge(s.product, f - 1)
                    act.activation(gel[f % 2][:, :], cg[f % 2], ACT.Gelu_apprx_tanh).then_inc(s.gelu_done, 1)
                else:
                    act.wait_ge(s.product, f + 1)
                    act.activation(ahi[:, f, :], cv[f % 2][:, :], ACT.Copy).then_inc(s.hi_done, 1)

            def low_pool(pool, s, t):
                kind, f = order[t]
                if kind == 1:
                    pool.wait_ge(s.hi_done, f + 1)
                    pool.tensor_tensor(alo[:, f, :], cv[f % 2][:, :], ahi[:, f, :].bitcast(fp32), ALU.subtract).then_inc(s.lo_done, 1)
            linear_stage(core, "up", tiles, xhi, xlo, act_tile=gelu_act, dve_tile=conv_dve, pool_tile=low_pool,
                         norm=Norm(core, core.h, g(4), xhi, xlo, "total"))
        y = sb(ctx, "y", [P, DK, SEQ])
        half = FF_TILES // 2
        tiles = [[(2 * t + q, slice(0, P), [(k, half * q + k) for k in range(half)], None) for q in range(2)]
                 for t in range(DK)]
        linear_stage(core, "down", tiles, ahi, alo, dve_tile=store_tile(core, lambda t: y[:, t, :]),
                     squares=stored_squares(core, y))
        add_normed_stage(core, "n5", y, g(5), total=False)


def constants():
    f32 = np.float32
    L, N = SEQ, 2 * SEQ
    t = np.arange(L)[:, None]
    f = np.arange(L)[None, :]
    angle = 2 * np.pi * ((t * f) % N) / N
    nyquist = (-1.0) ** np.arange(L)
    cos, sin = np.cos(angle), -np.sin(angle)
    sin[:, 0] = nyquist
    dft = np.concatenate([cos, sin], axis=1)
    weight = np.full(N, 2.0 / N)
    weight[0] = weight[L] = 1.0 / N
    idft = weight[:, None] * dft.T

    pos = np.linspace(0.0, 1.0, L, dtype=f32)[:, None]
    bands = 16
    w = (f32(2.0 * math.pi) * np.arange(L, dtype=f32)[:, None] / f32(L)).astype(f32)
    fr = np.linspace(1e-4, bands - 1, bands, dtype=f32)[None, :]
    fw = (fr * w).astype(f32)
    emb = np.concatenate([pos, np.cos(fw), -np.sin(fw)], axis=-1)
    deltas = np.abs(np.linspace(math.log(1e-2) / 1.5, math.log(1e-2) / 0.3, HY, dtype=f32))
    decay = np.exp(-pos * deltas)

    c = np.arange(64)
    start = np.clip(c - 8, 0, 48)
    inside = (c[None, :] >= start[:, None]) & (c[None, :] < start[:, None] + 16)
    mask = np.where(inside, 0.0, -1e30)
    anti = (np.arange(31)[:, None] + np.arange(127)[None, :] == 78)
    return {"dft": dft.astype(f32), "idft": idft.astype(f32), "pos_emb": emb.T.astype(f32),
            "hy_decay": decay.astype(f32), "column_mask": np.concatenate([mask, mask]).astype(f32),
            "anti_diagonal": anti.astype(f32)}


def weight_schedule(ins):
    m_in, w_in, wkv, up, down = (ins[n] for n in ("m_in", "w_in_2", "xa_wkv_2", "ffn_up_2", "ffn_down_2"))
    m_in, w_in, wkv = m_in[0], w_in[0], wkv[0]
    up, down = (a[0].rearrange("(k p) n -> p k n", p=P) for a in (up, down))
    conv_end = D_INNER + CONV_TILES * P
    sc0, gates0 = 6 * HY, 9 * HY
    dft, idft = ins["dft"], slabs_of(ins["idft"], 256)
    yield "mz", slabs_of(m_in, 256, 0, D_INNER)
    yield "mdt", slabs_of(m_in, HEADS, conv_end, conv_end + HEADS)
    yield "mx", slabs_of(m_in, 256, D_INNER, conv_end)
    yield "mout", slabs_of(ins["m_out"][0], P)
    yield "ple0", gated_slabs(ins["ple_proj"][0], ins["ple_gate"][0], 0)
    yield "sbk", slabs_of(ins["w_kv"], 256, 0, D)
    yield "sbv", slabs_of(ins["w_kv"], 256, D, 2 * D)
    yield "sbq", slabs_of(ins["s_in"][0], 256, 0, D)
    yield "sbg", slabs_of(ins["s_in"][0], 256, D, 2 * D)
    yield "sbo", slabs_of(ins["s_out"][0], 256)
    yield "ple1", gated_slabs(ins["ple_proj"][1], ins["ple_gate"][1], 0)
    yield "hyin", slabs_of(w_in, 256, 0, 3 * HY)
    yield "scin", slabs_of(w_in, 256, sc0 + HY, sc0 + 3 * HY) + slabs_of(w_in, 256, sc0, sc0 + HY)
    for order in range(2):
        yield f"kr{order}", slabs_of(dft, 512, 0, 512)
        yield f"ki{order}", slabs_of(dft, 512, 512, 1024)
        yield f"kn{order}", slabs_of(dft, 32, 512, 544)
        yield f"zr{order}", slabs_of(dft, 512)
        yield f"inv{order}", idft
    yield "naqk", slabs_of(w_in, 256, 3 * HY, 5 * HY)
    yield "nav", slabs_of(w_in, 256, 5 * HY, 6 * HY)
    for b in range(3):
        yield f"mg{b}", gated_slabs(ins["w_branch_2"][0, b], w_in, gates0 + D * b)
    yield "wout", slabs_of(ins["w_out_2"][0], 256)
    yield "xak", slabs_of(wkv, 256, 0, D)
    yield "xav", slabs_of(wkv, 256, D, 2 * D)
    yield "xaq", slabs_of(ins["xa_wq_2"][0], 256)
    yield "xao", slabs_of(ins["xa_wo_2"][0], 256)
    yield "up", [up[:, :, c:c + 256] for j in range(FF_TILES // 2) for c in (256 * j, D_FF + 256 * j)]
    half = FF_TILES // 2
    yield "down", [down[:, half * q:half * q + half, P * t:P * t + P] for t in range(DK) for q in range(2)]


def program(nc, ins, out):
    with ExitStack() as ctx:
        core = Core(nc, ctx, weight_schedule(ins))
        setup_stage(core, ins)
        mamba(core, ins)
        ple_stages(core, ins, 0)
        stick_breaking(core, ins)
        ple_stages(core, ins, 1)
        branches(core, ins)
        memory_attention(core, ins)
        feed_forward(core, ins)
        output_stage(core, out)


def kernel(**inputs):
    import numpy as _np
    import concourse.bacc as _bacc
    from concourse import mybir as _mybir
    from concourse.bass_utils import run_bass_kernel_spmd as _run

    nc = _bacc.Bacc("TRN2", target_bir_lowering=False, num_devices=1)
    arrays, ins = {}, {}
    for name, a in list(inputs.items()) + list(constants().items()):
        a = _np.ascontiguousarray(a)
        arrays[f"in_{name}"] = a
        ins[name] = nc.dram_tensor(f"in_{name}", a.shape, _mybir.dt.from_np(a.dtype), kind="ExternalInput").ap()
    out = nc.dram_tensor("out", (1, SEQ, D), _mybir.dt.float32, kind="ExternalOutput").ap()
    program(nc, ins, out)
    r = _run(nc, [arrays], core_ids=[0])
    return r.results[0]["out"]
```

```python
import math
from contextlib import ExitStack

import numpy as np
import concourse.bass as bass
from concourse import mybir

fp32 = mybir.dt.float32
fp32r = mybir.dt.float32r
ALU = mybir.AluOpType
ACT = mybir.ActivationFunctionType
AX = mybir.AxisListType

P = 128
SEQ = 512
TT = SEQ // P
D = 1024
DK = D // P
EPS = 1e-6

D_INNER = 2048
HEADS = 32
GROUPS = 4
HG = HEADS // GROUPS
HD = 64
CONV_TILES = 24

N_MEM = 256
MT = N_MEM // P
HY = 512
D_FF = 2816
FF_TILES = D_FF // P

PARAM_ROWS = [
    ("m_conv_w", 4 * CONV_TILES), ("m_conv_b", CONV_TILES), ("m_norm", DK),
    ("m_ynorm", 2 * DK), ("kv_norm", DK), ("s_norm", DK), ("ple_norm", 2 * DK), ("norm_gains_2", 6 * DK),
    ("mem_norm_2", DK), ("gate_bias_2", 3 * DK),
    ("hy_short_w_2", 36), ("sc_conv_w_2", 12), ("ffn_conv_2", 3 * 2 * FF_TILES),
]
PARAM_COL = {}
_col = 0
for _name, _rows in PARAM_ROWS:
    PARAM_COL[_name] = _col
    _col += _rows
PARAM_TOTAL = _col


class Chain:

    def __init__(self, eng, sem):
        self.eng, self.sem, self.n = eng, sem, 0

    def __call__(self, instruction):
        instruction.then_inc(self.sem, 1)
        self.n += 1

    def wait(self):
        self.eng.wait_ge(self.sem, self.n)


class Weights:

    def __init__(self, nc, ctx, schedule):
        self.raw = [ctx.enter_context(nc.sbuf_tensor(f"w_raw{i}", [P, 2048], fp32)) for i in range(2)]
        self.hi = [ctx.enter_context(nc.sbuf_tensor(f"w_hi{i}", [P, 2048], fp32r)) for i in range(2)]
        self.lo = [ctx.enter_context(nc.sbuf_tensor(f"w_lo{i}", [P, 2048], fp32r)) for i in range(2)]
        self.loaded = [nc.alloc_semaphore(f"w_loaded{i}") for i in range(2)]
        self.hi_done = nc.alloc_semaphore("w_hi_done")
        self.lo_done = nc.alloc_semaphore("w_lo_done")
        self.slabs, self.first = [], {}
        for name, slabs in schedule:
            self.first[name] = len(self.slabs)
            self.slabs += slabs

    def size(self, n):
        return self.slabs[n].shape[1] * self.slabs[n].shape[2]

    def load(self, sp, n):
        if n >= len(self.slabs):
            return
        if n >= 2:
            sp.wait_ge(self.lo_done, n - 1)
        sp.dma_start(self.raw[n % 2][:, 0:self.size(n)].rearrange("p (k c) -> p k c", k=self.slabs[n].shape[1]),
                     self.slabs[n]).then_inc(self.loaded[n % 2], 16)

    def split_hi(self, act, n):
        if n >= len(self.slabs):
            return
        act.wait_ge(self.loaded[n % 2], 16 * (n // 2 + 1))
        act.activation(self.hi[n % 2][:, 0:self.size(n)], self.raw[n % 2][:, 0:self.size(n)], ACT.Copy)\
           .then_inc(self.hi_done, 1)

    def split_lo(self, pool, n):
        if n >= len(self.slabs):
            return
        pool.wait_ge(self.hi_done, n + 1)
        pool.tensor_tensor(self.lo[n % 2][:, 0:self.size(n)], self.raw[n % 2][:, 0:self.size(n)],
                           self.hi[n % 2][:, 0:self.size(n)].bitcast(fp32), ALU.subtract).then_inc(self.lo_done, 1)

    def take(self, pe, n):
        pe.wait_ge(self.lo_done, n + 1)
        return [s[n % 2][:, 0:self.size(n)].rearrange("p (k c) -> p k c", k=self.slabs[n].shape[1])
                for s in (self.hi, self.lo)]


def slabs_of(w, cols, c0=0, c1=None):
    v = w.rearrange("(k p) n -> p k n", p=P)
    c1 = w.shape[1] if c1 is None else c1
    return [v[:, :, c:min(c + cols, c1)] for c in range(c0, c1, cols)]


class Core:

    def __init__(self, nc, ctx, schedule):
        self.nc = nc
        Sems.retired.clear()
        sb = lambda n, s, d=fp32: ctx.enter_context(nc.sbuf_tensor(n, s, d))
        self.h = sb("h", [P, DK, SEQ])
        self.params = sb("params", [P, PARAM_TOTAL])
        self.ident = sb("ident", [P, P])
        self.ones = sb("ones", [P, P])
        self.head_ones = sb("head_ones", [P, P])
        self.upto = sb("upto", [P, P])
        self.after = sb("after", [P, P])
        self.minus_from_r = sb("minus_from_r", [P, P], fp32r)
        self.minus_ones_r = sb("minus_ones_r", [P, P], fp32r)
        self.ident_r = sb("ident_r", [P, P], fp32r)
        self.causal_r = sb("causal_r", [P, P], fp32r)
        self.head_gain = sb("head_gain", [P, 2])
        self.ps = ctx.enter_context(nc.psum_tensor("ps", [P, 8, 512], fp32))
        self.w = Weights(nc, ctx, schedule)
        self.out_stored = nc.alloc_semaphore("out_stored")
        self.sq = [sb(f"sq{i}", [P, SEQ]) for i in range(2)]
        self.sq_sum = sb("sq_sum", [P, SEQ])
        self.inv = sb("inv", [P, SEQ])
        self.mean, self.rms, self.inv_rms = (sb(n, [P, TT]) for n in ("mean", "rms", "inv_rms"))
        self.split_buf = [sb(f"split_buf{i}", [P, SEQ]) for i in range(2)]

    def gain(self, name, k):
        c = PARAM_COL[name] + k
        return self.params[:, c:c + 1]


class Sems:

    retired = []

    def __init__(self, nc, stage):
        self.nc, self.stage, self.made = nc, stage, {}

    def __getattr__(self, name):
        if name not in self.made:
            self.made[name] = self.nc.alloc_semaphore(f"{self.stage}_{name}")
        return self.made[name]

    def clear(self):
        mine = list(self.made.values())
        for sem in mine:
            self.nc.gpsimd.sem_clear(sem)
        for sem in Sems.retired:
            self.nc.release_semaphore(sem)
        Sems.retired[:] = mine


def products(pe, out, whi, wlo, k, cols, xhi, xlo, xk, start, stop):
    pe.matmul(out, whi[:, k, cols], xhi[:, xk, :], start=start, stop=False)
    pe.matmul(out, whi[:, k, cols], xlo[:, xk, :], start=False, stop=False)
    return pe.matmul(out, wlo[:, k, cols], xhi[:, xk, :], start=False, stop=stop)


def token_products(pe, out, whi, wlo, k, cols, xhi, xlo, xk, toks, start, stop):
    pe.matmul(out, xhi[:, xk, toks], whi[:, k, cols], start=start, stop=False)
    pe.matmul(out, xhi[:, xk, toks], wlo[:, k, cols], start=False, stop=False)
    return pe.matmul(out, xlo[:, xk, toks], whi[:, k, cols], start=False, stop=stop)


class InverseRms:

    def __init__(self, core, sums, features, toks):
        self.sums, self.bank = sums, 7
        self.core, self.features, self.toks, self.tiles = core, features, toks, toks // P

    def act(self, act, s):
        core, n = self.core, self.tiles
        act.preload_act_table_set("sqrt_and_others")
        act.wait_ge(s.mean_ready, 1)
        act.activation(core.rms[:, 0:n], core.mean[:, 0:n], ACT.Sqrt).then_inc(s.root_ready, 1)

    def pe(self, pe, s):
        core, sums = self.core, self.core.ps[:, self.bank, :]
        for t in range(self.tiles):
            mm = pe.matmul(sums[:, t:t + 1], self.sums[:, P * t:P * t + P], core.ones[:, 0:1], start=True, stop=True)
        mm.then_inc(s.summed, 1)
        pe.wait_ge(s.inv_rms_ready, 1)
        for t in range(self.tiles):
            mm = pe.matmul(sums[:, P * t:P * t + P], core.inv_rms[:, t:t + 1].to_broadcast([P, P]), core.ident[:, :],
                           start=True, stop=True)
        mm.then_inc(s.spread, 1)

    def dve(self, dve, s):
        core, n = self.core, self.tiles
        dve.wait_ge(s.summed, 1)
        dve.tensor_scalar(core.mean[:, 0:n], core.ps[:, self.bank, 0:n], 1.0 / self.features, EPS, ALU.mult, ALU.add)\
           .then_inc(s.mean_ready, 1)
        dve.wait_ge(s.root_ready, 1)
        dve.reciprocal(core.inv_rms[:, 0:n], core.rms[:, 0:n]).then_inc(s.inv_rms_ready, 1)
        dve.wait_ge(s.spread, 1)
        dve.tensor_copy(core.inv[:, 0:self.toks], core.ps[:, self.bank, 0:self.toks]).then_inc(s.inv_ready, 1)
        dve.wait_ge(s.inv_ready, 1)


class Norm:

    def __init__(self, core, src, gains, xhi, xlo, have, kt=DK, toks=SEQ):
        self.core, self.src, self.gains, self.xhi, self.xlo = core, src, gains, xhi, xlo
        self.have, self.kt, self.toks = have, kt, toks
        self.sums = core.inv if have == "nothing" else core.sq_sum
        self.inverse = InverseRms(core, self.sums, kt * P, toks)
        self.pool_helps = True

    def act_squares(self, act, s):
        core, n = self.core, self.toks
        if self.have == "nothing":
            for k in range(self.kt):
                if k >= 3:
                    act.wait_ge(s.norm_sq_added, k - 2)
                act.activation((core.sq[k % 2] if k else self.sums)[:, 0:n], self.src[:, k, 0:n], ACT.Square)\
                   .then_inc(s.norm_sq_made, 1)

    def act_root(self, act, s):
        if self.have != "inverse":
            self.inverse.act(act, s)

    def act_scale(self, act, s):
        core, n = self.core, self.toks
        for k in range(self.kt):
            act.wait_ge(s.scaled, k + 1)
            act.activation(self.xhi[:, k, 0:n], core.split_buf[k % 2][:, 0:n], ACT.Copy).then_inc(s.x_hi, 1)

    def pe_sum(self, pe, s):
        if self.have == "nothing":
            pe.wait_ge(s.norm_sq_added, self.kt - 1)
        if self.have != "inverse":
            self.inverse.pe(pe, s)

    def pe_wait(self, pe, s, k):
        if not self.pool_helps:
            pe.wait_ge(s.x_lo, k + 1)
        elif k % 2 == 0:
            pe.wait_ge(s.x_lo_even, k // 2 + 1)
        else:
            pe.wait_ge(s.x_lo_odd, k // 2 + 1)

    def dve(self, dve, s):
        core, n, tmp = self.core, self.toks, self.core.split_buf
        if self.have != "inverse":
            self.inverse.dve(dve, s)

        def low(k):
            dve.wait_ge(s.x_hi, k + 1)
            dve.tensor_tensor(self.xlo[:, k, 0:n], tmp[k % 2][:, 0:n], self.xhi[:, k, 0:n].bitcast(fp32), ALU.subtract)\
               .then_inc(s.x_lo_odd if self.pool_helps else s.x_lo, 1)

        for k in range(self.kt):
            if k >= 2:
                if not self.pool_helps:
                    dve.wait_ge(s.x_lo, k - 1)
                elif k % 2 == 0:
                    dve.wait_ge(s.x_lo_even, k // 2)
                else:
                    dve.wait_ge(s.x_lo_odd, k // 2)
            dve.scalar_tensor_tensor(out=tmp[k % 2][:, 0:n], in0=self.src[:, k, 0:n], scalar=self.gains(k),
                                     in1=core.inv[:, 0:n], op0=ALU.mult, op1=ALU.mult).then_inc(s.scaled, 1)
            if self.pool_helps and k % 2 == 1:
                low(k)
            if not self.pool_helps and k >= 1:
                low(k - 1)
        if not self.pool_helps:
            low(self.kt - 1)

    def pool(self, pool, s):
        core, n, tmp = self.core, self.toks, self.core.split_buf
        if self.have == "nothing":
            for k in range(1, self.kt):
                pool.wait_ge(s.norm_sq_made, k + 1)
                if k >= 2:
                    pool.wait_ge(s.norm_sq_added, k - 1)
                pool.tensor_tensor(self.sums[:, 0:n], self.sums[:, 0:n], core.sq[k % 2][:, 0:n], ALU.add)\
                    .then_inc(s.norm_sq_added, 1)
        for k in range(0, self.kt if self.pool_helps else 0, 2):
            pool.wait_ge(s.x_hi, k + 1)
            pool.tensor_tensor(self.xlo[:, k, 0:n], tmp[0][:, 0:n], self.xhi[:, k, 0:n].bitcast(fp32), ALU.subtract)\
                .then_inc(s.x_lo_even, 1)


class SquareSum:

    def __init__(self, core, tile, wait):
        self.core, self.tile, self.wait = core, tile, wait

    def act(self, act, s, t):
        core = self.core
        self.wait(act, s, t)
        if t >= 3:
            act.wait_ge(s.sq_added, t - 2)
        act.activation((core.sq[t % 2] if t else core.sq_sum)[:, :], self.tile(t), ACT.Square).then_inc(s.sq_made, 1)

    def pool(self, pool, s, t):
        core = self.core
        if t >= 1:
            pool.wait_ge(s.sq_made, t + 1)
            if t >= 2:
                pool.wait_ge(s.sq_added, t - 1)
            pool.tensor_tensor(core.sq_sum[:, :], core.sq_sum[:, :], core.sq[t % 2][:, :], ALU.add).then_inc(s.sq_added, 1)


def add_normed_stage(core, name, y, gains, square=True):
    nc, s = core.nc, Sems(core.nc, name)
    tmp, inverse = core.split_buf, InverseRms(core, core.sq_sum, D, SEQ)
    def add_square(pool, k):
        pool.wait_ge(s.sq_made, k + 1)
        if k >= 2:
            pool.wait_ge(s.sq_added, k - 1)
        pool.tensor_tensor(core.sq_sum[:, :], core.sq_sum[:, :], core.sq[k % 2][:, :], ALU.add).then_inc(s.sq_added, 1)

    with nc.Block() as block:
        @block.tensor
        def _(pe):
            inverse.pe(pe, s)

        @block.scalar
        def _(act):
            inverse.act(act, s)
            for k in range(DK if square else 0):
                if k % 2 == 0:
                    act.wait_ge(s.added_even, k // 2 + 1)
                else:
                    act.wait_ge(s.added_odd, k // 2 + 1)
                if k >= 3:
                    act.wait_ge(s.sq_added, k - 2)
                act.activation((core.sq[k % 2] if k else core.sq_sum)[:, :], core.h[:, k, :], ACT.Square)\
                   .then_inc(s.sq_made, 1)

        @block.vector
        def _(dve):
            inverse.dve(dve, s)
            for k in range(DK):
                if k >= 2:
                    if k % 2 == 0:
                        dve.wait_ge(s.added_even, k // 2)
                    else:
                        dve.wait_ge(s.added_odd, k // 2)
                dve.scalar_tensor_tensor(out=tmp[k % 2][:, :], in0=y[:, k, :], scalar=gains(k),
                                         in1=core.inv[:, :], op0=ALU.mult, op1=ALU.mult).then_inc(s.scaled, 1)
                if k % 2 == 1:
                    dve.wait_ge(s.scaled, k + 1)
                    dve.tensor_tensor(core.h[:, k, :], core.h[:, k, :], tmp[1][:, :], ALU.add).then_inc(s.added_odd, 1)

        @block.gpsimd
        def _(pool):
            for k in range(DK):
                if k % 2 == 0:
                    pool.wait_ge(s.scaled, k + 1)
                    pool.tensor_tensor(core.h[:, k, :], core.h[:, k, :], tmp[0][:, :], ALU.add).then_inc(s.added_even, 1)
                if square and k >= 2:
                    add_square(pool, k - 1)
            if square:
                add_square(pool, DK - 1)
    s.clear()


def linear_stage(core, name, tiles, xhi, xlo, act_tile=None, dve_tile=None, pool_tile=None, pe_after=None,
                 banks=4, bank_need=None, lead=1, norm=None, together=(0, 1), squares=None,
                 first=None, pe_ready=None):
    nc, s, ps, w = core.nc, Sems(core.nc, name), core.ps, core.w
    base = w.first[name]
    together = together if norm else ()
    second_first = not norm or any(part[0] == 1 for t in together for part in tiles[t])
    slabs = 1 + max(part[0] for parts in tiles for part in parts)
    if norm:
        norm.pool_helps = not second_first
    first_tile, released, parts_done = {}, {}, 0
    for t, parts in enumerate(tiles):
        for slab, *_ in parts:
            first_tile.setdefault(slab, t)
            if slab == parts[-1][0]:
                released[slab] = ("tile", t + 1)
            else:
                parts_done += 1
                released[slab] = ("part", parts_done)
    with nc.Block() as block:
        @block.sync
        def _(sp):
            if first:
                first.sp(sp, s)
            for n in range(base + 2, base + slabs + 2):
                w.load(sp, n)

        def split(eng, n):
            if eng is nc.scalar and n >= 2:
                kind, count = released[n - 2]
                eng.wait_ge(s.tile_done if kind == "tile" else s.part_done, count)
            (w.split_hi if eng is nc.scalar else w.split_lo)(eng, base + n)

        def due(n, t):
            if n > slabs or first_tile[n - 1] > t:
                return False
            kind, count = released[n - 2]
            return kind == "part" or count <= t

        @block.scalar
        def _(act):
            if norm:
                norm.act_squares(act, s)
            if second_first:
                split(act, 1)
            if norm:
                norm.act_root(act, s)
            if first:
                first.act(act, s)
            if norm:
                norm.act_scale(act, s)
            if not second_first:
                split(act, 1)
            done = 2
            for t in range(len(tiles)):
                while due(done, t):
                    split(act, done)
                    done += 1
                if act_tile:
                    act_tile(act, s, t)
                if squares:
                    squares.act(act, s, t)
            for n in range(done, slabs + 1):
                split(act, n)

        @block.gpsimd
        def _(pool):
            if first:
                first.pool(pool, s)
            if second_first:
                split(pool, 1)
            if norm:
                norm.pool(pool, s)
            if not second_first:
                split(pool, 1)
            done = 2
            for t in range(len(tiles)):
                while due(done, t):
                    split(pool, done)
                    done += 1
                if pool_tile:
                    pool_tile(pool, s, t)
                if squares:
                    squares.pool(pool, s, t)
            for n in range(done, slabs + 1):
                split(pool, n)

        @block.vector
        def _(dve):
            if norm:
                norm.dve(dve, s)
            for t in range(len(tiles)):
                if dve_tile:
                    dve_tile(dve, s, t)

        @block.tensor
        def _(pe):
            if norm:
                norm.pe_sum(pe, s)
            if first:
                first.pe(pe, s)
            if pe_ready:
                pe_ready(pe, s)
            taken = {}

            def step(t, part, k, xk, start, stop):
                slab, cols, _, toks, *own = part
                ahi, alo = own if own else (xhi, xlo)
                if slab not in taken:
                    taken[slab] = w.take(pe, base + slab)
                whi, wlo = taken[slab]
                width, bank = cols.stop - cols.start, t % banks
                if toks is None:
                    return products(pe, ps[0:width, bank, 0:ahi.shape[2]], whi, wlo, k, cols, ahi, alo, xk, start, stop)
                return token_products(pe, ps[:, bank, 0:width], whi, wlo, k, cols, ahi, alo, xk, toks, start, stop)

            def bank_wait(t):
                if t >= banks:
                    pe.wait_ge(s.bank_free, bank_need(t) if bank_need else t - banks + 1)

            for t, parts in enumerate(tiles):
                if t in together:
                    if t == together[-1]:
                        for k in range(DK):
                            norm.pe_wait(pe, s, k)
                            for u in together:
                                mm = step(u, tiles[u][0], k, k, k == 0, k == DK - 1)
                                if k == DK - 1:
                                    mm.then_inc(s.tile_done, 1)
                        if pe_after:
                            for u in together:
                                if u >= lead:
                                    pe_after(pe, s, u - lead)
                    continue
                bank_wait(t)
                total = sum(len(part[2]) for part in parts)
                m = 0
                for n, part in enumerate(parts):
                    for k, xk in part[2]:
                        mm = step(t, part, k, xk, m == 0, m == total - 1)
                        m += 1
                    mm.then_inc(s.tile_done if n == len(parts) - 1 else s.part_done, 1)
                if pe_after and t >= lead:
                    pe_after(pe, s, t - lead)
            if pe_after:
                for t in range(max(0, len(tiles) - lead), len(tiles)):
                    pe_after(pe, s, t)
    s.clear()


def feature_tiles(slab0, n_slabs, cols, kt, width=P):
    return [[(slab0 + j, slice(c, min(c + width, cols)), [(k, k) for k in range(kt)], None)]
            for j in range(n_slabs) for c in range(0, cols, width)]


def token_tiles(slab0, n_slabs, cols, kt, token_tiles_n=TT):
    return [[(slab0 + j, slice(0, cols), [(k, k) for k in range(kt)], slice(P * tt, P * tt + P))]
            for j in range(n_slabs) for tt in range(token_tiles_n)]



def setup_stage(core, ins):
    nc, s, ps = core.nc, Sems(core.nc, "setup"), core.ps
    n_tables = (PARAM_TOTAL + P - 1) // P
    with ExitStack() as ctx:
        rows = ctx.enter_context(nc.sbuf_tensor("setup_rows", [P, n_tables, P], fp32))
        xt = ctx.enter_context(nc.sbuf_tensor("setup_x", [P, TT, D], fp32))
        minus_from, minus_ones = (ctx.enter_context(nc.sbuf_tensor(f"setup_{n}", [P, P], fp32))
                                  for n in ("minus_from", "minus_ones"))

        def stores():
            for name, count in PARAM_ROWS:
                src = ins[name].flatten().rearrange("(r c) -> r c", c=P)
                assert src.shape[0] == count, (name, src.shape)
                done = 0
                while done < count:
                    at = PARAM_COL[name] + done
                    m = min(count - done, P - at % P)
                    yield src[done:done + m, :], at // P, at % P
                    done += m
        parts = list(stores())
        with nc.Block() as block:
            @block.sync
            def _(sp):
                core.w.load(sp, 0)
                core.w.load(sp, 1)
                sp.dma_start(xt[:, :, :], ins["x"][0].rearrange("(t p) d -> p t d", p=P)).then_inc(s.x_loaded, 16)
                for half in range(2):
                    for c, name in enumerate(("k_norm", "q_norm")):
                        sp.dma_start(core.head_gain[HD * half:HD * half + HD, c:c + 1],
                                     ins[name].flatten().rearrange("(p a) -> p a", a=1)).then_inc(s.gains_loaded, 16)

            @block.scalar
            def _(act):
                for src, table, p0 in parts:
                    act.dma_start(rows[p0:p0 + src.shape[0], table, :], src).then_inc(s.rows_loaded, 16)
                core.w.split_hi(act, 0)
                for t in range(TT):
                    for half in range(2):
                        n = 2 * t + half
                        act.wait_ge(s.x_turned, n + 1)
                        act.activation(core.h[:, 4 * half:4 * half + 4, P * t:P * t + P],
                                       ps[:, 1 + n % 4, :].rearrange("p (k c) -> p k c", k=4), ACT.Copy).then_inc(s.x_stored, 1)

            @block.gpsimd
            def _(pool):
                c = Chain(pool, s.pool_chain)
                c(pool.memset(core.ident[:, :], 0.0))
                c(pool.memset(core.head_ones[:, :], 0.0))
                c(pool.memset(core.ones[:, :], 1.0))
                c(pool.memset(minus_ones[:, :], -1.0))
                c.wait()
                c(pool.memset(core.head_ones[0:HD, 0:HD], 1.0))
                c.wait()
                c(pool.memset(core.head_ones[HD:P, HD:P], 1.0))
                c.wait()
                pick = lambda out, src, op, fill, sign, base=0: pool.affine_select(
                    out=out[:, :], in_=src[:, :], compare_op=op, fill=fill, base=base,
                    pattern=[[sign, P]], channel_multiplier=-sign)
                c(pick(core.upto, core.ones, ALU.is_ge, 0.0, 1))
                c(pick(core.after, core.ones, ALU.is_gt, 0.0, -1))
                c(pick(minus_from, minus_ones, ALU.is_ge, 0.0, -1))
                c.wait()
                pick(core.ident, core.ident, ALU.not_equal, 1.0, 1).then_inc(s.ident_ready, 1)
                core.w.split_lo(pool, 0)

            @block.vector
            def _(dve):
                for i in range(n_tables):
                    m = min(P, PARAM_TOTAL - i * P)
                    dve.wait_ge(s.rows_turned, i + 1)
                    dve.tensor_copy(core.params[:, i * P:i * P + m], ps[:, 0, 0:m]).then_inc(s.rows_stored, 1)
                dve.wait_ge(s.ident_ready, 1)
                dve.tensor_copy(core.ident_r[:, :], core.ident[:, :]).then_inc(s.rows_stored, 1)
                dve.tensor_copy(core.minus_from_r[:, :], minus_from[:, :]).then_inc(s.rows_stored, 1)
                dve.tensor_copy(core.minus_ones_r[:, :], minus_ones[:, :]).then_inc(s.rows_stored, 1)
                dve.tensor_scalar(core.causal_r[:, :], minus_from[:, :], 1e30, None, ALU.mult)\
                   .then_inc(s.rows_stored, 1)
                dve.wait_ge(s.gains_loaded, 64)
                dve.tensor_scalar(core.head_gain[:, 1:2], core.head_gain[:, 1:2], HD ** -0.5, None, ALU.mult)\
                   .then_inc(s.rows_stored, 1)

            @block.tensor
            def _(pe):
                pe.wait_ge(s.ident_ready, 1)
                pe.wait_ge(s.x_loaded, 16)
                for t in range(TT):
                    for half in range(2):
                        n = 2 * t + half
                        if n >= 4:
                            pe.wait_ge(s.x_stored, n - 3)
                        for k in range(4):
                            mm = pe.transpose(ps[:, 1 + n % 4, P * k:P * k + P],
                                              xt[:, t, P * (4 * half + k):P * (4 * half + k) + P], core.ident[:, :])
                        mm.then_inc(s.x_turned, 1)
                pe.wait_ge(s.rows_loaded, 16 * len(parts))
                for i in range(n_tables):
                    m = min(P, PARAM_TOTAL - i * P)
                    if i >= 1:
                        pe.wait_ge(s.rows_stored, i)
                    pe.transpose(ps[:, 0, 0:m], rows[0:m, i, :], core.ident[0:m, 0:m]).then_inc(s.rows_turned, 1)
        s.clear()


def output_stage(core, out):
    nc, s, ps = core.nc, Sems(core.nc, "output"), core.ps
    with nc.sbuf_tensor("output_y", [P, TT, D], fp32) as y, nc.Block() as block:
        @block.tensor
        def _(pe):
            for t in range(TT):
                for half in range(2):
                    n = 2 * t + half
                    if n >= 4:
                        pe.wait_ge(s.copied, n - 3)
                    for k in range(4):
                        mm = pe.transpose(ps[:, n % 4, P * k:P * k + P],
                                          core.h[:, 4 * half + k, P * t:P * t + P], core.ident[:, :])
                    mm.then_inc(s.turned, 1)

        @block.vector
        def _(dve):
            for t in range(TT):
                for half in range(2):
                    n = 2 * t + half
                    dve.wait_ge(s.turned, n + 1)
                    dve.tensor_copy(y[:, t, 512 * half:512 * half + 512], ps[:, n % 4, :]).then_inc(s.copied, 1)

        @block.sync
        def _(sp):
            for t in range(TT):
                sp.wait_ge(s.copied, 2 * t + 2)
                sp.dma_start(out[0, P * t:P * t + P, :], y[:, t, :]).then_inc(core.out_stored, 16)
            sp.wait_ge(core.out_stored, 16 * TT)
    s.clear()


def residual_tile(core, banks=4):
    def step(dve, s, t):
        dve.wait_ge(s.tile_done, t + 1)
        dve.tensor_tensor(core.h[:, t, :], core.h[:, t, :], core.ps[:, t % banks, :], ALU.add).then_inc(s.bank_free, 1)
    return step


def residual_squares(core):
    return SquareSum(core, lambda t: core.h[:, t, :], lambda act, s, t: act.wait_ge(s.bank_free, t + 1))


def stored_squares(core, y):
    return SquareSum(core, lambda t: y[:, t, :], lambda act, s, t: act.wait_ge(s.bank_free, t + 1))


def store_tile(core, dst, banks=4):
    def step(dve, s, t):
        dve.wait_ge(s.tile_done, t + 1)
        dve.tensor_copy(dst(t), core.ps[:, t % banks, 0:dst(t).free_size()]).then_inc(s.bank_free, 1)
    return step



def mamba_in_stages(core, ins, z, xs, bc, dt_raw):
    nc, ps, w = core.nc, core.ps, core.w
    with ExitStack() as ctx:
        xhi = ctx.enter_context(nc.sbuf_tensor("mi_xhi", [P, DK, SEQ], fp32r))
        xlo = ctx.enter_context(nc.sbuf_tensor("mi_xlo", [P, DK, SEQ], fp32r))
        norm = Norm(core, core.h, lambda k: core.gain("m_norm", k), xhi, xlo, "nothing")

        def z_act(act, s, t):
            j, tt = t // TT, t % TT
            act.wait_ge(s.tile_done, t + 1)
            act.activation(z[:, tt, 256 * j:256 * j + 256], ps[:, t % 4, 0:256], ACT.Silu).then_inc(s.bank_free, 1)
        linear_stage(core, "mz", token_tiles(0, 8, 256, DK), xhi, xlo, act_tile=z_act, norm=norm)

        def dt_dve(dve, s, t):
            dve.wait_ge(s.tile_done, t + 1)
            dve.tensor_copy(dt_raw[:, HEADS * t:HEADS * t + HEADS], ps[:, t % 4, 0:HEADS]).then_inc(s.bank_free, 1)
        linear_stage(core, "mdt", token_tiles(0, 1, HEADS, DK), xhi, xlo,
                     dve_tile=dt_dve)

        conv = ctx.enter_context(nc.sbuf_tensor("mi_conv", [P, 2, SEQ], fp32))
        act_x = ctx.enter_context(nc.sbuf_tensor("mi_actx", [P, 2, SEQ], fp32))

        def conv_dve(dve, s, t):
            c = Chain(dve, s.conv_chain)
            c.n = 3 * t
            bank, acc = t % 4, conv[:, t % 2, :]
            tap = lambda j: core.gain("m_conv_w", j * CONV_TILES + t)
            dve.wait_ge(s.tile_done, t + 1)
            if t >= 2:
                dve.wait_ge(s.silu_done, t - 1)
            c(dve.tensor_scalar(acc, ps[:, bank, :], tap(3), core.gain("m_conv_b", t), ALU.mult, ALU.add))
            for back in (1, 2, 3):
                c.wait()
                i = dve.scalar_tensor_tensor(out=acc[:, back:SEQ], in0=ps[:, bank, 0:SEQ - back], scalar=tap(3 - back),
                                             in1=acc[:, back:SEQ], op0=ALU.mult, op1=ALU.add)
                if back < 3:
                    c(i)
                else:
                    i.then_inc(s.bank_free, 1)
            if 1 <= t <= 16:
                store_x(dve, s, t - 1)

        def store_x(dve, s, t):
            dve.wait_ge(s.x_turned, t + 1)
            dve.tensor_copy(xs[:, :, P * t:P * t + P], ps[:, 4 + t % 2, :].rearrange("p (c f) -> p c f", c=TT))\
               .then_inc(s.x_stored, 1)

        def silu_act(act, s, t):
            act.wait_ge(s.bank_free, t + 1)
            if t < 16:
                if t >= 2:
                    act.wait_ge(s.x_turned, t - 1)
                act.activation(act_x[:, t % 2, :], conv[:, t % 2, :], ACT.Silu).then_inc(s.silu_done, 1)
            else:
                act.activation(bc[:, t - 16, :], conv[:, t % 2, :], ACT.Silu).then_inc(s.silu_done, 1)

        def turn_pe(pe, s, t):
            if t >= 16:
                return
            pe.wait_ge(s.silu_done, t + 1)
            if t >= 2:
                pe.wait_ge(s.x_stored, t - 1)
            for c in range(TT):
                mm = pe.transpose(ps[:, 4 + t % 2, P * c:P * c + P], act_x[:, t % 2, P * c:P * c + P], core.ident[:, :])
            mm.then_inc(s.x_turned, 1)
        linear_stage(core, "mx", feature_tiles(0, 12, 256, DK),
                     xhi, xlo, act_tile=silu_act, dve_tile=conv_dve, pe_after=turn_pe)


def dt_stage(core, ins, dt_raw, dt, da, e_from_start, e_to_end, e_chunk, d_skip):
    nc, s, ps = core.nc, Sems(core.nc, "dt"), core.ps
    with ExitStack() as ctx:
        sb = lambda n: ctx.enter_context(nc.sbuf_tensor(f"dt_{n}", [P, P], fp32))
        bias, a_log, x, e, u, ln, t1, rest = (sb(n) for n in ("bias", "a_log", "x", "e", "u", "ln", "t1", "rest"))
        chunks = lambda a: a[:, :].rearrange("p (c h) -> p c h", c=TT)
        every = lambda a: a[:, 0:HEADS].unsqueeze(1).to_broadcast([P, TT, HEADS])
        with nc.Block() as block:
            @block.sync
            def _(sp):
                for dst, name in ((bias, "m_dt_bias"), (a_log, "m_A_log"), (d_skip, "m_D")):
                    sp.dma_start(dst[:, 0:HEADS], ins[name][0].partition_broadcast(P)).then_inc(s.loaded, 16)

            @block.vector
            def _(dve):
                c = Chain(dve, s.chain)
                dve.wait_ge(s.loaded, 48)
                c(dve.tensor_tensor(chunks(x), chunks(dt_raw), every(bias), ALU.add))
                c.wait()
                dve.scalar_tensor_tensor(out=t1[:, :], in0=x[:, :], scalar=-1.0, in1=x[:, :], op0=ALU.mult, op1=ALU.min)\
                   .then_inc(s.neg_abs, 1)
                dve.wait_ge(s.exp_done, 1)
                c(dve.tensor_scalar(u[:, :], e[:, :], 1.0, None, ALU.add))
                c.wait()
                c(dve.tensor_scalar(rest[:, :], u[:, :], -1.0, None, ALU.add))
                c.wait()
                c(dve.tensor_tensor(rest[:, :], e[:, :], rest[:, :], ALU.subtract))
                c(dve.reciprocal(t1[:, :], u[:, :]))
                c.wait()
                c(dve.tensor_tensor(rest[:, :], rest[:, :], t1[:, :], ALU.mult))
                c.wait()
                dve.wait_ge(s.ln_done, 1)
                c(dve.tensor_tensor(rest[:, :], rest[:, :], ln[:, :], ALU.add))
                c.wait()
                c(dve.scalar_tensor_tensor(out=dt[:, :], in0=x[:, :], scalar=0.0, in1=rest[:, :],
                                           op0=ALU.max, op1=ALU.add))
                c.wait()
                dve.wait_ge(s.a_done, 1)
                c(dve.tensor_tensor(chunks(da), chunks(dt), every(a_log), ALU.mult))
                c.wait()
                dve.tensor_scalar(da[:, :], da[:, :], -1.0, None, ALU.mult).then_inc(s.da_ready, 1)
                dve.wait_ge(s.sums_done, 2)
                c(dve.tensor_copy(t1[:, :], ps[:, 0, 0:P]))
                c.wait()
                dve.tensor_tensor(rest[:, :], ps[:, 1, 0:P], t1[:, :], ALU.subtract).then_inc(s.to_end, 1)

            @block.scalar
            def _(act):
                act.wait_ge(s.neg_abs, 1)
                act.activation(e[:, :], t1[:, :], ACT.Exp).then_inc(s.exp_done, 1)
                act.activation(a_log[:, 0:HEADS], a_log[:, 0:HEADS], ACT.Exp).then_inc(s.a_done, 1)
                act.wait_ge(s.exp_done, 1)
                act.activation(ln[:, :], e[:, :], ACT.Ln, bias=1.0).then_inc(s.ln_done, 1)
                act.wait_ge(s.to_end, 1)
                act.activation(e_from_start[:, :], ps[:, 0, 0:P], ACT.Exp).then_inc(s.exp_done, 1)
                act.activation(e_chunk[:, :], ps[:, 1, 0:P], ACT.Exp).then_inc(s.exp_done, 1)
                act.activation(e_to_end[:, :], rest[:, :], ACT.Exp).then_inc(s.exp_done, 1)

            @block.tensor
            def _(pe):
                pe.wait_ge(s.da_ready, 1)
                pe.matmul(ps[:, 0, 0:P], core.upto[:, :], da[:, :], start=True, stop=True).then_inc(s.sums_done, 1)
                pe.matmul(ps[:, 1, 0:P], core.ones[:, :], da[:, :], start=True, stop=True).then_inc(s.sums_done, 1)
        s.clear()


def scan_stage(core, z, xs, bc, dt, da, e_from_start, e_to_end, e_chunk, d_skip, square_sums):
    nc, s, ps = core.nc, Sems(core.nc, "scan"), core.ps
    GW = HG * HD
    with ExitStack() as ctx:
        sb = lambda n, sh: ctx.enter_context(nc.sbuf_tensor(f"scan_{n}", sh, fp32))
        b_tok = sb("b_tok", [P, TT - 1, GROUPS, P])
        state = sb("state", [P, GROUPS, GW])
        steps, mix = sb("steps", [P, 2, HG, P]), sb("mix", [P, 3, HG, P])
        cb = sb("cb", [P, GROUPS, P])
        inter, both, junk = sb("inter", [P, GW]), sb("both", [P, GW]), sb("junk", [P, GW])
        xdt, xend, skip = core.sq, core.split_buf, (core.sq_sum, core.inv)
        units = [(c, g) for c in range(TT) for g in range(GROUPS)]
        U, grown_units = len(units), GROUPS * (TT - 1)
        heads = lambda a: a.rearrange("p (h d) -> p h d", h=HG)
        per_head = lambda a, c, g, width=HD: a[:, HEADS * c + HG * g:HEADS * c + HG * g + HG].unsqueeze(2)\
            .to_broadcast([P, HG, width])
        tok = lambda c: slice(P * c, P * c + P)
        grp = lambda g: slice(GW * g, GW * g + GW)
        sums_bank = lambda u: 1 if u % 2 == 0 else 6

        with nc.Block() as block:
            @block.gpsimd
            def _(pool):
                for u in range(U + 1):
                    if u < U:
                        c, g = units[u]
                        if u >= 2:
                            pool.wait_ge(s.sums_done, u - 1)
                        pool.tensor_tensor(steps[:, u % 2, :, :], core.upto[:, :].unsqueeze(1).to_broadcast([P, HG, P]),
                                           per_head(da, c, g, P), ALU.mult).then_inc(s.steps_ready, 1)
                    if 1 <= u <= grown_units:
                        c, g = units[u - 1]
                        pool.wait_ge(s.xdt_ready, u)
                        if u >= 3:
                            pool.wait_ge(s.grown, u - 2)
                        pool.tensor_tensor(heads(xend[(u - 1) % 2][:, :]), heads(xdt[(u - 1) % 2][:, :]),
                                           per_head(e_to_end, c, g), ALU.mult).then_inc(s.xend_ready, 1)
                    if u >= 1:
                        c, g = units[u - 1]
                        if u >= 3:
                            pool.wait_ge(s.skip_used, u - 2)
                        pool.tensor_tensor(heads(skip[(u - 1) % 2][:, :]), heads(xs[:, c, grp(g)]),
                                           d_skip[:, HG * g:HG * g + HG].unsqueeze(2).to_broadcast([P, HG, HD]), ALU.mult)\
                            .then_inc(s.skip_ready, 1)

            @block.scalar
            def _(act):
                for c in range(TT - 1):
                    act.wait_ge(s.b_turned, c + 1)
                    act.activation(b_tok[:, c, :, :].rearrange("p g n -> p (g n)"), ps[:, 3 + c, :], ACT.Copy)\
                       .then_inc(s.b_stored, 1)

                def square(u):
                    c, g = units[u]
                    act.wait_ge(s.y_ready, u + 1)
                    if u >= 1:
                        act.wait_ge(s.squared, u)
                    act.activation(junk[:, :], z[:, c, grp(g)], ACT.Square,
                                   accum_out=square_sums[:, g * TT + c:g * TT + c + 1]).then_inc(s.squared, 1)
                for u in range(U):
                    act.wait_ge(s.sums_done, u + 1)
                    if u >= 3:
                        act.wait_ge(s.intra_done, u - 2)
                    b = sums_bank(u)
                    act.activation(mix[:, u % 3, :, :].rearrange("p h l -> p (h l)"),
                                   ps[:, b:b + 2, :].rearrange("p b l -> p (b l)"), ACT.Exp).then_inc(s.decay_ready, 1)
                    if u >= 3:
                        square(u - 3)
                for u in range(U - 3, U):
                    square(u)

            @block.vector
            def _(dve):
                c_ = Chain(dve, s.dve_chain)

                def begin(u):
                    c, g = units[u]
                    if g == 0:
                        dve.wait_ge(s.cb_done, c + 1)
                        if u >= 1:
                            dve.wait_ge(s.mix_ready, u)
                        dve.tensor_tensor(cb[:, :, :], ps[:, 0, :].rearrange("p (g l) -> p g l", g=GROUPS),
                                          core.upto[:, :].unsqueeze(1).to_broadcast([P, GROUPS, P]), ALU.mult)\
                           .then_inc(s.cb_masked, 1)
                    if u >= 2:
                        dve.wait_ge(s.intra_done, u - 1)
                        dve.wait_ge(s.xend_ready, min(u - 1, grown_units))
                    dve.tensor_tensor(heads(xdt[u % 2][:, :]), heads(xs[:, c, grp(g)]), per_head(dt, c, g), ALU.mult)\
                       .then_inc(s.xdt_ready, 1)
                    dve.wait_ge(s.cb_masked, c + 1)
                    dve.wait_ge(s.decay_ready, u + 1)
                    dve.tensor_tensor(mix[:, u % 3, :, :], mix[:, u % 3, :, :],
                                      cb[:, g, :].unsqueeze(1).to_broadcast([P, HG, P]),
                                      ALU.mult).then_inc(s.mix_ready, 1)

                def end(u):
                    c, g = units[u]
                    if c > 0:
                        dve.wait_ge(s.inter_done, u - 3)
                        if u >= 1:
                            dve.wait_ge(s.skip_used, u)
                        c_(dve.tensor_tensor(heads(inter[:, :]), heads(ps[:, 4, :]), per_head(e_from_start, c, g), ALU.mult))
                        dve.wait_ge(s.skip_ready, u + 1)
                        c_.wait()
                        c_(dve.tensor_tensor(inter[:, :], inter[:, :], skip[u % 2][:, :], ALU.add))
                        c_.wait()
                        rest = inter
                    else:
                        dve.wait_ge(s.skip_ready, u + 1)
                        rest = skip[u % 2]
                    dve.wait_ge(s.intra_done, u + 1)
                    if u >= 1:
                        dve.wait_ge(s.y_ready, u)
                    dve.tensor_tensor(both[:, :], ps[:, 3, :], rest[:, :], ALU.add).then_inc(s.skip_used, 1)
                    if c < TT - 1:
                        dve.wait_ge(s.grown, u + 1)
                        if c == 0:
                            dve.tensor_copy(state[:, g, :], ps[:, 5, :]).then_inc(s.state_ready, 1)
                        else:
                            c_(dve.tensor_tensor(heads(state[:, g, :]), heads(state[:, g, :]),
                                                 per_head(e_chunk, c, g), ALU.mult))
                            c_.wait()
                            dve.tensor_tensor(state[:, g, :], state[:, g, :], ps[:, 5, :], ALU.add)\
                               .then_inc(s.state_ready, 1)
                    dve.wait_ge(s.skip_used, u + 1)
                    dve.tensor_tensor(z[:, c, grp(g)], both[:, :], z[:, c, grp(g)], ALU.mult).then_inc(s.y_ready, 1)

                begin(0)
                for u in range(U):
                    if u + 1 < U:
                        begin(u + 1)
                    end(u)

            @block.tensor
            def _(pe):
                for c in range(TT - 1):
                    for g in range(GROUPS):
                        mm = pe.transpose(ps[:, 3 + c, P * g:P * g + P], bc[:, g, tok(c)], core.ident[:, :])
                    mm.then_inc(s.b_turned, 1)

                def front(u):
                    c, g = units[u]
                    if g == 0:
                        if c >= 1:
                            pe.wait_ge(s.cb_masked, c)
                        for i in range(GROUPS):
                            mm = pe.matmul(ps[:, 0, P * i:P * i + P], bc[:, i, tok(c)], bc[:, GROUPS + i, tok(c)],
                                           start=True, stop=True)
                        mm.then_inc(s.cb_done, 1)
                    pe.wait_ge(s.steps_ready, u + 1)
                    if u >= 2:
                        pe.wait_ge(s.decay_ready, u - 1)
                    for half in range(2):
                        mm = pe.matmul(ps[:, sums_bank(u) + half, :], core.after[:, :],
                                       steps[:, u % 2, 4 * half:4 * half + 4, :].rearrange("p h l -> p (h l)"),
                                       start=True, stop=True)
                    mm.then_inc(s.sums_done, 1)

                front(0)
                pe.wait_ge(s.b_stored, TT - 1)
                front(1)
                for u, (c, g) in enumerate(units):
                    if u + 2 < U:
                        front(u + 2)
                    if c > 0:
                        pe.wait_ge(s.state_ready, 4 * (c - 1) + g + 1)
                        pe.wait_ge(s.skip_used, u)
                        pe.matmul(ps[:, 4, :], bc[:, GROUPS + g, tok(c)], state[:, g, :], start=True, stop=True)\
                          .then_inc(s.inter_done, 1)
                    pe.wait_ge(s.mix_ready, u + 1)
                    if u >= 1:
                        pe.wait_ge(s.skip_used, u)
                    for h in range(HG):
                        mm = pe.matmul(ps[:, 3, HD * h:HD * h + HD], mix[:, u % 3, h, :],
                                       xdt[u % 2][:, HD * h:HD * h + HD], start=True, stop=True)
                    mm.then_inc(s.intra_done, 1)
                    if c < TT - 1:
                        pe.wait_ge(s.xend_ready, u + 1)
                        if u >= 1:
                            pe.wait_ge(s.state_ready, u)
                        pe.matmul(ps[:, 5, :], b_tok[:, c, g, :], xend[u % 2][:, :], start=True, stop=True)\
                          .then_inc(s.grown, 1)
        s.clear()


def y_norm_stage(core, y, total, yhi, ylo):
    nc, s, ps = core.nc, Sems(core.nc, "ynorm"), core.ps
    GW = HG * HD
    FT = D_INNER // P
    with ExitStack() as ctx:
        sb = lambda n, sh: ctx.enter_context(nc.sbuf_tensor(f"ynorm_{n}", sh, fp32))
        root, inv = sb("root", [P, TT * GROUPS]), sb("inv", [P, TT * GROUPS])
        tmp = core.split_buf
        with nc.Block() as block:
            @block.scalar
            def _(act):
                act.wait_ge(s.mean_ready, 1)
                act.activation(root[:, :], total[:, :], ACT.Sqrt).then_inc(s.root_ready, 1)
                for f in range(FT):
                    act.wait_ge(s.gained, f + 1)
                    act.activation(yhi[:, f, :], tmp[f % 2][:, :], ACT.Copy).then_inc(s.hi_done, 1)

            @block.vector
            def _(dve):
                dve.tensor_scalar(total[:, :], total[:, :], 1.0 / GW, EPS, ALU.mult, ALU.add).then_inc(s.mean_ready, 1)
                dve.wait_ge(s.root_ready, 1)
                dve.reciprocal(inv[:, :], root[:, :]).then_inc(s.inv_ready, 1)
                dve.wait_ge(s.inv_ready, 1)

                def scale(g):
                    for c in range(TT):
                        n = g * TT + c
                        dve.tensor_scalar(y[:, c, GW * g:GW * g + GW], y[:, c, GW * g:GW * g + GW],
                                          inv[:, n:n + 1], None, ALU.mult).then_inc(s.scaled, 1)
                scale(0)
                for f in range(FT):
                    if f % 4 == 0 and f // 4 + 1 < GROUPS:
                        scale(f // 4 + 1)
                    dve.wait_ge(s.turned, f + 1)
                    if f >= 2:
                        dve.wait_ge(s.lo_done, f - 1)
                    dve.tensor_scalar(tmp[f % 2][:, :], ps[:, f % 4, :], core.gain("m_ynorm", f), None, ALU.mult)\
                       .then_inc(s.gained, 1)

            @block.gpsimd
            def _(pool):
                for f in range(FT):
                    pool.wait_ge(s.hi_done, f + 1)
                    pool.tensor_tensor(ylo[:, f, :], tmp[f % 2][:, :], yhi[:, f, :].bitcast(fp32), ALU.subtract)\
                        .then_inc(s.lo_done, 1)

            @block.tensor
            def _(pe):
                for f in range(FT):
                    pe.wait_ge(s.scaled, TT * (f // 4 + 1))
                    if f >= 4:
                        pe.wait_ge(s.gained, f - 3)
                    for c in range(TT):
                        mm = pe.transpose(ps[:, f % 4, P * c:P * c + P], y[:, c, P * f:P * f + P], core.ident[:, :])
                    mm.then_inc(s.turned, 1)
        s.clear()


def mamba(core, ins):
    nc = core.nc
    with ExitStack() as ctx:
        z = ctx.enter_context(nc.sbuf_tensor("mamba_z", [P, TT, D_INNER], fp32))
        sums = ctx.enter_context(nc.sbuf_tensor("mamba_sums", [P, TT * GROUPS], fp32))
        with ExitStack() as inner:
            sb = lambda n, sh: inner.enter_context(nc.sbuf_tensor(f"mamba_{n}", sh, fp32))
            xs = sb("xs", [P, TT, D_INNER])
            bc = sb("bc", [P, 2 * GROUPS, SEQ])
            dt_raw, dt, da, e1, e2, e3 = (sb(n, [P, P]) for n in ("dt_raw", "dt", "da", "e_start", "e_end", "e_chunk"))
            d_skip = sb("d_skip", [P, HEADS])
            mamba_in_stages(core, ins, z, xs, bc, dt_raw)
            dt_stage(core, ins, dt_raw, dt, da, e1, e2, e3, d_skip)
            scan_stage(core, z, xs, bc, dt, da, e1, e2, e3, d_skip, sums)
        yhi = ctx.enter_context(nc.sbuf_tensor("mamba_yhi", [P, 16, SEQ], fp32r))
        ylo = ctx.enter_context(nc.sbuf_tensor("mamba_ylo", [P, 16, SEQ], fp32r))
        y_norm_stage(core, z, sums, yhi, ylo)
        linear_stage(core, "mout", feature_tiles(0, DK, P, 16), yhi, ylo,
                     dve_tile=residual_tile(core), squares=residual_squares(core))



class TurnEmbedding:

    def __init__(self, core, p, p_tok, tmp, xhi, xlo):
        self.core, self.p, self.p_tok, self.tmp, self.xhi, self.xlo = core, p, p_tok, tmp, xhi, xlo

    def sp(self, sp, s):
        sp.dma_start(self.p_tok[:, :, :], self.p.rearrange("(t p) d -> p t d", p=P)).then_inc(s.p_loaded, 16)

    def pe(self, pe, s):
        pe.wait_ge(s.p_loaded, 16)
        for k in range(2):
            for t in range(TT):
                mm = pe.transpose(self.core.ps[:, k, P * t:P * t + P], self.p_tok[:, t, P * k:P * k + P],
                                  self.core.ident[:, :])
            mm.then_inc(s.p_turned, 1)

    def act(self, act, s):
        for k in range(2):
            act.wait_ge(s.p_turned, k + 1)
            act.activation(self.tmp[:, k, :], self.core.ps[:, k, :], ACT.Copy).then_inc(s.p_copied, 1)
        for k in range(2):
            act.wait_ge(s.p_copied, k + 1)
            act.activation(self.xhi[:, DK + k, :], self.tmp[:, k, :], ACT.Copy).then_inc(s.p_high, 1)

    def pool(self, pool, s):
        for k in range(2):
            pool.wait_ge(s.p_high, k + 1)
            pool.tensor_tensor(self.xlo[:, DK + k, :], self.tmp[:, k, :], self.xhi[:, DK + k, :].bitcast(fp32),
                               ALU.subtract).then_inc(s.p_low, 1)


def ple_stages(core, ins, i):
    nc, ps = core.nc, core.ps
    with ExitStack() as ctx:
        sb = lambda n, sh, d=fp32: ctx.enter_context(nc.sbuf_tensor(f"ple{i}_{n}", sh, d))
        xhi, xlo = sb("xhi", [P, DK + 2, SEQ], fp32r), sb("xlo", [P, DK + 2, SEQ], fp32r)
        p_tok, sig, prod = sb("p", [P, TT, 2 * P]), sb("sig", [P, 2, SEQ]), sb("prod", [P, 2, SEQ])
        norm = Norm(core, core.h, lambda k: core.gain("ple_norm", i * DK + k), xhi, xlo, "sum")

        add = lambda dve, f, prod: dve.tensor_tensor(core.h[:, f, :], core.h[:, f, :], prod, ALU.add)
        squares = SquareSum(core, lambda f: core.h[:, f, :], lambda act, s, f: act.wait_ge(s.added, f + 1))
        gated_stage(core, f"ple{i}", [(0, DK), (1, DK + 1)], xhi, xlo, xhi, xlo, sig, prod, None, add, norm, squares,
                    first=TurnEmbedding(core, ins["p"][i, 0], p_tok, sig, xhi, xlo))


def gated_slabs(w_proj, w_gate, g0):
    return [a for c in (0, 512) for a in slabs_of(w_proj, 512, c, c + 512) + slabs_of(w_gate, 256, g0 + c, g0 + c + 512)]


def gated_stage(core, name, proj_ks, phi, plo, xhi, xlo, sig, prod, gate_bias, finish, norm=None, squares=None,
                first=None):
    ps = core.ps
    tiles, order = [], []
    for half in range(2):
        for n in range(4):
            order.append(("proj", 4 * half + n))
            tiles.append([(3 * half, slice(P * n, P * n + P), proj_ks, None, phi, plo)])
        for n in range(4):
            order.append(("gate", 4 * half + n))
            tiles.append([(3 * half + 1 + n // 2, slice(P * (n % 2), P * (n % 2) + P), [(k, k) for k in range(DK)], None)])

    def sig_act(act, s, t):
        kind, f = order[t]
        if kind == "gate":
            act.wait_ge(s.tile_done, t + 1)
            if f >= 2:
                act.wait_ge(s.bank_free, f - 1)
            act.activation(sig[:, f % 2, :], ps[:, t % 8, :], ACT.Sigmoid,
                           bias=gate_bias(f) if gate_bias else 0.0).then_inc(s.sig_done, 1)
            if squares and f >= 1:
                squares.act(act, s, f - 1)
            if squares and f == DK - 1:
                squares.act(act, s, f)

    def wait_embedding(pe, s):
        pe.wait_ge(s.p_low, 2)

    def sq_pool(pool, s, t):
        kind, f = order[t]
        if squares and kind == "gate" and f >= 1:
            squares.pool(pool, s, f - 1)
        if squares and kind == "gate" and f == DK - 1:
            squares.pool(pool, s, f)

    def add_dve(dve, s, t):
        kind, f = order[t]
        if kind == "proj":
            return
        dve.wait_ge(s.sig_done, f + 1)
        if f >= 2:
            dve.wait_ge(s.added, f - 1)
        dve.tensor_tensor(prod[:, f % 2, :], ps[:, (t - 4) % 8, :], sig[:, f % 2, :], ALU.mult).then_inc(s.bank_free, 1)
        dve.wait_ge(s.bank_free, f + 1)
        finish(dve, f, prod[:, f % 2, :]).then_inc(s.added, 1)
    linear_stage(core, name, tiles, xhi, xlo, act_tile=sig_act, dve_tile=add_dve, pool_tile=sq_pool, banks=8, norm=norm,
                 bank_need=lambda t: t % 4 + 1, together=(4, 5),
                 first=first, pe_ready=wait_embedding if first else None)



def head_norm_steps(core, name, dst, gain_col, sq, root, inv, banks=6):
    ps = core.ps

    def act_step(act, s, t):
        act.wait_ge(s.tile_done, t + 1)
        if t >= 2:
            act.wait_ge(s.sq_summed, t - 1)
        act.activation(sq[:, t % 2, :], ps[:, t % banks, :], ACT.Square).then_inc(s.head_sq_ready, 1)
        if t >= 1:
            act_root(act, s, t - 1)

    def act_root(act, s, t):
        act.wait_ge(s.head_mean_ready, t + 1)
        act.activation(root[:, t % 2, :], inv[:, t % 2, :], ACT.Sqrt).then_inc(s.head_root_ready, 1)

    def pe_sum(pe, s, t):
        pe.wait_ge(s.head_sq_ready, t + 1)
        if t >= 2:
            pe.wait_ge(s.head_mean_ready, t - 1)
        pe.matmul(ps[:, 6 + t % 2, :], core.head_ones[:, :], sq[:, t % 2, :], start=True, stop=True)\
          .then_inc(s.sq_summed, 1)

    def dve_step(dve, s, t):
        if t >= 1:
            dve_finish(dve, s, t - 1)

    def dve_mean(dve, s, t):
        dve.wait_ge(s.sq_summed, t + 1)
        if t >= 2:
            dve.wait_ge(s.bank_free, t - 1)
        dve.tensor_scalar(inv[:, t % 2, :], ps[:, 6 + t % 2, :], 1.0 / HD, EPS, ALU.mult, ALU.add).then_inc(s.head_mean_ready, 1)

    def dve_finish(dve, s, t):
        dve_mean(dve, s, t)
        dve.wait_ge(s.head_root_ready, t + 1)
        dve.reciprocal(inv[:, t % 2, :], root[:, t % 2, :]).then_inc(s.head_inv_ready, 1)
        dve.wait_ge(s.head_inv_ready, t + 1)
        dve.scalar_tensor_tensor(out=dst[:, t, :], in0=ps[:, t % banks, :], scalar=core.head_gain[:, gain_col:gain_col + 1],
                                 in1=inv[:, t % 2, :], op0=ALU.mult, op1=ALU.mult).then_inc(s.bank_free, 1)
    return act_step, act_root, pe_sum, dve_step, dve_finish


def head_norm_linear(core, name, dst, gain_col, xhi, xlo, norm):
    nc = core.nc
    with ExitStack() as ctx:
        sb = lambda n: ctx.enter_context(nc.sbuf_tensor(f"{name}_{n}", [P, 2, SEQ], fp32))
        sq, root, inv = sb("sq"), sb("root"), sb("inv")
        a, a_root, pe_sum, d, d_fin = head_norm_steps(core, name, dst, gain_col, sq, root, inv)

        def act_tile(act, s, t):
            a(act, s, t)
            if t == DK - 1:
                a_root(act, s, t)

        def dve_tile(dve, s, t):
            d(dve, s, t)
            if t == DK - 1:
                d_fin(dve, s, t)
        linear_stage(core, name, feature_tiles(0, 4, 256, DK), xhi, xlo, norm=norm, banks=6,
                     act_tile=act_tile, dve_tile=dve_tile, pe_after=pe_sum)


SB_OFF = [0, 512, 896 + 128, 896]
SB_W = [SEQ - P * i for i in range(TT)]
SB_ALL = sum(SB_W)


def stick_attention_stage(core, qf, kf, v, gate):
    nc, s, ps = core.nc, Sems(core.nc, "stick"), core.ps
    HN = D // HD
    with ExitStack() as ctx:
        sb = lambda n, sh: ctx.enter_context(nc.sbuf_tensor(f"stick_{n}", sh, fp32))
        ex, wt = sb("ex", [P, 2, SB_ALL]), sb("wt", [P, 2, SB_ALL])
        sp_hi, sp_lo = (ctx.enter_context(nc.sbuf_tensor(f"stick_{n}", [P, 2, SB_ALL], fp32r)) for n in ("sp_hi", "sp_lo"))
        sp_all = sb("sp_all", [P, 2, SB_ALL])
        banks = lambda h: ps[:, 3 * (h % 2):3 * (h % 2) + 3, :].rearrange("p b n -> p (b n)")[:, 0:SB_ALL]
        part = lambda a, i, lo=0, n=None: a[:, SB_OFF[i] + lo:SB_OFF[i] + lo + (SB_W[i] - lo if n is None else n)]

        with nc.Block() as block:
            @block.tensor
            def _(pe):
                def scores(h):
                    t, r = h // 2, HD * (h % 2)
                    for i in (0, 1, 3, 2):
                        if h >= 2 and i < 2:
                            pe.wait_ge(s.first_weights if i == 0 else s.weights_out, h - 1)
                        mm = pe.matmul(part(banks(h), i), kf[r:r + HD, t, P * i:P * i + P],
                                       qf[r:r + HD, t, P * i:SEQ], start=(i != 3), stop=False, skip_group_check=True)
                        mm = pe.matmul(part(banks(h), i, 0, P), core.ident_r[:, :], core.causal_r[:, :],
                                       start=False, stop=False, skip_group_check=True)
                        if i == 0:
                            mm.then_inc(s.first_scores, 1)
                    mm.then_inc(s.scores_done, 1)

                def suffix(h):
                    for a, ready in ((sp_hi[:, h % 2, :], s.sp_made), (sp_lo[:, h % 2, :], s.sp_low)):
                        pe.wait_ge(ready, h + 1)
                        last = ready is s.sp_low
                        for i in range(TT):
                            mm = pe.matmul(part(banks(h), i), core.minus_from_r[:, :], part(a, i), start=False,
                                           stop=(last and i == TT - 1), skip_group_check=True)
                            for j in range(i + 1, TT):
                                mm = pe.matmul(part(banks(h), i, P * (j - i)), core.minus_ones_r[:, :], part(a, j),
                                               start=False, stop=(last and j == TT - 1), skip_group_check=True)
                            if last and i == 0:
                                mm.then_inc(s.first_logs, 1)
                    mm.then_inc(s.logs_done, 1)

                def values(h):
                    t, r = h // 2, HD * (h % 2)
                    pe.wait_ge(s.weights_out, h + 1)
                    pe.wait_ge(s.first_weights, h + 1)
                    if h % 2 == 0 and t >= 2:
                        pe.wait_ge(s.out_used, t - 1)
                    for i in range(TT):
                        mm = pe.matmul(ps[r:r + HD, 6 + t % 2, P * i:SEQ], v[:, i, HD * h:HD * h + HD],
                                       part(wt[:, h % 2, :], i), start=(i == 0), stop=(i == TT - 1),
                                       skip_group_check=True)
                    mm.then_inc(s.values_done, 1)

                for h in range(HN + 2):
                    if h < HN:
                        scores(h)
                    if 1 <= h <= HN:
                        suffix(h - 1)
                    if h >= 2:
                        values(h - 2)

            @block.scalar
            def _(act):
                def first(h):
                    act.wait_ge(s.first_scores, h + 1)
                    if h >= 2:
                        act.wait_ge(s.sp_made, h - 1)
                    e = ex[:, h % 2, :]
                    act.activation(e[:, 0:SEQ], banks(h)[:, 0:SEQ], ACT.Abs).then_inc(s.mag_done, 1)
                    act.wait_ge(s.scores_done, h + 1)
                    act.activation(e[:, SEQ:SB_ALL], banks(h)[:, SEQ:SB_ALL], ACT.Abs).then_inc(s.mag_done, 1)
                    act.wait_ge(s.mag_done, 2 * h + 2)
                    act.activation(e, e, ACT.Exp, scale=-1.0).then_inc(s.exp_done, 1)
                    act.wait_ge(s.exp_done, h + 1)
                    act.activation(e, e, ACT.Ln, bias=1.0).then_inc(s.ln_done, 1)

                def second(h):
                    act.wait_ge(s.first_logs, h + 1)
                    if h >= 2:
                        act.wait_ge(s.values_done, h - 1)
                    act.activation(wt[:, h % 2, 0:SEQ], banks(h)[:, 0:SEQ], ACT.Exp).then_inc(s.first_weights, 1)
                    act.wait_ge(s.logs_done, h + 1)
                    act.activation(wt[:, h % 2, SEQ:SB_ALL], banks(h)[:, SEQ:SB_ALL], ACT.Exp).then_inc(s.weights_out, 1)

                act.preload_act_table_set("natural_log_exp_and_others")
                for h in range(HN + 1):
                    if h < HN:
                        first(h)
                    if h >= 1:
                        second(h - 1)

            @block.vector
            def _(dve):
                def gated(t):
                    dve.wait_ge(s.values_done, 2 * t + 2)
                    dve.tensor_tensor(qf[:, t, :], gate[:, t, :], ps[:, 6 + t % 2, :], ALU.mult).then_inc(s.out_used, 1)

                for h in range(HN):
                    dve.wait_ge(s.ln_done, h + 1)
                    if h >= 2:
                        dve.wait_ge(s.logs_done, h - 1)
                    dve.scalar_tensor_tensor(out=sp_hi[:, h % 2, :], in0=banks(h), scalar=0.0, in1=ex[:, h % 2, :],
                                             op0=ALU.max, op1=ALU.add).then_inc(s.sp_high, 1)
                    dve.scalar_tensor_tensor(out=sp_all[:, h % 2, :], in0=banks(h), scalar=0.0, in1=ex[:, h % 2, :],
                                             op0=ALU.max, op1=ALU.add).then_inc(s.sp_made, 1)
                    dve.wait_ge(s.sp_high, h + 1)
                    dve.wait_ge(s.sp_made, h + 1)
                    dve.tensor_tensor(sp_lo[:, h % 2, :], sp_all[:, h % 2, :], sp_hi[:, h % 2, :].bitcast(fp32),
                                      ALU.subtract).then_inc(s.sp_low, 1)
                    if h >= 3 and h % 2 == 1:
                        gated((h - 3) // 2)
                gated(HN // 2 - 1)
        s.clear()


def stick_breaking(core, ins):
    nc, ps = core.nc, core.ps
    with ExitStack() as ctx:
        sb = lambda n, sh, d=fp32: ctx.enter_context(nc.sbuf_tensor(f"sb_{n}", sh, d))
        kf, qf, v, gate = (sb(n, [P, DK, SEQ]) for n in ("k", "q", "v", "gate"))
        v = v[:, :, :].rearrange("p a b -> p (a b)").rearrange("p (t n) -> p t n", t=TT)
        with ExitStack() as inner:
            xhi, xlo = (inner.enter_context(nc.sbuf_tensor(f"sb_{n}", [P, DK, SEQ], fp32r)) for n in ("xhi", "xlo"))
            head_norm_linear(core, "sbk", kf, 0, xhi, xlo,
                             Norm(core, core.h, lambda k: core.gain("kv_norm", k), xhi, xlo, "sum"))
            linear_stage(core, "sbv", token_tiles(0, 4, 256, DK), xhi, xlo,
                         dve_tile=store_tile(core, lambda t: v[:, t % TT, 256 * (t // TT):256 * (t // TT) + 256]))
            head_norm_linear(core, "sbq", qf, 1, xhi, xlo,
                             Norm(core, core.h, lambda k: core.gain("s_norm", k), xhi, xlo, "inverse"))

            def silu_act(act, s, t):
                act.wait_ge(s.tile_done, t + 1)
                act.activation(gate[:, t, :], ps[:, t % 4, :], ACT.Silu).then_inc(s.bank_free, 1)
            linear_stage(core, "sbg", feature_tiles(0, 4, 256, DK), xhi, xlo,
                         act_tile=silu_act)
        stick_attention_stage(core, qf, kf, v, gate)
        xhi, xlo = sb("ohi", [P, DK, SEQ], fp32r), sb("olo", [P, DK, SEQ], fp32r)
        split_stage(core, "sbs", qf, xhi, xlo, DK)
        linear_stage(core, "sbo", feature_tiles(0, 4, 256, DK), xhi, xlo,
                     dve_tile=residual_tile(core), squares=residual_squares(core))



def split_stage(core, name, src, hi, lo, tiles):
    nc, s = core.nc, Sems(core.nc, name)
    with nc.Block() as block:
        @block.scalar
        def _(act):
            for k in range(tiles):
                act.activation(hi[:, k, :], src[:, k, :], ACT.Copy).then_inc(s.hi_done, 1)

        @block.gpsimd
        def _(pool):
            for k in range(0, tiles, 2):
                pool.wait_ge(s.hi_done, k + 1)
                pool.tensor_tensor(lo[:, k, :], src[:, k, :], hi[:, k, :].bitcast(fp32), ALU.subtract).then_inc(s.lo_done, 1)

        @block.vector
        def _(dve):
            for k in range(1, tiles, 2):
                dve.wait_ge(s.hi_done, k + 1)
                dve.tensor_tensor(lo[:, k, :], src[:, k, :], hi[:, k, :].bitcast(fp32), ALU.subtract).then_inc(s.lo_done, 1)
    s.clear()


def centred_conv(dve, c, acc, x, taps, bias=None):
    c(dve.tensor_scalar(acc, x, taps[1], None, ALU.mult))
    c.wait()
    c(dve.scalar_tensor_tensor(out=acc[:, 1:SEQ], in0=x[:, 0:SEQ - 1], scalar=taps[0], in1=acc[:, 1:SEQ],
                               op0=ALU.mult, op1=ALU.add))
    c.wait()
    return dve.scalar_tensor_tensor(out=acc[:, 0:SEQ - 1], in0=x[:, 1:SEQ], scalar=taps[2], in1=acc[:, 0:SEQ - 1],
                                    op0=ALU.mult, op1=ALU.add)


def hyena_in(core, xhi, xlo, v_tok, x1_tok, x2f, norm):
    nc, ps = core.nc, core.ps
    with ExitStack() as ctx:
        conv = ctx.enter_context(nc.sbuf_tensor("hyin_conv", [P, 2, SEQ], fp32))

        def conv_dve(dve, s, t):
            c = Chain(dve, s.conv_chain)
            c.n = 2 * t
            acc = conv[:, t % 2, :] if t < 8 else x2f[:, t - 8, :]
            dve.wait_ge(s.tile_done, t + 1)
            if 2 <= t < 8:
                dve.wait_ge(s.turned, t - 1)
            centred_conv(dve, c, acc, ps[:, t % 4, :],
                         [core.gain("hy_short_w_2", 12 * j + t) for j in range(3)]).then_inc(s.bank_free, 1)

        def turn_pe(pe, s, t):
            if t >= 8:
                return
            pe.wait_ge(s.bank_free, t + 1)
            if t >= 2:
                pe.wait_ge(s.stored, t - 1)
            for c in range(TT):
                mm = pe.transpose(ps[:, 4 + t % 2, P * c:P * c + P], conv[:, t % 2, P * c:P * c + P], core.ident[:, :])
            mm.then_inc(s.turned, 1)

        def store_act(act, s, t):
            if 1 <= t <= 8:
                u = t - 1
                dst = (v_tok if u < 4 else x1_tok)[:, :, P * (u % 4):P * (u % 4) + P]
                act.wait_ge(s.turned, u + 1)
                act.activation(dst, ps[:, 4 + u % 2, :].rearrange("p (c f) -> p c f", c=TT), ACT.Copy).then_inc(s.stored, 1)
        linear_stage(core, "hyin", feature_tiles(0, 6, 256, DK), xhi, xlo, norm=norm,
                     act_tile=store_act, dve_tile=conv_dve, pe_after=turn_pe)


def short_conv_in(core, ins, xhi, xlo, yc, hidden):
    nc, ps = core.nc, core.ps
    with ExitStack() as ctx:
        sb = lambda n: ctx.enter_context(nc.sbuf_tensor(f"scin_{n}", [P, 4, SEQ], fp32))
        cg, cx = sb("c"), sb("cx")
        basis = FilterBasis(ctx, core, ins, hidden)

        def step(dve, s, t):
            c = Chain(dve, s.chain)
            f = t % 4
            dve.wait_ge(s.tile_done, t + 1)
            if t < 4:
                dve.tensor_copy(cg[:, f, :], ps[:, t % 4, :]).then_inc(s.bank_free, 1)
            elif t < 8:
                dve.wait_ge(s.bank_free, f + 1)
                dve.tensor_tensor(cx[:, f, :], cg[:, f, :], ps[:, t % 4, :], ALU.mult).then_inc(s.bank_free, 1)
            else:
                c.n = 3 * f
                dve.wait_ge(s.bank_free, 4 + f + 1)
                c(centred_conv(dve, c, cg[:, f, :], cx[:, f, :], [core.gain("sc_conv_w_2", 4 * j + f) for j in range(3)]))
                c.wait()
                dve.tensor_tensor(yc[:, f, :], cg[:, f, :], ps[:, t % 4, :], ALU.mult).then_inc(s.bank_free, 1)
            if t in (2, 7):
                basis.dve_reduce(dve, s, (2, 7).index(t))

        def product(pe, s, t):
            if t in (0, 4):
                basis.pe_product(pe, s, (0, 4).index(t))

        def sine(act, s, t):
            if t in (3, 8):
                basis.act_sine(act, s, (3, 8).index(t))
        linear_stage(core, "scin", feature_tiles(0, 6, 256, DK), xhi, xlo, dve_tile=step, act_tile=sine,
                     first=basis, pe_after=product)


class FilterBasis:
    H, E = 64, 33

    def __init__(self, ctx, core, ins, hidden):
        H, E = self.H, self.E
        sb = lambda n, sh: ctx.enter_context(core.nc.sbuf_tensor(f"filt_{n}", sh, fp32))
        self.core, self.ins, self.hidden = core, ins, hidden
        self.w1, self.w2, self.emb = sb("w1", [E, H]), sb("w2", [H, H]), sb("emb", [E, SEQ])
        self.cols = sb("cols", [H, 4])
        self.arg, self.turns, self.inner = sb("arg", [H, SEQ]), sb("turns", [H, SEQ]), sb("inner", [H, SEQ])

    def sp(self, sp, s):
        ins, cols = self.ins, self.cols
        col = lambda a: a.rearrange("(p a) -> p a", a=1)
        for dst, src in ((self.w1[:, :], ins["hy_w1_2"][0]), (self.w2[:, :], ins["hy_w2_2"][0]),
                         (self.emb[:, :], ins["pos_emb"]),
                         (cols[:, 0:1], col(ins["hy_b1_2"][0])), (cols[:, 1:2], col(ins["hy_b2_2"][0])),
                         (cols[:, 2:3], col(ins["hy_freq_2"][0, 0])), (cols[:, 3:4], col(ins["hy_freq_2"][0, 1]))):
            sp.dma_start(dst, src).then_inc(s.basis_loaded, 16)

    def act(self, act, s):
        pass

    def pe(self, pe, s):
        pass

    def pool(self, pool, s):
        pass

    def pe_product(self, pe, s, n):
        ps, H = self.core.ps, self.H
        pe.wait_ge(s.basis_loaded, 16 * 7)
        if n == 0:
            pe.matmul(ps[0:H, 4, :], self.w1[:, :], self.emb[:, :], start=True, stop=True).then_inc(s.product, 1)
        else:
            pe.wait_ge(s.sine, 1)
            pe.matmul(ps[0:H, 5, :], self.w2[:, :], self.inner[:, :], start=True, stop=True).then_inc(s.product, 1)

    def dve_reduce(self, dve, s, n):
        arg, turns, cols = self.arg, self.turns, self.cols
        two_pi = 2 * math.pi
        c1 = 6.28125
        c2 = float(np.float32(two_pi - c1))
        c3 = float(np.float32(two_pi - c1 - c2))
        magic = 1.5 * 2.0 ** 23
        pi = float(np.nextafter(np.float32(math.pi), np.float32(0)))
        c = Chain(dve, s.basis_chain)
        c.n = 6 * n
        dve.wait_ge(s.basis_loaded, 16 * 7)
        dve.wait_ge(s.product, n + 1)
        if n:
            dve.wait_ge(s.sine, 1)
        c(dve.tensor_scalar(arg[:, :], self.core.ps[0:self.H, 4 + n, :], cols[:, n:n + 1], cols[:, 2 + n:3 + n],
                            ALU.add, ALU.mult))
        c.wait()
        c(dve.tensor_scalar(turns[:, :], arg[:, :], 1.0 / two_pi, magic, ALU.mult, ALU.add))
        c.wait()
        c(dve.tensor_scalar(turns[:, :], turns[:, :], -magic, None, ALU.add))
        for part in (c1, c2, c3):
            c.wait()
            c(dve.scalar_tensor_tensor(out=arg[:, :], in0=turns[:, :], scalar=-part, in1=arg[:, :],
                                       op0=ALU.mult, op1=ALU.add))
        c.wait()
        dve.tensor_scalar(arg[:, :], arg[:, :], pi, -pi, ALU.min, ALU.max).then_inc(s.reduced, 1)

    def act_sine(self, act, s, n):
        act.wait_ge(s.reduced, n + 1)
        act.activation((self.hidden if n else self.inner)[:, :], self.arg[:, :], ACT.Sin).then_inc(s.sine, 1)


def filter_stage(core, ins, order, hidden, su_hi, su_lo, di_hi, di_lo):
    nc, s, ps = core.nc, Sems(core.nc, f"fl{order}"), core.ps
    with ExitStack() as ctx:
        sb = lambda n, sh: ctx.enter_context(nc.sbuf_tensor(f"fl{order}_{n}", sh, fp32))
        w3, decay = sb("w3", [64, 2, HY]), sb("decay", [P, 2, HY])
        fwd, bwd, tmp, bias = sb("fwd", [P, 2, HY]), sb("bwd", [P, 2, HY]), sb("tmp", [P, 2, HY]), sb("bias", [1, HY])
        with nc.Block() as block:
            @block.sync
            def _(sp):
                for direction in range(2):
                    c0 = (2 * direction + order) * HY
                    sp.dma_start(w3[:, direction, :], ins["hy_w3_2"][0, :, c0:c0 + HY]).then_inc(s.loaded, 16)
                sp.dma_start(bias[:, :], ins["hy_bias_2"][0, order:order + 1, :]).then_inc(s.loaded, 16)
                for t in range(TT):
                    if t >= 2:
                        sp.wait_ge(s.halves, 2 * (t - 1))
                    sp.dma_start(decay[:, t % 2, :], ins["hy_decay"][P * t:P * t + P, :]).then_inc(s.decay_even if t % 2 == 0 else s.decay_odd, 16)

            @block.tensor
            def _(pe):
                pe.wait_ge(s.loaded, 48)
                for t in range(TT):
                    for direction in range(2):
                        pe.matmul(ps[:, 2 * t + direction, :], hidden[:, P * t:P * t + P], w3[:, direction, :],
                                  start=True, stop=True).then_inc(s.product, 1)

            @block.vector
            def _(dve):
                c = Chain(dve, s.chain)
                for t in range(TT):
                    b = t % 2
                    dve.wait_ge(s.decay_even if b == 0 else s.decay_odd, 16 * (t // 2 + 1))
                    dve.wait_ge(s.product, 2 * t + 2)
                    if t >= 2:
                        dve.wait_ge(s.lo_done, 2 * (t - 1))
                    dve.tensor_tensor(fwd[:, b, :], ps[:, 2 * t, :], decay[:, b, :], ALU.mult).then_inc(s.halves, 1)
                    dve.tensor_tensor(bwd[:, b, :], ps[:, 2 * t + 1, :], decay[:, b, :], ALU.mult).then_inc(s.halves, 1)
                    dve.wait_ge(s.halves, 2 * t + 2)
                    if t == 0:
                        c(dve.memset(bwd[0:1, 0, :], 0.0))
                        c(dve.tensor_tensor(fwd[0:1, 0, :], fwd[0:1, 0, :], bias[:, :], ALU.add))
                        c.wait()
                    dve.tensor_tensor(tmp[:, b, :], fwd[:, b, :], bwd[:, b, :], ALU.add).then_inc(s.combined, 1)
                    dve.wait_ge(s.combined, 2 * t + 1)
                    dve.tensor_tensor(fwd[:, b, :], fwd[:, b, :], bwd[:, b, :], ALU.subtract).then_inc(s.combined, 1)

            @block.scalar
            def _(act):
                for t in range(TT):
                    act.wait_ge(s.combined, 2 * t + 2)
                    act.activation(su_hi[:, t, :], tmp[:, t % 2, :], ACT.Copy).then_inc(s.hi_done, 1)
                    act.activation(di_hi[:, t, :], fwd[:, t % 2, :], ACT.Copy).then_inc(s.hi_done, 1)

            @block.gpsimd
            def _(pool):
                for t in range(TT):
                    pool.wait_ge(s.hi_done, 2 * t + 2)
                    pool.tensor_tensor(su_lo[:, t, :], tmp[:, t % 2, :], su_hi[:, t, :].bitcast(fp32), ALU.subtract).then_inc(s.lo_done, 1)
                    pool.tensor_tensor(di_lo[:, t, :], fwd[:, t % 2, :], di_hi[:, t, :].bitcast(fp32), ALU.subtract).then_inc(s.lo_done, 1)
        s.clear()


def long_conv(core, ins, order, hidden, src, finish):
    nc, ps = core.nc, core.ps
    with ExitStack() as ctx:
        f32t = lambda n, sh, d=fp32: ctx.enter_context(nc.sbuf_tensor(f"lc{order}_{n}", sh, d))
        su_hi, su_lo, di_hi, di_lo = (f32t(n, [P, 4, HY], fp32r) for n in ("su_hi", "su_lo", "di_hi", "di_lo"))
        filter_stage(core, ins, order, hidden, su_hi, su_lo, di_hi, di_lo)
        z_hi, z_lo = (f32t(n, [P, 4, HY], fp32r) for n in ("z_hi", "z_lo"))
        split_stage(core, f"zs{order}", src, z_hi, z_lo, 4)
        yhi, ylo = f32t("yhi", [P, 8, HY], fp32r), f32t("ylo", [P, 8, HY], fp32r)
        k_re, k_im = f32t("k_re", [P, 2, HY]), f32t("k_im", [P, 2, HY])
        k_re0 = f32t("k_re0", [P, HY])
        a, b, y = core.sq, core.sq_sum, core.split_buf

        ks = [(k, k) for k in range(4)]
        freqs, parts = (1, 2, 3, 0), ("k_re", "z_re", "k_im", "z_im")
        tiles = []
        for f in freqs:
            if f == 0:
                tiles.append([(1, slice(0, 32), ks, None, su_hi, su_lo)])
            cols = slice(P * f, P * f + P)
            tiles += [[(slab, cols, ks, None, hi, lo)] for slab, hi, lo in
                      ((0, su_hi, su_lo), (0, z_hi, z_lo), (1, di_hi, di_lo), (1, z_hi, z_lo))]
        nyquist = 12
        what = lambda t: (t // 4, parts[t % 4]) if t < nyquist else (3, "nyquist" if t == nyquist else parts[t - nyquist - 1])

        def round_high(act, s, g):
            for im in range(2):
                act.wait_ge(s.y_ready, 2 * g + im + 1)
                act.activation(yhi[:, freqs[g] + 4 * im, :], y[im][:, :], ACT.Copy).then_inc(s.hi_done, 1)

        def act_tile(act, s, t):
            g, part = what(t)
            if part in ("k_re", "k_im"):
                act.wait_ge(s.tile_done, t + 1)
                if g >= 2:
                    act.wait_ge(s.y_ready, 2 * (g - 1))
                act.activation((k_re if part == "k_re" else k_im)[:, g % 2, :], ps[:, t % 8, :], ACT.Copy)\
                   .then_inc(s.k_kept, 1)
            if part == "k_im" and g >= 1:
                round_high(act, s, g - 1)
            if t == 16:
                round_high(act, s, 3)

        def take_low(pool, s, g):
            for im in range(2):
                pool.wait_ge(s.hi_done, 2 * g + im + 1)
                pool.tensor_tensor(ylo[:, freqs[g] + 4 * im, :], y[im][:, :], yhi[:, freqs[g] + 4 * im, :].bitcast(fp32), ALU.subtract)\
                    .then_inc(s.lo_done, 1)

        def pool_tile(pool, s, t):
            g, part = what(t)
            if part == "k_im" and g >= 1:
                take_low(pool, s, g - 1)
            if t == 16:
                take_low(pool, s, 3)

        def dve_tile(dve, s, t):
            g, part = what(t)
            if part != "z_im":
                return
            z_re, z_im = ps[:, (t - 2) % 8, :], ps[:, t % 8, :]
            re, im = k_re[:, g % 2, :], k_im[:, g % 2, :]
            dve.wait_ge(s.k_kept, 2 * g + 2)
            dve.wait_ge(s.tile_done, t + 1)
            if freqs[g] == 0:
                dve.tensor_copy(k_re0[:, :], re).then_inc(s.patched, 1)
                dve.memset(im[0:1, :], 0.0).then_inc(s.patched, 1)
                dve.wait_ge(s.patched, 1)
                dve.tensor_copy(k_re0[0:1, :], ps[0:1, nyquist % 8, :]).then_inc(s.patched, 1)
                dve.wait_ge(s.patched, 3)
            if g >= 1:
                dve.wait_ge(s.y_ready, 2 * g)
            dve.tensor_tensor(a[0][:, :], z_re, re, ALU.mult).then_inc(s.terms, 1)
            dve.tensor_tensor(b[:, :], z_im, im, ALU.mult).then_inc(s.terms, 1)
            dve.tensor_tensor(a[1][:, :], z_re, im, ALU.mult).then_inc(s.terms, 1)
            last = k_re0[:, :] if freqs[g] == 0 else re
            dve.tensor_tensor(last, z_im, last, ALU.mult).then_inc(s.bank_free, 1)
            dve.wait_ge(s.terms, 3 * g + 2)
            if g >= 1:
                dve.wait_ge(s.lo_done, 2 * g - 1)
            dve.tensor_tensor(y[0][:, :], a[0][:, :], b[:, :], ALU.subtract).then_inc(s.y_ready, 1)
            dve.wait_ge(s.terms, 3 * g + 3)
            dve.wait_ge(s.bank_free, g + 1)
            if g >= 1:
                dve.wait_ge(s.lo_done, 2 * g)
            dve.tensor_tensor(y[1][:, :], a[1][:, :], last, ALU.add).then_inc(s.y_ready, 1)
        linear_stage(core, f"sp{order}", tiles, None, None, act_tile=act_tile, dve_tile=dve_tile, pool_tile=pool_tile,
                     banks=8, bank_need=lambda t: (t - 8) // 4 + 1)
        finish(yhi, ylo)


def hyena(core, ins, hidden, v_tok, x1_tok, x2f):
    nc, ps = core.nc, core.ps

    def first(yhi, ylo):
        def step(dve, s, t):
            dve.wait_ge(s.tile_done, t + 1)
            dve.tensor_tensor(x1_tok[:, t, :], x1_tok[:, t, :], ps[:, t % 4, :], ALU.mult).then_inc(s.bank_free, 1)
        linear_stage(core, "inv0", feature_tiles(0, 2, 256, 8), yhi, ylo, dve_tile=step)
    long_conv(core, ins, 0, hidden, v_tok, first)

    def second(yhi, ylo):
        def step(dve, s, t):
            j, f = t // 4, t % 4
            cols = slice(256 * j, 256 * j + 256)
            dve.wait_ge(s.tile_done, t + 1)
            dve.tensor_tensor(x2f[:, f, cols], x2f[:, f, cols], ps[:, t % 4, 0:256], ALU.mult).then_inc(s.bank_free, 1)
        linear_stage(core, "inv1", token_tiles(0, 2, 256, 8), yhi, ylo, dve_tile=step)
    long_conv(core, ins, 1, hidden, x1_tok, second)


class WindowBias:
    NH, NR, NC = 8, 15, 31

    def __init__(self, ctx, core, ins, bias):
        sb = lambda n, sh: ctx.enter_context(core.nc.sbuf_tensor(f"wb_{n}", sh, fp32))
        self.core, self.ins, self.bias = core, ins, bias
        self.rows, self.cols = sb("rows", [self.NH * self.NR, self.NC]), sb("cols", [self.NC, self.NH * self.NR])
        self.anti, self.mask = sb("anti", [self.NC, 63 + P]), sb("mask", [P, 64])

    def columns(self, t):
        return range(16 * (t - 1) // 7, 16 * t // 7) if t else ()

    def sp(self, sp, s):
        for dst, src in ((self.rows, self.ins["na_rpb_2"][0].rearrange("h r c -> (h r) c")),
                         (self.anti, self.ins["anti_diagonal"]), (self.mask, self.ins["column_mask"])):
            sp.dma_start(dst[:, :], src).then_inc(s.bias_loaded, 16)

    def act(self, act, s):
        pass

    def pool(self, pool, s):
        pass

    def pe(self, pe, s):
        pass

    def pe_after(self, pe, s, t):
        ps, rows = self.core.ps, self.NH * self.NR
        if t == 0:
            pe.wait_ge(s.bias_loaded, 48)
            pe.transpose(ps[0:self.NC, 7, 0:rows], self.rows[:, :], self.core.ident[0:rows, 0:rows]).then_inc(s.turned, 1)
            return
        pe.wait_ge(s.cols_ready, 1)
        for n in self.columns(t):
            if n >= 4:
                pe.wait_ge(s.stored, 2 * (n - 3))
            for q in range(4):
                x = 63 - (4 * n + q)
                mm = pe.matmul(ps[:, 4 + n % 4, rows * q:rows * q + rows], self.anti[:, x:x + P], self.cols[:, :],
                               start=True, stop=True)
            mm.then_inc(s.picked, 1)

    def dve_after(self, dve, s, t):
        ps, rows = self.core.ps, self.NH * self.NR
        if t == 0:
            dve.wait_ge(s.turned, 1)
            dve.tensor_copy(self.cols[:, :], ps[0:self.NC, 7, 0:rows]).then_inc(s.cols_ready, 1)
        for n in self.columns(t):
            dve.wait_ge(s.picked, n + 1)
            for half in range(2):
                r = slice(64 * half, 64 * half + 64)
                out = self.bias[r, :, half:half + self.NR, 4 * n:4 * n + 4].rearrange("p h m c -> p c h m")
                dve.tensor_tensor(out, ps[r, 4 + n % 4, 0:4 * rows].rearrange("p (c h m) -> p c h m", c=4, h=self.NH),
                                  self.mask[r, 4 * n:4 * n + 4].unsqueeze(2).unsqueeze(3)
                                  .to_broadcast([64, 4, self.NH, self.NR]), ALU.add).then_inc(s.stored, 1)


def neighbourhood_stage(core, qf, kf, v, bias, yb):
    nc, s, ps = core.nc, Sems(core.nc, "na"), core.ps
    NH = 8
    with ExitStack() as ctx:
        sb = lambda n, sh: ctx.enter_context(nc.sbuf_tensor(f"na_{n}", sh, fp32))
        sc, pr, pt = sb("sc", [P, 2, SEQ]), sb("pr", [P, 4, SEQ]), sb("pt", [P, 2, TT, SEQ])
        neg, tot, inv = sb("neg", [P, 4]), sb("tot", [P, 4]), sb("inv", [P, 4])
        units = [(h, i) for h in range(NH) for i in range(TT)]
        U = len(units)
        score_bank = lambda u: (0, 1, 6, 7)[u % 4]
        with nc.Block() as block:
            @block.tensor
            def _(pe):
                def scores(u):
                    h, i = units[u]
                    t, r = h // 2, HD * (h % 2)
                    if u >= 4:
                        pe.wait_ge(s.biased, u - 3)
                    pe.matmul(ps[:, score_bank(u), :], qf[r:r + HD, t, P * i:P * i + P], kf[r:r + HD, t, :],
                              start=True, stop=True).then_inc(s.scores_done, 1)

                def turn(u):
                    pe.wait_ge(s.normed, u + 1)
                    if u >= 2:
                        pe.wait_ge(s.copied, u - 1)
                    for j in range(TT):
                        mm = pe.transpose(ps[:, 2 + u % 2, P * j:P * j + P], pr[:, u % 4, P * j:P * j + P], core.ident[:, :])
                    mm.then_inc(s.turned, 1)

                def values(h, j):
                    t, r = h // 2, HD * (h % 2)
                    if j == 0:
                        pe.wait_ge(s.copied, 4 * h + 4)
                        if h % 2 == 0 and t >= 2:
                            pe.wait_ge(s.out_done, t - 1)
                    mm = pe.matmul(ps[r:r + HD, 4 + t % 2, :], v[:, j, HD * h:HD * h + HD], pt[:, h % 2, j, :],
                                   start=(j == 0), stop=(j == TT - 1))
                    if j == TT - 1:
                        mm.then_inc(s.values_done, 1)
                for u in range(U + 8):
                    if u < U:
                        scores(u)
                    if 4 <= u < U + 4:
                        turn(u - 4)
                    if u >= 8:
                        values((u - 8) // 4, (u - 8) % 4)

            @block.vector
            def _(dve):
                def out(dve, t):
                    dve.wait_ge(s.values_done, 2 * t + 2)
                    dve.tensor_copy(yb[:, t, :], ps[:, 4 + t % 2, :]).then_inc(s.out_done, 1)

                def soften(u):
                    h, i = units[u]
                    dve.wait_ge(s.scores_done, u + 1)
                    if u >= 2:
                        dve.wait_ge(s.exp_done, u - 1)
                    m0 = 8 - 2 * i
                    dve.tensor_tensor(sc[:, u % 2, :].rearrange("p (m c) -> p m c", m=8),
                                      ps[:, score_bank(u), :].rearrange("p (m c) -> p m c", m=8),
                                      bias[:, h, m0 - 1:m0 + 7, :], ALU.add).then_inc(s.biased, 1)
                    dve.wait_ge(s.biased, u + 1)
                    dve.tensor_reduce(neg[:, u % 4:u % 4 + 1], sc[:, u % 2, :], AX.X, ALU.max, negate=True).then_inc(s.max_done, 1)

                def normalise(u):
                    dve.wait_ge(s.exp_done, u + 1)
                    dve.reciprocal(inv[:, u % 4:u % 4 + 1], tot[:, u % 4:u % 4 + 1]).then_inc(s.inv_done, 1)
                    dve.wait_ge(s.inv_done, u + 1)
                    dve.tensor_scalar(pr[:, u % 4, :], pr[:, u % 4, :], inv[:, u % 4:u % 4 + 1], None, ALU.mult).then_inc(s.normed, 1)

                for u in range(U + 1):
                    if u < U:
                        soften(u)
                    if u >= 1:
                        normalise(u - 1)
                    if u >= 16 and u % 8 == 0:
                        out(dve, (u - 16) // 8)
                out(dve, NH // 2 - 1)

            @block.scalar
            def _(act):
                def copy(u):
                    h, i = units[u]
                    act.wait_ge(s.turned, u + 1)
                    if h >= 2:
                        act.wait_ge(s.values_done, h - 1)
                    act.activation(pt[:, h % 2, :, P * i:P * i + P], ps[:, 2 + u % 2, :].rearrange("p (j q) -> p j q", j=TT),
                                   ACT.Copy).then_inc(s.copied, 1)
                for u in range(U + 4):
                    if u < U:
                        act.wait_ge(s.max_done, u + 1)
                        if u >= 4:
                            act.wait_ge(s.turned, u - 3)
                        act.activation(pr[:, u % 4, :], sc[:, u % 2, :], ACT.Exp, bias=neg[:, u % 4:u % 4 + 1],
                                       accum_out=tot[:, u % 4:u % 4 + 1]).then_inc(s.exp_done, 1)
                    if u >= 4:
                        copy(u - 4)
        s.clear()


class SplitSum:

    def __init__(self, merged, parts):
        self.merged, self.parts = merged, parts

    def act(self, act, s, f):
        act.wait_ge(s.added, f + 1)
        act.activation(self.parts[f // 4][0][:, f % 4, :], self.merged[:, f, :], ACT.Copy).then_inc(s.hi_done, 1)

    def pool(self, pool, s, f):
        hi, lo = self.parts[f // 4]
        pool.wait_ge(s.hi_done, f + 1)
        pool.tensor_tensor(lo[:, f % 4, :], self.merged[:, f, :], hi[:, f % 4, :].bitcast(fp32), ALU.subtract)\
            .then_inc(s.lo_done, 1)


def merge_stages(core, xhi, xlo, parts, merged, norm):
    nc, ps = core.nc, core.ps
    with ExitStack() as ctx:
        sig, prod = (ctx.enter_context(nc.sbuf_tensor(f"mg_{n}", [P, 2, SEQ], fp32)) for n in ("sig", "prod"))
        for b, (yhi, ylo) in enumerate(parts):
            if b == 0:
                add = lambda dve, f, pr: dve.tensor_copy(merged[:, f, :], pr)
            else:
                add = lambda dve, f, pr: dve.tensor_tensor(merged[:, f, :], merged[:, f, :], pr, ALU.add)
            gated_stage(core, f"mg{b}", [(k, k) for k in range(4)], yhi, ylo, xhi, xlo, sig, prod,
                        lambda f: core.gain("gate_bias_2", DK * b + f), add, norm if b == 0 else None,
                        SplitSum(merged, parts) if b == 2 else None)


def branches(core, ins):
    nc = core.nc
    g = lambda n: (lambda k: core.gain("norm_gains_2", DK * n + k))
    with ExitStack() as ctx:
        sb = lambda c, n, sh, d=fp32: c.enter_context(nc.sbuf_tensor(f"b2_{n}", sh, d))
        y_all = sb(ctx, "y_all", [P, 12, SEQ])
        ya, yb, yc = (y_all[:, 4 * b:4 * b + 4, :] for b in range(3))
        with ExitStack() as mid:
            x1_tok = sb(mid, "x1_tok", [P, 4, SEQ])
            hidden = sb(mid, "hy_hidden", [64, SEQ])
            with ExitStack() as c1:
                xhi, xlo = sb(c1, "xhi", [P, DK, SEQ], fp32r), sb(c1, "xlo", [P, DK, SEQ], fp32r)
                hyena_in(core, xhi, xlo, yb, x1_tok, ya, Norm(core, core.h, g(0), xhi, xlo, "sum"))
                short_conv_in(core, ins, xhi, xlo, yc, hidden)
            hyena(core, ins, hidden, yb, x1_tok, ya)
        with ExitStack() as mid:
            qf, kf, nv = (sb(mid, n, [P, 4, SEQ]) for n in ("qf", "kf", "nv"))
            bias = sb(mid, "bias", [P, 8, 16, 64])
            with ExitStack() as c1:
                window = WindowBias(c1, core, ins, bias)
                xhi, xlo = sb(c1, "x1hi", [P, DK, SEQ], fp32r), sb(c1, "x1lo", [P, DK, SEQ], fp32r)
                def qk(dve, s, t):
                    dve.wait_ge(s.tile_done, t + 1)
                    dst, scale = (qf, HD ** -0.5) if t < 4 else (kf, 1.0)
                    dve.tensor_scalar(dst[:, t % 4, :], core.ps[:, t % 4, :], scale, None, ALU.mult).then_inc(s.bank_free, 1)
                    if t >= 1:
                        window.dve_after(dve, s, t - 1)
                    if t == 7:
                        window.dve_after(dve, s, t)
                linear_stage(core, "naqk", feature_tiles(0, 4, 256, DK), xhi, xlo, dve_tile=qk, first=window, pe_after=window.pe_after,
                             norm=Norm(core, core.h, g(0), xhi, xlo, "inverse"))
                linear_stage(core, "nav", token_tiles(0, 2, 256, DK), xhi, xlo,
                             dve_tile=store_tile(core, lambda t: nv[:, t % TT, 256 * (t // TT):256 * (t // TT) + 256]))
            neighbourhood_stage(core, qf, kf, nv, bias, yb)
        y3 = (ya, yb, yc)
        parts = []
        for b in range(3):
            hi, lo = sb(ctx, f"yh{b}", [P, 4, SEQ], fp32r), sb(ctx, f"yl{b}", [P, 4, SEQ], fp32r)
            split_stage(core, f"ys{b}", y3[b], hi, lo, 4)
            parts.append((hi, lo))
        merged = y_all[:, 0:DK, :]
        with ExitStack() as c2:
            xhi, xlo = sb(c2, "x2hi", [P, DK, SEQ], fp32r), sb(c2, "x2lo", [P, DK, SEQ], fp32r)
            merge_stages(core, xhi, xlo, parts, merged, Norm(core, core.h, g(0), xhi, xlo, "inverse"))
            tiles = [[(t // 2, slice(P * (t % 2), P * (t % 2) + P), [(4 * b + k, k) for k in range(4)], None, *parts[b])
                      for b in range(2)] for t in range(DK)]
            linear_stage(core, "wout", tiles, None, None,
                         dve_tile=store_tile(core, lambda t: merged[:, t, :]), squares=stored_squares(core, merged))
        add_normed_stage(core, "n1", merged, g(1))


def memory_attention_stage(core, qf, kf, v, ohi, olo):
    nc, s, ps = core.nc, Sems(core.nc, "xa"), core.ps
    NH, W = 4, 256
    with ExitStack() as ctx:
        sb = lambda n, sh: ctx.enter_context(nc.sbuf_tensor(f"xa_{n}", sh, fp32))
        pr, pt = sb("pr", [P, 2, W]), sb("pt", [P, 2, MT, SEQ])
        neg, tot, inv = sb("neg", [P, 4]), sb("tot", [P, 4]), sb("inv", [P, 4])
        tmp = core.split_buf
        units = [(h, i) for h in range(NH) for i in range(TT)]
        U = len(units)
        with nc.Block() as block:
            @block.tensor
            def _(pe):
                def scores(u):
                    h, i = units[u]
                    if u >= 2:
                        pe.wait_ge(s.exp_done, u - 1)
                    for k in range(2):
                        mm = pe.matmul(ps[:, u % 2, 0:W], qf[:, 2 * h + k, P * i:P * i + P], kf[:, 2 * h + k, :],
                                       start=(k == 0), stop=(k == 1))
                    mm.then_inc(s.scores_done, 1)

                def turn(u):
                    pe.wait_ge(s.normed, u + 1)
                    if u >= 2:
                        pe.wait_ge(s.copied, u - 1)
                    for j in range(MT):
                        mm = pe.transpose(ps[:, 2 + u % 2, P * j:P * j + P], pr[:, u % 2, P * j:P * j + P], core.ident[:, :])
                    mm.then_inc(s.turned, 1)

                def values(h):
                    pe.wait_ge(s.copied, 4 * h + 4)
                    for d in range(2):
                        n = 2 * h + d
                        if n >= 2:
                            pe.wait_ge(s.out_done, n - 1)
                        for j in range(MT):
                            mm = pe.matmul(ps[:, 4 + n % 2, :], v[:, j, P * n:P * n + P], pt[:, h % 2, j, :],
                                           start=(j == 0), stop=(j == MT - 1))
                        mm.then_inc(s.values_done, 1)
                for u in range(U + 3):
                    if u < U:
                        scores(u)
                    if 2 <= u < U + 2:
                        turn(u - 2)
                    if u >= 3 and (u - 3) % 4 == 3:
                        values((u - 3) // 4)

            @block.vector
            def _(dve):
                def out(n):
                    dve.wait_ge(s.values_done, n + 1)
                    if n >= 2:
                        dve.wait_ge(s.lo_done, n - 1)
                    dve.tensor_copy(tmp[n % 2][:, :], ps[:, 4 + n % 2, :]).then_inc(s.out_done, 1)

                for u in range(U + 1):
                    if u < U:
                        dve.wait_ge(s.scores_done, u + 1)
                        dve.tensor_reduce(neg[:, u % 4:u % 4 + 1], ps[:, u % 2, 0:W], AX.X, ALU.max, negate=True)\
                           .then_inc(s.max_done, 1)
                    if u >= 1:
                        w = u - 1
                        dve.wait_ge(s.exp_done, w + 1)
                        dve.reciprocal(inv[:, w % 4:w % 4 + 1], tot[:, w % 4:w % 4 + 1]).then_inc(s.inv_done, 1)
                        dve.wait_ge(s.inv_done, w + 1)
                        dve.tensor_scalar(pr[:, w % 2, :], pr[:, w % 2, :], inv[:, w % 4:w % 4 + 1], None, ALU.mult)\
                           .then_inc(s.normed, 1)
                    if u >= 7 and (u - 7) % 4 == 0:
                        out(2 * ((u - 7) // 4))
                        out(2 * ((u - 7) // 4) + 1)
                for n in range(6, 8):
                    out(n)

            @block.scalar
            def _(act):
                def high(n):
                    act.wait_ge(s.out_done, n + 1)
                    act.activation(ohi[:, n, :], tmp[n % 2][:, :], ACT.Copy).then_inc(s.hi_done, 1)

                def copy(u):
                    h, i = units[u]
                    act.wait_ge(s.turned, u + 1)
                    if h >= 2:
                        act.wait_ge(s.values_done, 2 * (h - 1))
                    act.activation(pt[:, h % 2, :, P * i:P * i + P],
                                   ps[:, 2 + u % 2, 0:W].rearrange("p (j q) -> p j q", j=MT), ACT.Copy).then_inc(s.copied, 1)
                for u in range(U + 2):
                    if u < U:
                        act.wait_ge(s.max_done, u + 1)
                        if u >= 2:
                            act.wait_ge(s.turned, u - 1)
                        act.activation(pr[:, u % 2, :], ps[:, u % 2, 0:W], ACT.Exp, bias=neg[:, u % 4:u % 4 + 1],
                                       accum_out=tot[:, u % 4:u % 4 + 1]).then_inc(s.exp_done, 1)
                    if u >= 2:
                        copy(u - 2)
                    if u >= 7 and (u - 7) % 4 == 0:
                        high(2 * ((u - 7) // 4))
                        high(2 * ((u - 7) // 4) + 1)
                for n in range(6, 8):
                    high(n)

            @block.gpsimd
            def _(pool):
                for n in range(8):
                    pool.wait_ge(s.hi_done, n + 1)
                    pool.tensor_tensor(olo[:, n, :], tmp[n % 2][:, :], ohi[:, n, :].bitcast(fp32), ALU.subtract)\
                        .then_inc(s.lo_done, 1)
        s.clear()


def memory_attention(core, ins):
    nc, ps = core.nc, core.ps
    g = lambda n: (lambda k: core.gain("norm_gains_2", DK * n + k))
    with ExitStack() as ctx:
        sb = lambda n, sh, d=fp32: ctx.enter_context(nc.sbuf_tensor(f"xm_{n}", sh, d))
        qf, kf, v = sb("q", [P, DK, SEQ]), sb("k", [P, DK, N_MEM]), sb("v", [P, MT, D])
        xhi, xlo = sb("xhi", [P, DK, SEQ], fp32r), sb("xlo", [P, DK, SEQ], fp32r)
        with ExitStack() as c1:
            mem = c1.enter_context(nc.sbuf_tensor("xm_mem", [P, MT, D], fp32))
            mt = c1.enter_context(nc.sbuf_tensor("xm_memt", [P, DK, N_MEM], fp32))
            mhi = c1.enter_context(nc.sbuf_tensor("xm_mhi", [P, DK, N_MEM], fp32r))
            mlo = c1.enter_context(nc.sbuf_tensor("xm_mlo", [P, DK, N_MEM], fp32r))
            s = Sems(nc, "mt")
            with nc.Block() as block:
                @block.sync
                def _(sp):
                    sp.dma_start(mem[:, :, :], ins["mem_2"][0].rearrange("(t p) d -> p t d", p=P)).then_inc(s.loaded, 16)

                @block.tensor
                def _(pe):
                    pe.wait_ge(s.loaded, 16)
                    for n in range(4):
                        t, half = n // 2, n % 2
                        for k in range(4):
                            c = P * (4 * half + k)
                            mm = pe.transpose(ps[:, n, P * k:P * k + P], mem[:, t, c:c + P], core.ident[:, :])
                        mm.then_inc(s.turned, 1)

                @block.scalar
                def _(act):
                    for n in range(4):
                        t, half = n // 2, n % 2
                        act.wait_ge(s.turned, n + 1)
                        act.activation(mt[:, 4 * half:4 * half + 4, P * t:P * t + P],
                                       ps[:, n, :].rearrange("p (k c) -> p k c", k=4), ACT.Copy).then_inc(s.stored, 1)
            s.clear()
            linear_stage(core, "xak", feature_tiles(0, 4, 256, DK), mhi, mlo,
                         norm=Norm(core, mt, lambda k: core.gain("mem_norm_2", k), mhi, mlo, "nothing", toks=N_MEM),
                         dve_tile=store_tile(core, lambda t: kf[:, t, :]))
            linear_stage(core, "xav", token_tiles(0, 4, 256, DK, MT), mhi, mlo,
                         dve_tile=store_tile(core, lambda t: v[:, t % MT, 256 * (t // MT):256 * (t // MT) + 256]))
        def scaled_q(dve, s, t):
            dve.wait_ge(s.tile_done, t + 1)
            dve.tensor_scalar(qf[:, t, :], ps[:, t % 4, :], 256 ** -0.5, None, ALU.mult).then_inc(s.bank_free, 1)
        linear_stage(core, "xaq", feature_tiles(0, 4, 256, DK), xhi, xlo, dve_tile=scaled_q,
                     norm=Norm(core, core.h, g(2), xhi, xlo, "sum"))
        memory_attention_stage(core, qf, kf, v, xhi, xlo)
        linear_stage(core, "xao", feature_tiles(0, 4, 256, DK), xhi, xlo,
                     dve_tile=store_tile(core, lambda t: qf[:, t, :]), squares=stored_squares(core, qf))
        add_normed_stage(core, "n3", qf, g(3))


def feed_forward(core, ins):
    nc, ps = core.nc, core.ps
    g = lambda n: (lambda k: core.gain("norm_gains_2", DK * n + k))
    with ExitStack() as ctx:
        sb = lambda c, n, sh, d=fp32: c.enter_context(nc.sbuf_tensor(f"ff_{n}", sh, d))
        ahi, alo = sb(ctx, "ahi", [P, FF_TILES, SEQ], fp32r), sb(ctx, "alo", [P, FF_TILES, SEQ], fp32r)
        with ExitStack() as c1:
            xhi, xlo = sb(c1, "xhi", [P, DK, SEQ], fp32r), sb(c1, "xlo", [P, DK, SEQ], fp32r)
            gate = sb(c1, "gate", [P, 2, SEQ])
            cg, cv, gel = (gate[:, 0, :], gate[:, 1, :]), core.sq, core.split_buf
            tiles, order = [], []
            for j in range(FF_TILES // 2):
                for kind in range(2):
                    for c in range(2):
                        tiles.append([(2 * j + kind, slice(P * c, P * c + P), [(k, k) for k in range(DK)], None)])
                        order.append((kind, 2 * j + c))

            def conv_dve(dve, s, t):
                c = Chain(dve, s.chain)
                c.n = 2 * t
                kind, f = order[t]
                dve.wait_ge(s.tile_done, t + 1)
                if f >= 2:
                    if kind == 0:
                        dve.wait_ge(s.gelu_done, f - 1)
                    else:
                        dve.wait_ge(s.lo_done, f - 1)
                buf = (cv if kind else cg)[f % 2][:, 0:SEQ]
                centred_conv(dve, c, buf, ps[:, t % 4, :],
                             [core.gain("ffn_conv_2", 2 * FF_TILES * j + FF_TILES * kind + f) for j in range(3)])\
                    .then_inc(s.bank_free, 1)
                if kind == 1:
                    dve.wait_ge(s.gelu_done, f + 1)
                    dve.wait_ge(s.bank_free, t + 1)
                    dve.tensor_tensor(buf, buf, gel[f % 2][:, :], ALU.mult).then_inc(s.product, 1)

            def gelu_act(act, s, t):
                kind, f = order[t]
                if kind == 0:
                    act.wait_ge(s.bank_free, t + 1)
                    if f >= 2:
                        act.wait_ge(s.product, f - 1)
                    act.activation(gel[f % 2][:, :], cg[f % 2], ACT.Gelu_apprx_tanh).then_inc(s.gelu_done, 1)
                else:
                    act.wait_ge(s.product, f + 1)
                    act.activation(ahi[:, f, :], cv[f % 2][:, :], ACT.Copy).then_inc(s.hi_done, 1)

            def low_pool(pool, s, t):
                kind, f = order[t]
                if kind == 1:
                    pool.wait_ge(s.hi_done, f + 1)
                    pool.tensor_tensor(alo[:, f, :], cv[f % 2][:, :], ahi[:, f, :].bitcast(fp32), ALU.subtract).then_inc(s.lo_done, 1)
            linear_stage(core, "up", tiles, xhi, xlo, act_tile=gelu_act, dve_tile=conv_dve, pool_tile=low_pool,
                         norm=Norm(core, core.h, g(4), xhi, xlo, "sum"))
        y = sb(ctx, "y", [P, DK, SEQ])
        half = FF_TILES // 2
        tiles = [[(2 * t + q, slice(0, P), [(k, half * q + k) for k in range(half)], None) for q in range(2)]
                 for t in range(DK)]
        linear_stage(core, "down", tiles, ahi, alo, dve_tile=store_tile(core, lambda t: y[:, t, :]),
                     squares=stored_squares(core, y))
        add_normed_stage(core, "n5", y, g(5), square=False)


def constants():
    f32 = np.float32
    L, N = SEQ, 2 * SEQ
    t = np.arange(L)[:, None]
    f = np.arange(L)[None, :]
    angle = 2 * np.pi * ((t * f) % N) / N
    nyquist = (-1.0) ** np.arange(L)
    cos, sin = np.cos(angle), -np.sin(angle)
    sin[:, 0] = nyquist
    dft = np.concatenate([cos, sin], axis=1)
    weight = np.full(N, 2.0 / N)
    weight[0] = weight[L] = 1.0 / N
    idft = weight[:, None] * dft.T

    pos = np.linspace(0.0, 1.0, L, dtype=f32)[:, None]
    bands = 16
    w = (f32(2.0 * math.pi) * np.arange(L, dtype=f32)[:, None] / f32(L)).astype(f32)
    fr = np.linspace(1e-4, bands - 1, bands, dtype=f32)[None, :]
    fw = (fr * w).astype(f32)
    emb = np.concatenate([pos, np.cos(fw), -np.sin(fw)], axis=-1)
    deltas = np.abs(np.linspace(math.log(1e-2) / 1.5, math.log(1e-2) / 0.3, HY, dtype=f32))
    decay = np.exp(-pos * deltas)

    c = np.arange(64)
    start = np.clip(c - 8, 0, 48)
    inside = (c[None, :] >= start[:, None]) & (c[None, :] < start[:, None] + 16)
    mask = np.where(inside, 0.0, -1e30)
    anti = (np.arange(31)[:, None] + np.arange(63 + P)[None, :] - 78) % 64 == 0
    return {"dft": dft.astype(f32), "idft": idft.astype(f32), "pos_emb": emb.T.astype(f32),
            "hy_decay": decay.astype(f32), "column_mask": np.concatenate([mask, mask]).astype(f32),
            "anti_diagonal": anti.astype(f32)}


def weight_schedule(ins):
    m_in, w_in, wkv, up, down = (ins[n] for n in ("m_in", "w_in_2", "xa_wkv_2", "ffn_up_2", "ffn_down_2"))
    m_in, w_in, wkv = m_in[0], w_in[0], wkv[0]
    up, down = (a[0].rearrange("(k p) n -> p k n", p=P) for a in (up, down))
    conv_end = D_INNER + CONV_TILES * P
    sc0, gates0 = 6 * HY, 9 * HY
    dft, idft = ins["dft"], slabs_of(ins["idft"], 256)
    yield "mz", slabs_of(m_in, 256, 0, D_INNER)
    yield "mdt", slabs_of(m_in, HEADS, conv_end, conv_end + HEADS)
    yield "mx", slabs_of(m_in, 256, D_INNER, conv_end)
    yield "mout", slabs_of(ins["m_out"][0], P)
    yield "ple0", gated_slabs(ins["ple_proj"][0], ins["ple_gate"][0], 0)
    yield "sbk", slabs_of(ins["w_kv"], 256, 0, D)
    yield "sbv", slabs_of(ins["w_kv"], 256, D, 2 * D)
    yield "sbq", slabs_of(ins["s_in"][0], 256, 0, D)
    yield "sbg", slabs_of(ins["s_in"][0], 256, D, 2 * D)
    yield "sbo", slabs_of(ins["s_out"][0], 256)
    yield "ple1", gated_slabs(ins["ple_proj"][1], ins["ple_gate"][1], 0)
    yield "hyin", slabs_of(w_in, 256, 0, 3 * HY)
    yield "scin", slabs_of(w_in, 256, sc0 + HY, sc0 + 3 * HY) + slabs_of(w_in, 256, sc0, sc0 + HY)
    for order in range(2):
        yield f"sp{order}", slabs_of(dft, 512)
        yield f"inv{order}", idft
    yield "naqk", slabs_of(w_in, 256, 3 * HY, 5 * HY)
    yield "nav", slabs_of(w_in, 256, 5 * HY, 6 * HY)
    for b in range(3):
        yield f"mg{b}", gated_slabs(ins["w_branch_2"][0, b], w_in, gates0 + D * b)
    yield "wout", slabs_of(ins["w_out_2"][0], 256)
    yield "xak", slabs_of(wkv, 256, 0, D)
    yield "xav", slabs_of(wkv, 256, D, 2 * D)
    yield "xaq", slabs_of(ins["xa_wq_2"][0], 256)
    yield "xao", slabs_of(ins["xa_wo_2"][0], 256)
    yield "up", [up[:, :, c:c + 256] for j in range(FF_TILES // 2) for c in (256 * j, D_FF + 256 * j)]
    half = FF_TILES // 2
    yield "down", [down[:, half * q:half * q + half, P * t:P * t + P] for t in range(DK) for q in range(2)]


def program(nc, ins, out):
    with ExitStack() as ctx:
        core = Core(nc, ctx, weight_schedule(ins))
        setup_stage(core, ins)
        mamba(core, ins)
        ple_stages(core, ins, 0)
        stick_breaking(core, ins)
        ple_stages(core, ins, 1)
        branches(core, ins)
        memory_attention(core, ins)
        feed_forward(core, ins)
        output_stage(core, out)


def kernel(**inputs):
    import numpy as _np
    import concourse.bacc as _bacc
    from concourse import mybir as _mybir
    from concourse.bass_utils import run_bass_kernel_spmd as _run

    nc = _bacc.Bacc("TRN2", target_bir_lowering=False, num_devices=1)
    arrays, ins = {}, {}
    for name, a in list(inputs.items()) + list(constants().items()):
        a = _np.ascontiguousarray(a)
        arrays[f"in_{name}"] = a
        ins[name] = nc.dram_tensor(f"in_{name}", a.shape, _mybir.dt.from_np(a.dtype), kind="ExternalInput").ap()
    out = nc.dram_tensor("out", (1, SEQ, D), _mybir.dt.float32, kind="ExternalOutput").ap()
    program(nc, ins, out)
    r = _run(nc, [arrays], core_ids=[0])
    return r.results[0]["out"]
```
